# Optimizing a Trainium2 kernel written in Bass

```python
import math
import jax, jax.numpy as jnp
from jax import lax
import numpy as np

D_MODEL = 2048
BATCH = 1
SEQ = 256
DEPTH = 1

N_META = 16
GRID_W = 64
ROW_WIN = 8
COL_WIN = 16
NA_HEAD_DIM = 64
NA_WIDTH = D_MODEL // 2
NA_HEADS = NA_WIDTH // NA_HEAD_DIM
SSM_WIDTH = D_MODEL // 2
SSM_GROUP = 16
SSM_GROUPS = SSM_WIDTH // SSM_GROUP
SSM_STATE = 64
DT_MIN = 1e-3
DT_MAX = 1e-1
D_FF = ((8 * D_MODEL // 3 + 255) // 256) * 256
CONV_W = 3
RMS_EPS = 1e-6
IN_SPLITS = [NA_WIDTH, 2 * NA_WIDTH, 3 * NA_WIDTH, 3 * NA_WIDTH + SSM_WIDTH,
             3 * NA_WIDTH + SSM_WIDTH + D_MODEL]
IN_COLS = 3 * NA_WIDTH + SSM_WIDTH + 2 * D_MODEL

kernel_name = "hybrid_natten_s5_convffn_encoder"

def rms_norm(x, g):
    xf = x.astype(jnp.float32)
    y = xf * lax.rsqrt(jnp.mean(xf * xf, axis=-1, keepdims=True) + RMS_EPS)
    return (y * g.astype(jnp.float32)).astype(x.dtype)

def neighbourhood_attention(q, k, v, rpb):
    b, L, h, dh = q.shape
    rows = (L - N_META) // GRID_W
    kr = min(ROW_WIN, rows)
    scale = dh ** -0.5
    qm, km, vm = q[:, :N_META], k[:, :N_META], v[:, :N_META]
    qg = q[:, N_META:].reshape(b, rows, GRID_W, h, dh)
    kg = k[:, N_META:].reshape(b, rows, GRID_W, h, dh)
    vg = v[:, N_META:].reshape(b, rows, GRID_W, h, dh)

    s_m = jnp.einsum('bqhd,bkhd->bhqk', qm, km).astype(jnp.float32) * scale
    p_m = jax.nn.softmax(s_m, axis=-1).astype(v.dtype)
    o_m = jnp.einsum('bhqk,bkhd->bqhd', p_m, vm)

    r_idx = jnp.arange(rows)
    row_start = jnp.clip(r_idx - kr // 2, 0, rows - kr)
    dr = row_start[:, None] + jnp.arange(kr)[None] - r_idx[:, None] + (ROW_WIN - 1)
    c_idx = jnp.arange(GRID_W)
    col_start = jnp.clip(c_idx - COL_WIN // 2, 0, GRID_W - COL_WIN)
    col_keys = col_start[:, None] + jnp.arange(COL_WIN)[None]
    dc = col_keys - c_idx[:, None] + (COL_WIN - 1)

    def row_block(args):
        q_r, r0, dr_r = args
        k_rows = lax.dynamic_slice_in_dim(kg, r0, kr, axis=1)
        v_rows = lax.dynamic_slice_in_dim(vg, r0, kr, axis=1)
        k_win = k_rows[:, :, col_keys]
        v_win = v_rows[:, :, col_keys]
        bias = rpb[:, dr_r[:, None, None], dc[None]]
        s_loc = (jnp.einsum('bchd,bicjhd->bhcij', q_r, k_win).astype(jnp.float32) * scale
                 + jnp.transpose(bias, (0, 2, 1, 3))[None].astype(jnp.float32))
        s_loc = s_loc.reshape(b, h, GRID_W, kr * COL_WIN)
        s_meta = jnp.einsum('bchd,bmhd->bhcm', q_r, km).astype(jnp.float32) * scale
        p = jax.nn.softmax(jnp.concatenate([s_loc, s_meta], axis=-1), axis=-1).astype(v.dtype)
        p_loc = p[..., :kr * COL_WIN].reshape(b, h, GRID_W, kr, COL_WIN)
        p_meta = p[..., kr * COL_WIN:]
        return (jnp.einsum('bhcij,bicjhd->bchd', p_loc, v_win)
                + jnp.einsum('bhcm,bmhd->bchd', p_meta, vm))

    o_g = lax.map(row_block, (jnp.moveaxis(qg, 1, 0), row_start, dr))
    o_g = jnp.moveaxis(o_g, 0, 1).reshape(b, rows * GRID_W, h, dh)
    return jnp.concatenate([o_m, o_g], axis=1)

def _ssm_combine(left, right):
    a_l, b_l = left
    a_r, b_r = right
    return a_r * a_l, a_r * b_l + b_r

def s5_direction(u, lam_re, lam_im, log_step, b_re, b_im, c_re, c_im, reverse):
    f32 = jnp.float32
    lam = lax.complex(lam_re.astype(f32), lam_im.astype(f32))
    step = jnp.exp(log_step.astype(f32))[:, None]
    lam_bar = jnp.exp(lam * step)
    b_mat = lax.complex(b_re.astype(f32), b_im.astype(f32))
    b_bar = ((lam_bar - 1.0) / lam)[..., None] * b_mat
    bu = jnp.einsum('blgc,gnc->blgn', u.astype(jnp.complex64), b_bar)
    a = jnp.broadcast_to(lam_bar, bu.shape)
    _, states = lax.associative_scan(_ssm_combine, (a, bu), axis=1, reverse=reverse)
    c_mat = lax.complex(c_re.astype(f32), c_im.astype(f32))
    return jnp.real(jnp.einsum('blgn,gcn->blgc', states, c_mat))

def s5_branch(u, lam_re, lam_im, log_step, b_re, b_im, c_re, c_im, d_skip, w_glu):
    b, L, _ = u.shape
    ug = u.astype(jnp.float32).reshape(b, L, SSM_GROUPS, SSM_GROUP)
    y = (s5_direction(ug, lam_re[0], lam_im[0], log_step[0], b_re[0], b_im[0], c_re[0], c_im[0], False)
         + s5_direction(ug, lam_re[1], lam_im[1], log_step[1], b_re[1], b_im[1], c_re[1], c_im[1], True)
         + ug * d_skip.astype(jnp.float32).reshape(SSM_GROUPS, SSM_GROUP))
    y = jax.nn.gelu(y.reshape(b, L, SSM_WIDTH).astype(u.dtype))
    return y * jax.nn.sigmoid(y @ w_glu)

def conv_gated_ffn(h, w_up, conv_w, conv_b, w_down):
    a, g = jnp.split(h @ w_up, 2, axis=-1)
    ap = jnp.pad(a, ((0, 0), (1, 1), (0, 0)))
    a = ap[:, :-2] * conv_w[0] + ap[:, 1:-1] * conv_w[1] + ap[:, 2:] * conv_w[2] + conv_b
    return (jax.nn.gelu(a) * g) @ w_down

def setup_inputs(seed: int = 0) -> dict:
    key = jax.random.key(seed)
    ks = jax.random.split(key, 24)
    f32 = jnp.float32
    G, N, C = SSM_GROUPS, SSM_STATE, SSM_GROUP

    def nrm(k, shape, scale):
        return jax.random.normal(k, shape, f32) * scale

    n_idx = jnp.arange(N, dtype=f32)
    lam_re = -0.5 + 0.01 * jax.random.normal(ks[5], (DEPTH, 2, G, N), f32)
    lam_im = math.pi * n_idx + 0.01 * jax.random.normal(ks[6], (DEPTH, 2, G, N), f32)
    log_step = jax.random.uniform(ks[7], (DEPTH, 2, G), f32, math.log(DT_MIN), math.log(DT_MAX))
    b_scale = (2.0 * C) ** -0.5
    c_scale = (2.0 * N) ** -0.5
    return {
        "x": nrm(ks[0], (BATCH, SEQ, D_MODEL), 1.0),
        "meta_tokens": nrm(ks[1], (N_META, D_MODEL), 1.0),
        "norm1_g": 1.0 + nrm(ks[2], (DEPTH, D_MODEL), 0.02),
        "w_in": nrm(ks[3], (DEPTH, D_MODEL, IN_COLS), D_MODEL ** -0.5),
        "na_rpb": nrm(ks[4], (DEPTH, NA_HEADS, 2 * ROW_WIN - 1, 2 * COL_WIN - 1), 0.02),
        "ssm_lam_re": lam_re,
        "ssm_lam_im": lam_im,
        "ssm_log_step": log_step,
        "ssm_b_re": nrm(ks[8], (DEPTH, 2, G, N, C), b_scale),
        "ssm_b_im": nrm(ks[9], (DEPTH, 2, G, N, C), b_scale),
        "ssm_c_re": nrm(ks[10], (DEPTH, 2, G, C, N), c_scale),
        "ssm_c_im": nrm(ks[11], (DEPTH, 2, G, C, N), c_scale),
        "ssm_d": nrm(ks[12], (DEPTH, SSM_WIDTH), 1.0),
        "w_glu": nrm(ks[13], (DEPTH, SSM_WIDTH, SSM_WIDTH), SSM_WIDTH ** -0.5),
        "w_proj_na": nrm(ks[14], (DEPTH, NA_WIDTH, D_MODEL), NA_WIDTH ** -0.5),
        "w_proj_ssm": nrm(ks[15], (DEPTH, SSM_WIDTH, D_MODEL), SSM_WIDTH ** -0.5),
        "w_out": nrm(ks[16], (DEPTH, D_MODEL, D_MODEL), D_MODEL ** -0.5),
        "norm2_g": 1.0 + nrm(ks[17], (DEPTH, D_MODEL), 0.02),
        "w_up": nrm(ks[18], (DEPTH, D_MODEL, 2 * D_FF), D_MODEL ** -0.5),
        "conv_w": nrm(ks[19], (DEPTH, CONV_W, D_FF), CONV_W ** -0.5),
        "conv_b": nrm(ks[20], (DEPTH, D_FF), 0.01),
        "w_down": nrm(ks[21], (DEPTH, D_FF, D_MODEL), D_FF ** -0.5),
        "final_g": 1.0 + nrm(ks[22], (D_MODEL,), 0.02),
    }

def reference(x, meta_tokens, norm1_g, w_in, na_rpb, ssm_lam_re, ssm_lam_im, ssm_log_step,
              ssm_b_re, ssm_b_im, ssm_c_re, ssm_c_im, ssm_d, w_glu, w_proj_na, w_proj_ssm,
              w_out, norm2_g, w_up, conv_w, conv_b, w_down, final_g):
    b = x.shape[0]
    meta = jnp.broadcast_to(meta_tokens.astype(x.dtype)[None], (b, N_META, D_MODEL))
    h = jnp.concatenate([meta, x], axis=1)
    L = h.shape[1]
    for l in range(DEPTH):
        hn = rms_norm(h, norm1_g[l])
        q, k, v, u, g_na, g_ssm = jnp.split(hn @ w_in[l], IN_SPLITS, axis=-1)
        q = q.reshape(b, L, NA_HEADS, NA_HEAD_DIM)
        k = k.reshape(b, L, NA_HEADS, NA_HEAD_DIM)
        v = v.reshape(b, L, NA_HEADS, NA_HEAD_DIM)
        y_na = neighbourhood_attention(q, k, v, na_rpb[l]).reshape(b, L, NA_WIDTH) @ w_proj_na[l]
        y_ssm = s5_branch(u, ssm_lam_re[l], ssm_lam_im[l], ssm_log_step[l], ssm_b_re[l],
                          ssm_b_im[l], ssm_c_re[l], ssm_c_im[l], ssm_d[l], w_glu[l]) @ w_proj_ssm[l]
        mixed = jax.nn.sigmoid(g_na) * y_na + jax.nn.sigmoid(g_ssm) * y_ssm
        h = h + mixed @ w_out[l]
        h = h + conv_gated_ffn(rms_norm(h, norm2_g[l]), w_up[l], conv_w[l], conv_b[l], w_down[l])
    h = rms_norm(h, final_g)
    return h[:, N_META:]


_drawn_inputs = setup_inputs


def setup_inputs(seed=0):
    import zlib

    import numpy as np

    out = dict(_drawn_inputs(seed))
    spreads = {}
    factors = {'norm1_g': 8.0,
     'na_rpb': 23.808,
     'ssm_lam_re': 64.0,
     'ssm_lam_im': 27.286,
     'ssm_log_step': 25.911,
     'ssm_b_re': 39.76,
     'ssm_b_im': 39.432,
     'ssm_c_re': 39.392,
     'ssm_c_im': 39.568,
     'norm2_g': 3.647,
     'conv_b': 23.946,
     'final_g': 7.971}
    for name, (base, spread) in spreads.items():
        noise = np.random.default_rng([zlib.crc32(name.encode()), seed]).standard_normal(out[name].shape)
        drawn = base * np.exp(spread * noise) if base else spread * noise
        out[name] = __import__('jax').numpy.asarray(drawn.astype(out[name].dtype))
    for name, factor in factors.items():
        out[name] = (out[name] * factor).astype(out[name].dtype)
    return out
```

```python
import math
from contextlib import ExitStack

import numpy as np
import concourse.bass as bass
from concourse import mybir

D_MODEL = 2048
SEQ = 256
N_META = 16
GRID_W = 64
ROW_WIN = 8
COL_WIN = 16
DH = 64
HEADS = (D_MODEL // 2) // DH
HALF = D_MODEL // 2
GROUP = 16
GROUPS = HALF // GROUP
STATE = 64
D_FF = ((8 * D_MODEL // 3 + 255) // 256) * 256
EPS = 1e-6
SEED = 3
DIRS = 2

P = 128
L = N_META + SEQ
LIVE = N_META - 2
NL = L - LIVE
KT = D_MODEL // P
KH = HALF // P
FT = D_FF // P
DEPTH = 4
UNIT = 1024
CB = 256
UKT = UNIT // CB
CHUNK = 4
NCH = L // CHUNK
PAIRS = GROUPS // 2
PB = P // (2 * GROUP)
GRID_ROWS = SEQ // GRID_W
SCALE = DH ** -0.5
MASKED = -1e30
PADW = 2 * GRID_W - 1
RPB_ROWS = 2 * ROW_WIN - 1
RPB_COLS = 2 * COL_WIN - 1
QROWS = P // GRID_W
DROWS = 2 * GRID_ROWS - 1
EWIN = GRID_ROWS + QROWS * (SEQ // P - 1)
TWO_PI_HI = 6.28125
TWO_PI_MID = 0.0019350051879882812
TWO_PI_LO = 2 * math.pi - TWO_PI_HI - TWO_PI_MID
ROUND = 1.5 * 2 ** 23
PI_BELOW = 3.1415925


def encoder_block(nc, x, meta, norm1_g, w_in, rpb, lam_re, lam_im, log_step, b_re, b_im, c_re, c_im,
                  ssm_d, w_glu, w_proj_na, w_proj_ssm, w_out, norm2_g, w_up, conv_w, conv_b, w_down,
                  final_g, out):
    F = mybir.dt.float32
    R = mybir.dt.float32r
    ACT = mybir.ActivationFunctionType
    ALU = mybir.AluOpType
    AX = mybir.AxisListType
    ds = bass.ds

    q_d = nc.dram_tensor("q_scratch", [KH, P, NL], F, kind="Internal").ap()
    k_d = nc.dram_tensor("k_scratch", [KH, P, L], F, kind="Internal").ap()
    v_d = nc.dram_tensor("v_scratch", [L, HALF], F, kind="Internal").ap()
    xT_d = nc.dram_tensor("xT_scratch", [P, KT * L], F, kind="Internal").ap()
    pad_d = nc.dram_tensor("rpb_scratch", [HEADS * DROWS, PADW], F, kind="Internal").ap()
    skew_d = nc.dram_tensor("skew_scratch", [GRID_W, HEADS * DROWS, GRID_W], F, kind="Internal").ap()

    ctx = ExitStack()
    with ctx:
        def sem(name):
            return ctx.enter_context(nc.semaphore(name))

        base = (nc.sbuf_base + 31) // 32 * 32
        cursor = [base]

        def keep(name, shape, dt=F):
            t = nc.alloc_sbuf_tensor_at(name, shape, dt, offset=cursor[0])
            cursor[0] += (int(np.prod(shape[1:])) * 4 + 31) // 32 * 32
            return t

        raw = keep("w_raw", [P, DEPTH, UNIT])
        whi = keep("w_hi", [P, DEPTH, UNIT], R)
        wlo = keep("w_lo", [P, DEPTH, UNIT], R)
        hnh = keep("act_hi", [P, KT, L], R)
        hnl = keep("act_lo", [P, KT, L], R)
        o_tr = cursor[0]
        tr = keep("norm_ring", [P, DEPTH, L])
        vm = nc.alloc_sbuf_tensor_at("v_meta", [N_META, KH, P], F, offset=o_tr)
        sq = keep("square_ring", [P, 2, L])
        rstd = keep("rstd", [P, L])
        ident = keep("ident", [P, P])
        ones = keep("ones", [P, P])
        gains = keep("gains", [P, 3 * KT])
        cvw = keep("conv_params", [P, 4 * FT])
        mask = keep("col_mask", [P, GRID_W])
        stat = keep("att_stats", [P, 4, 2, 2])
        arena = (cursor[0] + 31) // 32 * 32

        def at(name, off, shape, dt=F):
            assert off % 32 == 0 and arena + off + int(np.prod(shape[1:])) * 4 <= nc.sbuf_usable_end, (name, off)
            return nc.alloc_sbuf_tensor_at(name, shape, dt, offset=arena + off)

        xtok = at("x_tokens", 0, [P, 3, D_MODEL])
        X = at("scan_states", 0, [P, NCH + 1, 2 * DIRS, PAIRS])
        gates = at("gates", 0, [P, 2 * KT, NL])
        o_y = 35328
        yT = at("y_ssm", o_y, [P, KH, L])
        x0T = at("x_feature_major", o_y, [P, KT, L])
        braw = at("b_raw", 24576, [P, 2, DIRS * PAIRS, GROUP])
        o_u = o_y + KH * L * 4
        U = at("u_chunks", o_u, [P, PAIRS, NCH])
        stg = at("qkv_stage", o_u + 8704, [P, 2, 2, L])
        vst = at("v_stage", o_u + 8704 + 4352, [P, 3, CB])
        anh = at("attn_hi", o_u, [P, KH, NL], R)
        anl = at("attn_lo", o_u + 8256, [P, KH, NL], R)
        o_p = o_u + 2 * 8256
        BB = at("b_bar", o_p, [P, DIRS * PAIRS, 3, GROUP])
        CC = at("c_slots", o_p + 12288, [P, DIRS * PAIRS, 3, GROUP])
        pwW = at("pow_in", o_p + 24576, [P, DIRS * PAIRS, 2, CHUNK, 2])
        pwG = at("pow_out", o_p + 28672, [P, DIRS * PAIRS, 2, CHUNK + 1, 2])
        A4R = at("chunk_re", o_p + 33792, [P, DIRS, 2, PAIRS])
        A4I = at("chunk_im", o_p + 34304, [P, DIRS, 2, PAIRS])
        drep = at("d_skip", o_p + 34816, [P, PAIRS])
        o_r = o_p + 34944
        cnat = at("c_rows", o_r, [P, DIRS, KH, 2, STATE])
        prm = at("params", o_r + 8192, [P, 24, DIRS * PAIRS])
        pw = at("powers", o_r + 8192 + 6144, [P, CHUNK + 1, 2, DIRS * PAIRS])
        rows = at("param_rows", o_r + 8192 + 6144 + 2560, [DIRS * PAIRS, 3, P])
        lst = at("step_rows", o_r + 18432, [DIRS * PAIRS, 8])
        drow = at("d_rows", o_r + 18464, [PAIRS, CHUNK, 2 * GROUP])
        btmp = at("b_tmp", 0, [P, 2, UNIT])
        grow = at("gain_rows", o_r + 18976, [3 * KT, P])
        crow = at("conv_rows", o_r + 19488, [2 * FT, 2, P])
        padt = at("rpb_pad", o_u + 13056, [HEADS * DROWS, P])
        Wn = at("w_nat", o_r, [P, 2, DIRS, 2, P])
        t1v = at("t1_v", o_r + 4096, [P, 2, 160])
        t2v = at("t2_v", o_r + 5376, [P, 2, 160])
        t1p = at("t1_p", o_r + 6656, [P, 2, 160])
        t2p = at("t2_p", o_r + 7936, [P, 2, 160])
        WT = at("w_tr", o_r + 9216, [P, 2, 2 * DIRS, P])
        Gn = at("g_nat", o_r + 13312, [P, 2, DIRS, 2, 160])
        Tm = at("toeplitz", o_r + 18432, [P, 2, P])
        Bm = at("b_masked", o_r + 19456, [P, 2, DIRS, 2, 2 * GROUP])
        sc1 = at("scan_t1", o_r + 20480, [P, P])
        sc2 = at("scan_t2", o_r + 20992, [P, P])
        qm = at("q_meta", o_r + 21504, [P, KH, 2])
        km = at("k_meta", o_r + 21568, [P, KH, N_META])
        o_a = o_p
        qs = at("q_ring", o_a, [P, 2, NL])
        ks = at("k_ring", o_a + 2080, [P, 2, L])
        vs = at("v_ring", o_a + 4256, [P, 2, 3, P])
        bi = at("bias_ring", o_a + 7328, [P, 4, EWIN, GRID_W])
        S = at("scores", o_a + 13472, [P, 2, 2, L])
        PT = at("probs_t", o_a + 17824, [P, 2, 2 * SEQ])
        PT2 = at("probs_t2", o_a + 21920, [N_META, 2, SEQ])
        sm = at("meta_scores", o_a + 23968, [2, 2, KH, N_META])
        smx = at("meta_stats", o_a + 24992, [2, 4, HEADS])
        ptm = at("meta_probs_t", o_a + 25248, [N_META, 2 * HEADS])
        ygh = at("gelu_hi", o_a + 25376, [P, KH, NL], R)
        ygl = at("gelu_lo", o_a + 25376 + 8256, [P, KH, NL], R)
        zh = at("z_hi", o_a, [P, KH, NL], R)
        zl = at("z_lo", o_a + 8256, [P, KH, NL], R)
        gt = at("glu_ring", o_a + 16512, [P, 4, NL])
        mt = at("mix_ring", o_a + 16512 + 4128, [P, 4, NL])
        ah = at("hidden_hi", 0, [P, FT, SEQ], R)
        al = at("hidden_lo", 45056, [P, FT, SEQ], R)
        cv = at("conv_ring", 90112, [P, 2, 2, SEQ])
        ge = at("gelu_ring", 94208, [P, 2, 2, SEQ])
        o_x = 98304
        xT = at("xT", o_x, [P, KT, L])
        otok = at("out_tokens", 0, [P, SEQ // P, D_MODEL])

        ps = ctx.enter_context(nc.psum_tensor("ps", [P, 8, 512], F))

        s_x = sem("x_loaded")
        s_par = sem("params_loaded")
        s_raw = [sem(f"unit_loaded_{i}") for i in range(DEPTH)]
        s_hi = sem("unit_hi_made")
        s_lo = sem("unit_split")
        s_used = sem("unit_consumed")
        s_const = sem("constants_made")
        s_xtp = sem("x_transposed")
        s_xt = sem("xT_copied")
        s_sq = sem("squares_made")
        s_ss = sem("squares_summed")
        s_sq_used = sem("square_tile_summed")
        s_var = sem("variance_made")
        s_sd = sem("deviation_made")
        s_nt = sem("norm_tile_made")
        s_nh = sem("norm_hi_made")
        s_nl = sem("norm_lo_made")
        s_spill = sem("xT_spilled")
        s_xre = sem("xT_reloaded")
        s_rows = sem("rows_ready")
        s_ptp = sem("params_transposed")
        s_pcp = sem("params_copied")
        s_pd = sem("param_step_dve")
        s_pa = sem("param_step_act")
        s_ctp = sem("c_transposed")
        s_ccp = sem("c_copied")
        s_u = sem("u_chunks_ready")
        s_kev = sem("qkv_block_copied")
        s_kst = sem("qk_stored")
        s_vtd = sem("v_block_copied")
        s_vtp = sem("v_transposed")
        s_vcp = sem("v_copied")
        s_vst = sem("v_stored")
        s_wd = sem("w_fwd_made")
        s_wp = sem("w_bwd_made")
        s_wtp = sem("w_transposed")
        s_wts = sem("w_copied")
        s_sps = sem("chunk_inputs_summed")
        s_ssb = sem("chunk_inputs_copied")
        s_scan = sem("scan_done")
        s_gd = sem("g_fwd_made")
        s_gp = sem("g_bwd_made")
        s_kps = sem("kernel_summed")
        s_tm = sem("toeplitz_copied")
        s_yps = sem("y_summed")
        s_ysb = sem("y_copied")
        s_yg = sem("gelu_made")
        s_ygh = sem("gelu_hi_made")
        s_ygl = sem("gelu_lo_made")
        s_pad1 = sem("pad_zeroed")
        s_pad2 = sem("pad_filled")
        s_pad3 = sem("pad_skewed")
        s_qkv = [sem(f"qkv_loaded_{i}") for i in range(2)]
        s_bl = [sem(f"bias_loaded_{i}") for i in range(4)]
        s_bm = sem("bias_masked")
        s_qk = sem("scores_summed")
        s_nm = sem("row_max_ready")
        s_e = sem("exp_made")
        s_p = sem("probs_ready")
        s_ptps = sem("probs_transposed")
        s_ptsb = sem("probs_copied")
        s_pv = sem("pv_summed")
        s_ah = sem("attn_hi_made")
        s_al = sem("attn_lo_made")
        s_m1 = sem("meta_scores_summed")
        s_m2 = sem("meta_shifted")
        s_m3 = sem("meta_exp_made")
        s_m4 = sem("meta_probs_ready")
        s_m5 = sem("meta_probs_transposed")
        s_m6 = sem("meta_probs_copied")
        s_m7 = sem("meta_pv_summed")
        s_m8 = sem("meta_hi_made")
        s_g = sem("gates_made")
        s_sg = sem("glu_gate_made")
        s_z = sem("z_made")
        s_zh = sem("z_hi_made")
        s_zl = sem("z_lo_made")
        s_mx = sem("mix_made")
        s_mh = sem("mix_hi_made")
        s_ml = sem("mix_lo_made")
        s_h1 = sem("h1_block_added")
        s_c = sem("conv_started")
        s_cd = sem("conv_made")
        s_ge = sem("hidden_gelu_made")
        s_fm = sem("hidden_made")
        s_fh = sem("hidden_hi_made")
        s_fl = sem("hidden_lo_made")
        s_dn = sem("down_done")
        s_h2 = sem("h2_made")
        s_ot = sem("out_transposed")
        s_oc = sem("out_copied")
        s_out = sem("out_stored")

        block = ctx.enter_context(nc.Block())

        U_U, U_K, U_V, U_Q, U_G = 0, 16, 32, 48, 64
        U_GLU = U_G + 64
        U_PROJ = U_GLU + 8
        U_OUT = U_PROJ + 32
        U_UP = U_OUT + 32
        U_DOWN = U_UP + 4 * FT
        U_END = U_DOWN + 2 * FT
        ITERS_IN = 2

        def kblock(w, col, kq):
            return w[kq * UKT * P:(kq + 1) * UKT * P, ds(col, CB)].rearrange("(t p) c -> p t c", p=P)

        def slot(ring, k):
            return ring[:, k % DEPTH, :]

        @block.sync
        def _(sp):
            sp.dma_start(xtok[0:N_META, 0, :], meta).then_inc(s_x, 16)
            sp.dma_start(xtok[N_META:P, 0, :], x[0, 0:P - N_META, :]).then_inc(s_x, 16)
            sp.dma_start(xtok[:, 1, :], x[0, P - N_META:2 * P - N_META, :]).then_inc(s_x, 16)
            sp.dma_start(xtok[0:N_META, 2, :], x[0, 2 * P - N_META:SEQ, :]).then_inc(s_x, 16)

            def load(base_u, k, src):
                if isinstance(base_u, int) and base_u + k < DEPTH:
                    pass
                else:
                    sp.wait_ge(s_lo, base_u + (k - DEPTH + 1))
                dst = slot(raw, k)
                if len(src.shape) == 3:
                    dst = dst.rearrange("p (t c) -> p t c", t=src.shape[1])
                sp.dma_start(dst, src).then_inc(s_raw[k % DEPTH], 16)

            def load_in(first, col0, i, units=range(8)):
                for k in units:
                    load(first + 8 * i, k, kblock(w_in[0], i * (2 * CB) + (col0 + (k // 4) * CB), k % 4))

            load_in(U_U, 3 * HALF, 0)
            sp.wait_ge(s_xt, KT)
            sp.dma_start(xT_d, x0T[:, :, :].rearrange("p k t -> p (k t)")).then_inc(s_spill, 16)
            with sp.Fori(1, ITERS_IN) as i:
                load_in(U_U, 3 * HALF, i)
            sp.wait_ge(s_pad2, 16)
            with sp.Fori(0, GRID_W) as c:
                sp.dma_start(skew_d[ds(c, 1), :, :].rearrange("a r w -> (a r) w"),
                             pad_d[:, ds((GRID_W - 1) - c, GRID_W)]).then_inc(s_pad3, 16)
            for first, col0 in ((U_K, HALF), (U_V, 2 * HALF), (U_Q, 0)):
                with sp.Fori(0, ITERS_IN) as i:
                    load_in(first, col0, i)

            load_in(U_G, 4 * HALF, 0, range(4))
            sp.wait_ge(s_pad3, 16 * GRID_W)
            sp.wait_ge(s_kst, 16 * 16)
            sp.wait_ge(s_vst, 16 * 8)
            sp.wait_ge(s_ysb, PAIRS)
            with sp.Fori(0, KH // 2) as i:
                for j in range(2):
                    b = 2 * i + j
                    sp.wait_ge(s_pv, 4 * i + (2 * j - 2 + SEED))
                    sp.dma_start(qs[:, j, :], q_d[ds(b, 1), :, :].rearrange("b p t -> p (b t)")).then_inc(s_qkv[j], 16)
                    sp.dma_start(ks[:, j, :], k_d[ds(b, 1), :, :].rearrange("b p t -> p (b t)")).then_inc(s_qkv[j], 16)
                    sp.dma_start(vs[:, j, 0:2, :],
                                 v_d[0:2 * P, ds(b * P, P)].rearrange("(k p) c -> p k c", p=P)).then_inc(s_qkv[j], 16)
                    sp.dma_start(vs[0:N_META, j, 2, :], v_d[2 * P:L, ds(b * P, P)]).then_inc(s_qkv[j], 16)
                    for hh in range(2):
                        for r in range(QROWS):
                            row = b * (2 * DROWS) + (hh * DROWS + GRID_ROWS - 1 - QROWS - r)
                            sp.dma_start(bi[GRID_W * r:GRID_W * (r + 1), 2 * j + hh, :, :], skew_d[:, ds(row, EWIN), :])\
                              .then_inc(s_bl[2 * j + hh], 16)

            load_in(U_G, 4 * HALF, 0, range(4, 8))
            with sp.Fori(1, 8) as i:
                load_in(U_G, 4 * HALF, i)
            for k in range(8):
                load(U_GLU, k, kblock(w_glu[0], (k // 2) * CB, k % 2))
            with sp.Fori(0, 4) as i:
                for k in range(8):
                    w = (w_proj_na, w_proj_ssm)[k % 4 // 2]
                    load(U_PROJ + 8 * i, k, kblock(w[0], i * (2 * CB) + (k // 4) * CB, k % 2))
            sp.wait_ge(s_used, U_PROJ)
            sp.wait_ge(s_spill, 16)
            sp.dma_start(xT[:, :, :].rearrange("p k t -> p (k t)"), xT_d).then_inc(s_xre, 16)
            with sp.Fori(0, 4) as i:
                for k in range(8):
                    load(U_OUT + 8 * i, k, kblock(w_out[0], i * (2 * CB) + (k // 4) * CB, k % 4))
            with sp.Fori(0, FT // 4) as i:
                for k in range(16):
                    col = i * (2 * CB) + ((k // 8) * CB + (k % 8 // 4) * D_FF)
                    load(U_UP + 16 * i, k, kblock(w_up[0], col, k % 4))
            with sp.Fori(0, FT // 2) as i:
                for k in range(4):
                    src = w_down[0][ds(i * (2 * P) + (k // 2) * P, P), (k % 2) * UNIT:(k % 2 + 1) * UNIT]
                    load(U_DOWN + 4 * i, k, src)
            for n in range(KT // DEPTH):
                sp.wait_ge(s_oc, n + 1)
                cs = slice(512 * n, 512 * (n + 1))
                sp.dma_start(out[0, :, cs].rearrange("(t p) c -> p t c", p=P), otok[:, :, cs]).then_inc(s_out, 16)
            sp.wait_ge(s_out, 16 * (KT // DEPTH))

        def hi_unit(act, base_u, k):
            act.wait_ge(s_raw[k % DEPTH], base_u * 4 + 16 * (k // DEPTH + 1))
            if not (isinstance(base_u, int) and base_u + k < DEPTH):
                act.wait_ge(s_used, base_u + (k - DEPTH + 1))
            act.activation(slot(whi, k), slot(raw, k), ACT.Copy).then_inc(s_hi, 1)

        def lo_unit(pool, base_u, k):
            pool.wait_ge(s_hi, base_u + (k + 1))
            pool.tensor_tensor(slot(wlo, k), slot(raw, k), slot(whi, k).bitcast(F), ALU.subtract).then_inc(s_lo, 1)

        def split_loop(eng, unit, first, iters, per):
            with eng.Fori(0, iters) as i:
                for k in range(per):
                    unit(eng, (first + DEPTH) + per * i, k)

        def norm_lo(pool, which, n):
            with pool.Fori(0, KT // DEPTH) as i:
                for k in range(DEPTH):
                    pool.wait_ge(s_nh, DEPTH * i + (KT * which + k + 1))
                    pool.tensor_tensor(hnl[:, ds(DEPTH * i + k, 1), 0:n].rearrange("p k n -> p (k n)"), tr[:, k, 0:n],
                                       hnh[:, ds(DEPTH * i + k, 1), 0:n].rearrange("p k n -> p (k n)").bitcast(F),
                                       ALU.subtract).then_inc(s_nl, 1)

        def w_make(eng, pair, sl, d, t1, t2):
            n = 2 * CHUNK
            dq = pair + d * PAIRS
            pr = pwW[:, ds(dq, 1), 0:1, :, :].rearrange("p q r k g -> p (q r) (k g)").unsqueeze(3)
            pi = pwW[:, ds(dq, 1), 1:2, :, :].rearrange("p q r k g -> p (q r) (k g)").unsqueeze(3)
            ri = BB[:, ds(dq, 1), 1:3, :].rearrange("p q r c -> p (q r) c").unsqueeze(2)
            nr = BB[:, ds(dq, 1), 0:2, :].rearrange("p q r c -> p (q r) c").unsqueeze(2)
            full = [P, 2, n, GROUP]
            a = t1[:, :, 0:n * GROUP].rearrange("p r (n c) -> p r n c", c=GROUP)
            b = t2[:, :, 0:n * GROUP].rearrange("p r (n c) -> p r n c", c=GROUP)
            eng.tensor_tensor(a, pr.to_broadcast(full), ri.to_broadcast(full), ALU.mult)
            eng.tensor_tensor(b, pi.to_broadcast(full), nr.to_broadcast(full), ALU.mult)
            eng.drain()
            ins = eng.tensor_tensor(Wn[:, sl, d, :, :], t1[:, :, 0:n * GROUP], t2[:, :, 0:n * GROUP], ALU.add)
            return ins

        def g_make(eng, pair, sl, d, t1, t2):
            n = 2 * (CHUNK + 1)
            dq = pair + d * PAIRS
            pr = pwG[:, ds(dq, 1), 0:1, :, :].rearrange("p q r k g -> p (q r) (k g)").unsqueeze(3)
            pi = pwG[:, ds(dq, 1), 1:2, :, :].rearrange("p q r k g -> p (q r) (k g)").unsqueeze(3)
            c0 = CC[:, ds(dq, 1), 0:2, :].rearrange("p q r c -> p (q r) c").unsqueeze(2)
            c1 = CC[:, ds(dq, 1), 1:3, :].rearrange("p q r c -> p (q r) c").unsqueeze(2)
            full = [P, 2, n, GROUP]
            a = t1[:, :, :].rearrange("p r (n c) -> p r n c", c=GROUP)
            b = t2[:, :, :].rearrange("p r (n c) -> p r n c", c=GROUP)
            eng.tensor_tensor(a, pr.to_broadcast(full), c0.to_broadcast(full), ALU.mult)
            eng.tensor_tensor(b, pi.to_broadcast(full), c1.to_broadcast(full), ALU.mult)
            eng.drain()
            return eng.tensor_tensor(Gn[:, sl, d, :, :], t1[:, :, :], t2[:, :, :], ALU.add)

        @block.gpsimd
        def _(pool):
            pool.sem_inc(s_nl, SEED)
            pool.memset(ones[:, :], 1.0).then_inc(s_const, 1)
            pool.memset(ident[:, :], 0.0)
            pool.memset(mask[:, :], 0.0)
            pool.memset(padt[:, :], 0.0)
            pool.drain()
            pool.affine_select(out=ident[:, :], in_=ident[:, :], compare_op=ALU.not_equal, fill=1.0,
                               base=0, pattern=[[-1, P]], channel_multiplier=1).then_inc(s_const, 1)
            pool.drain()
            far = GRID_W - COL_WIN
            for r in range(QROWS):
                m = mask[r * GRID_W:(r + 1) * GRID_W, 0:far]
                pool.affine_select(out=m, in_=m, compare_op=ALU.is_ge, fill=MASKED, base=COL_WIN // 2,
                                   pattern=[[1, far]], channel_multiplier=-1)
                pool.drain()
            pool.drain()
            for r in range(QROWS):
                m = mask[r * GRID_W:(r + 1) * GRID_W, COL_WIN:GRID_W]
                pool.affine_select(out=m, in_=m, compare_op=ALU.is_ge, fill=MASKED,
                                   base=COL_WIN // 2 - 1 - COL_WIN, pattern=[[-1, far]], channel_multiplier=1)
                pool.drain()
            pool.drain()
            for k in range(DEPTH):
                lo_unit(pool, 0, k)
            pool.dma_start(pad_d, padt[:, 0:PADW]).then_inc(s_pad1, 16)
            pool.wait_ge(s_pad1, 16)
            pool.dma_start(pad_d[:, GRID_W - COL_WIN:GRID_W - COL_WIN + RPB_COLS].rearrange("(h d) c -> h d c", h=HEADS),
                           rpb[0, :, ROW_WIN - GRID_ROWS:ROW_WIN - GRID_ROWS + DROWS, :]).then_inc(s_pad2, 16)
            norm_lo(pool, 0, L)

            split_loop(pool, lo_unit, U_U, ITERS_IN, 8)

            def store_block(i, k, dst):
                for m in range(2):
                    n = dst.shape[2]
                    pool.dma_start(dst[ds(4 * i + (2 * k + m), 1), :, :].rearrange("b p t -> p (b t)"),
                                   stg[:, k, m, 0:n]).then_inc(s_kst, 16)

            def k_or_q(first, blocks_before, dst):
                with pool.Fori(0, ITERS_IN) as i:
                    for k in range(2):
                        for n in range(4):
                            lo_unit(pool, (first + DEPTH) + 8 * i, 4 * k + n)
                        pool.wait_ge(s_kev, 2 * i + (blocks_before + k + 1) + SEED)
                        store_block(i, k, dst)

            k_or_q(U_K, 0, k_d)
            with pool.Fori(0, ITERS_IN) as i:
                for k in range(8):
                    lo_unit(pool, (U_V + DEPTH) + 8 * i, k)
                for k in range(2):
                    pool.wait_ge(s_vcp, 2 * i + (k + 1) + SEED)
                    col = i * (2 * CB) + k * CB
                    pool.dma_start(v_d[0:2 * P, ds(col, CB)].rearrange("(k p) c -> p k c", p=P),
                                   vst[:, 0:2, :]).then_inc(s_vst, 16)
                    pool.dma_start(v_d[2 * P:L, ds(col, CB)], vst[0:N_META, 2, :]).then_inc(s_vst, 16)
            k_or_q(U_Q, 4, q_d)

            pool.wait_ge(s_pd, 1)
            pool.memset(Bm[:, :, :, :, :], 0.0)
            def w_bwd(p, k):
                pool.wait_ge(s_wtp, p + (k - 1)) if not (isinstance(p, int) and p + k < 2) else None
                w_make(pool, p + k, k % 2, 1, t1p, t2p).then_inc(s_wp, 1)
                pool.drain()
            w_bwd(0, 0)
            w_bwd(0, 1)
            with pool.Fori(1, PAIRS // 2) as i:
                for k in range(2):
                    w_bwd(2 * i, k)

            def g_bwd(p, k):
                if not (isinstance(p, int) and p + k < 2):
                    pool.wait_ge(s_yps, p + (k - 1))
                for h in range(2):
                    hs = slice(64 * h, 64 * h + 64)
                    src = BB[hs, :, 1:3, :].rearrange("p (d q) r c -> p d q r c", d=DIRS)[:, :, ds(p + k, 1), :, :]
                    pool.tensor_copy(Bm[hs, k % 2, :, :, GROUP * h:GROUP * (h + 1)],
                                     src.rearrange("p d q r c -> p d (q r) c"))
                    pool.drain()
                g_make(pool, p + k, k % 2, 1, t1p, t2p).then_inc(s_gp, 1)
                pool.drain()
            g_bwd(0, 0)
            g_bwd(0, 1)
            with pool.Fori(1, PAIRS // 2) as i:
                for k in range(2):
                    g_bwd(2 * i, k)

            with pool.Fori(0, HEADS // 4) as i:
                for k in range(4):
                    pool.wait_ge(s_bl[k], 32 * i + 32)
                    pool.tensor_tensor(bi[:, k, :, :], bi[:, k, :, :],
                                       mask[:, :].unsqueeze(1).to_broadcast([P, EWIN, GRID_W]), ALU.add)\
                        .then_inc(s_bm, 1)
            split_loop(pool, lo_unit, U_G, 8, 8)
            for k in range(8):
                lo_unit(pool, U_GLU + DEPTH, k)
            split_loop(pool, lo_unit, U_PROJ, 4, 8)
            split_loop(pool, lo_unit, U_OUT, 4, 8)
            norm_lo(pool, 1, NL)
            split_loop(pool, lo_unit, U_UP, FT // 4, 16)
            split_loop(pool, lo_unit, U_DOWN, FT // 2 - 1, 4)

        @block.scalar
        def _(act):
            for seeded in (s_ptsb, s_g, s_ge):
                act.sem_inc(seeded, SEED)
            act.dma_start(rows[:, 0, :], lam_re[0].rearrange("d (q g) n -> (d q) (g n)", g=2)).then_inc(s_par, 16)
            act.dma_start(rows[:, 1, :], lam_im[0].rearrange("d (q g) n -> (d q) (g n)", g=2)).then_inc(s_par, 16)
            act.dma_start(lst[:, 0:2], log_step[0].rearrange("d (q g) -> (d q) g", g=2)).then_inc(s_par, 16)
            act.dma_start(drow[:, 0, :], ssm_d[0].rearrange("(q c) -> q c", q=PAIRS)).then_inc(s_par, 16)
            for n, g in enumerate((norm1_g[0], norm2_g[0], final_g)):
                act.dma_start(grow[n * KT:(n + 1) * KT, :], g.rearrange("(k p) -> k p", p=P)).then_inc(s_par, 16)
            for n in range(3):
                act.dma_start(crow[n % 2 * FT:(n % 2 + 1) * FT, n // 2, :],
                              conv_w[0, n].rearrange("(k p) -> k p", p=P)).then_inc(s_par, 16)
            act.dma_start(crow[FT:2 * FT, 1, :], conv_b[0].rearrange("(k p) -> k p", p=P)).then_inc(s_par, 16)
            for r, b in enumerate((b_re, b_im)):
                for d in range(DIRS):
                    act.dma_start(braw[:, r, d * PAIRS:(d + 1) * PAIRS, :],
                                  b[0, d].rearrange("(q g) n c -> (g n) q c", g=2)).then_inc(s_par, 16)
            for r, c in enumerate((c_re, c_im)):
                for d in range(DIRS):
                    act.dma_start(cnat[:, d, :, r, :],
                                  c[0, d].rearrange("(k g) c n -> (g c) k n", k=KH)).then_inc(s_par, 16)
            for k in range(DEPTH):
                hi_unit(act, 0, k)

            def norm_squares(which, lo, n):
                src = xT if which else x0T
                with act.Fori(0, KT // 2) as i:
                    for k in range(2):
                        if which == 0:
                            act.wait_ge(s_xt, 2 * i + (k + 1))
                        act.wait_ge(s_sq_used, 2 * i + (KT * which + k - 1 + SEED))
                        act.activation(sq[:, k, 0:n], src[:, ds(2 * i + k, 1), lo:lo + n].rearrange("p k n -> p (k n)"),
                                       ACT.Square).then_inc(s_sq, 1)
                act.wait_ge(s_var, which + 1)
                act.activation(rstd[:, 0:n], rstd[:, 0:n], ACT.Sqrt).then_inc(s_sd, 1)

            def norm_hi(which, n):
                with act.Fori(0, KT // DEPTH) as i:
                    for k in range(DEPTH):
                        act.wait_ge(s_nt, DEPTH * i + (KT * which + k + 1))
                        act.activation(hnh[:, ds(DEPTH * i + k, 1), 0:n].rearrange("p k n -> p (k n)"),
                                       tr[:, k, 0:n], ACT.Copy).then_inc(s_nh, 1)

            norm_squares(0, 0, L)
            norm_hi(0, L)

            v = lambda n: prm[:, n, :]
            act.wait_ge(s_pcp, 1)
            act.activation(v(3), v(2), ACT.Exp).then_inc(s_pa, 1)
            act.wait_ge(s_pcp, 2)
            act.activation(v(6), v(4), ACT.Exp).then_inc(s_pa, 1)
            act.wait_ge(s_pcp, 3)
            act.activation(v(8), v(7), ACT.Sin)
            act.activation(v(9), v(7), ACT.Sin, scale=0.5).then_inc(s_pa, 1)
            for d in range(DIRS):
                for q in range(2):
                    n = 2 * d + q
                    act.wait_ge(s_ctp, n + 1)
                    for h in range(2):
                        hs = slice(64 * h, 64 * h + 64)
                        for sl, part, sign in ((0, 0, 1.0), (1, 1, -1.0), (2, 0, -1.0)):
                            src = ps[64 * part:64 * part + 64, 4 + n % 2, :].rearrange("p (q g c) -> p q g c", g=2, c=GROUP)
                            last = act.activation(CC[hs, d * PAIRS + 16 * q:d * PAIRS + 16 * (q + 1), sl, :],
                                                  src[:, :, h, :], ACT.Copy, scale=sign)
                    last.then_inc(s_ccp, 1)

            split_loop(act, hi_unit, U_U, ITERS_IN, 8)
            split_loop(act, hi_unit, U_K, ITERS_IN, 8)
            split_loop(act, hi_unit, U_V, ITERS_IN, 8)
            split_loop(act, hi_unit, U_Q, ITERS_IN, 8)

            def wt_copy(p, k):
                act.wait_ge(s_wtp, p + (k + 1))
                if not (isinstance(p, int) and p + k < 2):
                    act.wait_ge(s_sps, p + (k - 1))
                act.activation(WT[:, k % 2, :, :].rearrange("p a b -> p (a b)"), ps[:, 4 + k % 2, :], ACT.Copy)\
                   .then_inc(s_wts, 1)
            wt_copy(0, 0)
            wt_copy(0, 1)
            with act.Fori(1, PAIRS // 2) as i:
                for k in range(2):
                    wt_copy(2 * i, k)

            def tm_copy(p, k):
                act.wait_ge(s_kps, p + (k + 1))
                if not (isinstance(p, int) and p + k < 2):
                    act.wait_ge(s_yps, p + (k - 1))
                for j in range(CHUNK):
                    lo = (CHUNK - 1 - j) * 2 * GROUP
                    last = act.activation(Tm[32 * j:32 * j + 32, k % 2, :], ps[0:32, 4 + k % 2, lo:lo + P], ACT.Copy)
                last.then_inc(s_tm, 1)
            tm_copy(0, 0)
            tm_copy(0, 1)
            with act.Fori(1, PAIRS // 2) as i:
                for k in range(2):
                    tm_copy(2 * i, k)

            act.wait_ge(s_ysb, PAIRS)
            act.activation(yT[:, :, LIVE:L], yT[:, :, LIVE:L], ACT.Gelu_apprx_tanh).then_inc(s_yg, 1)
            act.drain()
            act.activation(ygh[:, :, :], yT[:, :, LIVE:L], ACT.Copy).then_inc(s_ygh, 1)

            def att_exp(i, k):
                act.wait_ge(s_nm, 4 * i + (k + 1) + SEED)
                for t in range(2):
                    last = act.activation(S[:, k % 2, t, :], S[:, k % 2, t, :], ACT.Exp,
                                          bias=stat[:, k, 0, t:t + 1], accum_out=stat[:, k, 1, t:t + 1])
                last.then_inc(s_e, 1)

            def att_pt(i, k):
                act.wait_ge(s_ptps, 4 * i + (k + 1) + SEED)
                if k < 2:
                    act.wait_ge(s_pv, 4 * i + SEED)
                else:
                    act.wait_ge(s_pv, 4 * i + (k - 1) + SEED)
                act.activation(PT[:, k % 2, :], ps[:, 4 + k % 2, :], ACT.Copy)
                two = ps[0:N_META, 2 * (k % 2):2 * (k % 2) + 2, L:L + P]
                act.activation(PT2[:, k % 2, :].rearrange("p (t q) -> p t q", t=2), two, ACT.Copy).then_inc(s_ptsb, 1)

            def att_hi(i, j):
                act.wait_ge(s_pv, 4 * i + 2 * (j + 1) + SEED)
                act.activation(anh[:, ds(2 * i + j, 1), 2:NL].rearrange("p k n -> p (k n)"), ps[:, 6 + j, 0:SEQ],
                               ACT.Copy).then_inc(s_ah, 1)

            with act.Fori(0, HEADS // 4) as i:
                att_exp(i, 0)
                att_exp(i, 1)
                att_pt(i, 0)
                att_exp(i, 2)
                att_pt(i, 1)
                att_hi(i, 0)
                att_exp(i, 3)
                att_pt(i, 2)
                att_pt(i, 3)
                att_hi(i, 1)
            act.wait_ge(s_m2, 1)
            act.activation(sm[:, :, :, :], sm[:, :, :, :], ACT.Exp).then_inc(s_m3, 1)
            act.wait_ge(s_m5, 1)
            act.activation(ptm[:, :], ps[0:N_META, 2, 0:2 * HEADS], ACT.Copy).then_inc(s_m6, 1)
            act.wait_ge(s_m7, 1)
            act.activation(anh[:, :, 0:2], ps[:, 3, 0:2 * KH].rearrange("p (b t) -> p b t", t=2), ACT.Copy)\
               .then_inc(s_m8, 1)

            with act.Fori(0, 8) as i:
                for k in range(2):
                    for n in range(4):
                        hi_unit(act, (U_G + DEPTH) + 8 * i, 4 * k + n)
                    act.wait_ge(s_used, 8 * i + (U_G + 4 * (k + 1)))
                    for m in range(2):
                        last = act.activation(gates[:, ds(4 * i + (2 * k + m), 1), :].rearrange("p k n -> p (k n)"),
                                              ps[:, 2 * k + m, 0:NL], ACT.Sigmoid)
                    last.then_inc(s_g, 1)

            for q in range(2):
                for n in range(4):
                    hi_unit(act, U_GLU + DEPTH, 4 * q + n)
                act.wait_ge(s_used, U_GLU + 4 * (q + 1))
                if q:
                    act.wait_ge(s_z, 4)
                for m in range(4):
                    act.activation(gt[:, m, :], ps[:, 4 * q + m, 0:NL], ACT.Sigmoid).then_inc(s_sg, 1)
                for m in range(4):
                    act.wait_ge(s_z, 4 * q + m + 1)
                    act.activation(zh[:, 4 * q + m, :], mt[:, m, :], ACT.Copy).then_inc(s_zh, 1)

            with act.Fori(0, 4) as i:
                for k in range(2):
                    for n in range(4):
                        hi_unit(act, (U_PROJ + DEPTH) + 8 * i, 4 * k + n)
                    for m in range(2):
                        act.wait_ge(s_mx, 4 * i + (2 * k + m + 1) + SEED)
                        act.activation(hnh[:, ds(4 * i + (2 * k + m), 1), 0:NL].rearrange("p k n -> p (k n)"),
                                       mt[:, 2 * k + m, :], ACT.Copy).then_inc(s_mh, 1)
            split_loop(act, hi_unit, U_OUT, 4, 8)
            act.wait_ge(s_h1, KT // 2 + SEED)
            norm_squares(1, LIVE, NL)
            norm_hi(1, NL)

            with act.Fori(0, FT // 4) as i:
                for k in range(2):
                    for n in range(4):
                        hi_unit(act, (U_UP + DEPTH) + 16 * i, 8 * k + n)
                    act.wait_ge(s_used, 16 * i + (U_UP + 8 * k + 4))
                    if k == 0:
                        act.wait_ge(s_ge, 4 * i + SEED)
                    for m in range(2):
                        f = 4 * i + (2 * k + m)
                        act.activation(cv[:, k, m, :], ps[:, 4 * k + m, 2:NL], ACT.Identity,
                                       scale=cvw[:, ds(f + FT, 1)], bias=cvw[:, ds(f + 3 * FT, 1)]).then_inc(s_c, 1)
                    for n in range(4, 8):
                        hi_unit(act, (U_UP + DEPTH) + 16 * i, 8 * k + n)
                    if k == 0:
                        act.wait_ge(s_fl, 4 * i + SEED)
                    for m in range(2):
                        act.wait_ge(s_cd, 4 * i + (2 * k + m + 1))
                        act.activation(ge[:, k, m, :], cv[:, k, m, :], ACT.Gelu_apprx_tanh).then_inc(s_ge, 1)
                    for m in range(2):
                        act.wait_ge(s_fm, 4 * i + (2 * k + m + 1) + SEED)
                        act.activation(ah[:, ds(4 * i + (2 * k + m), 1), :].rearrange("p k n -> p (k n)"),
                                       ge[:, k, m, :], ACT.Copy).then_inc(s_fh, 1)
            split_loop(act, hi_unit, U_DOWN, FT // 2 - 1, 4)
            act.wait_ge(s_h2, 1)
            norm_squares(2, N_META, SEQ)

        @block.vector
        def _(dve):
            for seeded in (s_nm, s_al, s_mx, s_h1, s_fm, s_fl, s_u, s_kev, s_vtd, s_vcp):
                dve.sem_inc(seeded, SEED)
            dve.wait_ge(s_par, 16 * 19)
            dve.tensor_copy(rows[:, 2, :].rearrange("p (g n) -> p g n", g=2),
                            lst[:, 0:2].unsqueeze(2).to_broadcast([DIRS * PAIRS, 2, STATE]))
            for j in range(1, CHUNK):
                last = dve.tensor_copy(drow[:, j, :], drow[:, 0, :])
            last.then_inc(s_rows, 1)
            for k in range(KT):
                dve.wait_ge(s_xtp, k + 1)
                dve.tensor_copy(x0T[:, k, :], ps[:, k % 4, 0:L]).then_inc(s_xt, 1)
            dve.wait_ge(s_ptp, 1)
            dve.tensor_copy(gains[:, :], ps[:, 7, 0:3 * KT])
            dve.tensor_copy(cvw[:, :], ps[:, 7, 48:48 + 4 * FT])
            dve.tensor_copy(drep[:, :], ps[:, 7, 416:448])
            dve.tensor_copy(prm[:, 0:3, :], ps[:, 7, 224:416].rearrange("p (a b) -> p a b", a=3)).then_inc(s_pcp, 1)
            dve.drain()

            def norm(which, lo, n):
                dve.wait_ge(s_ss, which + 1)
                dve.tensor_scalar(rstd[:, 0:n], ps[:, 6, 0:n], 1.0 / D_MODEL, EPS, ALU.mult, ALU.add).then_inc(s_var, 1)
                dve.wait_ge(s_sd, which + 1)
                dve.reciprocal(rstd[:, 0:n], rstd[:, 0:n])
                dve.drain()
                src = xT if which else x0T
                if which < 2:
                    with dve.Fori(0, KT // DEPTH) as i:
                        for k in range(DEPTH):
                            dve.wait_ge(s_nl, DEPTH * i + (KT * which + SEED))
                            dve.scalar_tensor_tensor(
                                out=tr[:, k, 0:n], in0=src[:, ds(DEPTH * i + k, 1), lo:lo + n].rearrange("p k n -> p (k n)"),
                                scalar=gains[:, ds(DEPTH * i + (KT * which + k), 1)], in1=rstd[:, 0:n],
                                op0=ALU.mult, op1=ALU.mult).then_inc(s_nt, 1)

            norm(0, 0, L)

            v = lambda n: prm[:, n, :]

            def mul(o, a, b):
                dve.tensor_tensor(o, a, b, ALU.mult)

            def cmul(o, a, b, t):
                mul(t[0], a[0], b[0])
                mul(t[1], a[1], b[1])
                mul(t[2], a[0], b[1])
                mul(t[3], a[1], b[0])
                dve.drain()
                dve.tensor_tensor(o[0], t[0], t[1], ALU.subtract)
                dve.tensor_tensor(o[1], t[2], t[3], ALU.add)
                dve.drain()

            dve.wait_ge(s_pa, 1)
            mul(v(4), v(0), v(3))
            mul(v(5), v(1), v(3))
            dve.drain()
            dve.tensor_scalar(v(10), v(5), 1.0 / (2 * math.pi), ROUND, ALU.mult, ALU.add).then_inc(s_pcp, 1)
            dve.drain()
            dve.tensor_scalar(v(10), v(10), ROUND, None, ALU.subtract)
            for c in (TWO_PI_HI, TWO_PI_MID, TWO_PI_LO):
                dve.drain()
                dve.scalar_tensor_tensor(out=v(5), in0=v(10), scalar=-c, in1=v(5), op0=ALU.mult, op1=ALU.add)
            dve.drain()
            dve.tensor_scalar(v(7), v(5), PI_BELOW, -PI_BELOW, ALU.min, ALU.max).then_inc(s_pcp, 1)
            dve.wait_ge(s_pa, 3)
            mul(v(10), v(9), v(9))
            dve.drain()
            dve.tensor_scalar(v(10), v(10), -2.0, 1.0, ALU.mult, ALU.add)
            dve.memset(pw[:, 0, 0, :], 1.0)
            dve.memset(pw[:, 0, 1, :], 0.0)
            dve.drain()
            a1 = (pw[:, 1, 0, :], pw[:, 1, 1, :])
            a2 = (pw[:, 2, 0, :], pw[:, 2, 1, :])
            tmp = [v(n) for n in (11, 12, 13, 14)]
            mul(a1[0], v(6), v(10))
            mul(a1[1], v(6), v(8))
            dve.drain()
            cmul(a2, a1, a1, tmp)
            cmul((pw[:, 3, 0, :], pw[:, 3, 1, :]), a2, a1, tmp)
            cmul((pw[:, 4, 0, :], pw[:, 4, 1, :]), a2, a2, tmp)
            dve.tensor_scalar(v(15), a1[0], 1.0, None, ALU.subtract)
            mul(v(16), v(0), v(0))
            mul(v(17), v(1), v(1))
            dve.drain()
            dve.tensor_tensor(v(16), v(16), v(17), ALU.add)
            mul(v(18), v(15), v(0))
            mul(v(19), a1[1], v(1))
            mul(v(20), a1[1], v(0))
            mul(v(21), v(15), v(1))
            dve.drain()
            dve.reciprocal(v(16), v(16))
            dve.tensor_tensor(v(18), v(18), v(19), ALU.add)
            dve.tensor_tensor(v(20), v(20), v(21), ALU.subtract)
            dve.drain()
            mul(v(18), v(18), v(16))
            mul(v(20), v(20), v(16))
            dve.drain()
            full = [P, DIRS * PAIRS, GROUP]
            qr = v(18).unsqueeze(2).to_broadcast(full)
            qi = v(20).unsqueeze(2).to_broadcast(full)
            ta = btmp[:, 0, :].rearrange("p (a b) -> p a b", b=GROUP)
            tb = btmp[:, 1, :].rearrange("p (a b) -> p a b", b=GROUP)
            mul(ta, qr, braw[:, 0, :, :])
            mul(tb, qi, braw[:, 1, :, :])
            dve.drain()
            dve.tensor_tensor(BB[:, :, 1, :], ta, tb, ALU.subtract)
            dve.drain()
            mul(ta, qr, braw[:, 1, :, :])
            mul(tb, qi, braw[:, 0, :, :])
            dve.drain()
            dve.tensor_tensor(BB[:, :, 2, :], ta, tb, ALU.add)
            dve.drain()
            dve.tensor_scalar(BB[:, :, 0, :], BB[:, :, 2, :], -1.0, None, ALU.mult)
            dve.memset(pwW[:, :, :, :, :], 0.0)
            dve.memset(pwG[:, :, :, :, :], 0.0)
            dve.drain()
            for h in range(2):
                hs = slice(64 * h, 64 * h + 64)
                for d in range(DIRS):
                    dq = slice(d * PAIRS, (d + 1) * PAIRS)
                    kin = pw[hs, 0:CHUNK, :, dq] if d else pw[hs, CHUNK - 1::-1, :, dq]
                    kout = pw[hs, CHUNK::-1, :, dq] if d else pw[hs, :, :, dq]
                    for r in range(2):
                        dve.tensor_copy(pwW[hs, dq, r, :, h], kin[:, :, r, :].rearrange("p k q -> p q k"))
                        dve.tensor_copy(pwG[hs, dq, r, :, h], kout[:, :, r, :].rearrange("p k q -> p q k"))
            a4r = pw[:, CHUNK, 0, :].rearrange("p (d q) -> p d q", d=DIRS)
            a4i = pw[:, CHUNK, 1, :].rearrange("p (d q) -> p d q", d=DIRS)
            for r in range(2):
                dve.tensor_copy(A4R[:, :, r, :], a4r)
            dve.tensor_copy(A4I[:, :, 0, :], a4i)
            dve.tensor_scalar(A4I[:, :, 1, :], a4i, -1.0, None, ALU.mult)
            dve.drain()
            dve.nop().then_inc(s_pd, 1)

            dve.wait_ge(s_spill, 16)
            with dve.Fori(0, ITERS_IN) as i:
                for k in range(2):
                    dve.wait_ge(s_used, 8 * i + (U_U + 4 * (k + 1)))
                    for m in range(2):
                        for b in range(PB):
                            for j in range(CHUNK):
                                src = ps[32 * b:32 * b + 32, 2 * k + m, 0:L].rearrange("p (c j) -> p j c", j=CHUNK)
                                pair = i * (4 * PB) + ((2 * k + m) * PB + b)
                                last = dve.tensor_copy(U[32 * j:32 * j + 32, ds(pair, 1), :].rearrange("p a c -> p (a c)"),
                                                       src[:, j, :])
                    last.then_inc(s_u, 1)

            def qkv_blocks(first, n, what, i, start):
                for k in range(2):
                    dve.wait_ge(s_used, 8 * i + (first + 4 * (k + 1)))
                    if what == "v":
                        dve.wait_ge(s_kst, 128)
                        dve.wait_ge(s_vtp, 2 * i + SEED)
                    elif what == "q":
                        dve.wait_ge(s_vtp, 4 + SEED)
                        dve.wait_ge(s_kst, 64 * i + 128)
                    elif not start:
                        dve.wait_ge(s_kst, 64 * i)
                    for m in range(2):
                        dve.tensor_copy(stg[:, k, m, 0:n], ps[:, 2 * k + m, 0:n])
                        tile = ds(4 * i + (2 * k + m), 1)
                        if what == "k":
                            dve.tensor_copy(km[:, tile, :].rearrange("p a b -> p (a b)"), ps[:, 2 * k + m, 0:N_META])
                        if what == "q":
                            dve.tensor_copy(qm[:, tile, :].rearrange("p a b -> p (a b)"), ps[:, 2 * k + m, 0:2])
                    dve.drain()
                    dve.nop().then_inc(s_vtd if what == "v" else s_kev, 1)
                if what == "v":
                    for k in range(2):
                        dve.wait_ge(s_vtp, 2 * i + (k + 1 + SEED))
                        if k or not start:
                            dve.wait_ge(s_vst, 64 * i + 32 * k)
                        dve.tensor_copy(vst[:, 0:2, :], ps[:, 4 + 2 * k, :].rearrange("p (a b) -> p a b", a=2))
                        dve.tensor_copy(vst[0:N_META, 2, :], ps[0:N_META, 5 + 2 * k, 0:CB])
                        dve.tensor_copy(vm[:, ds(4 * i + 2 * k, 2), :].rearrange("p a b -> p (a b)"),
                                        ps[0:N_META, 4 + 2 * k, 0:CB])
                        dve.drain()
                        dve.nop().then_inc(s_vcp, 1)

            for first, n, what in ((U_K, L, "k"), (U_V, L, "v"), (U_Q, NL, "q")):
                qkv_blocks(first, n, what, 0, True)
                with dve.Fori(1, ITERS_IN) as i:
                    qkv_blocks(first, n, what, i, False)

            dve.memset(X[:, 0, :, :], 0.0)

            def w_fwd(p, k):
                if not (isinstance(p, int) and p + k < 2):
                    dve.wait_ge(s_wtp, p + (k - 1))
                w_make(dve, p + k, k % 2, 0, t1v, t2v).then_inc(s_wd, 1)
                dve.drain()

            def s_copy(p, k):
                dve.wait_ge(s_sps, p + (k + 1))
                dst = X[:, 1:NCH + 1, :, ds(p + k, 1)].rearrange("p c r q -> p (r q) c")
                src = ps[:, 6 + k % 2, 0:4 * NCH].rearrange("p (r c) -> p r c", c=NCH)
                dve.tensor_copy(dst[:, 0:2, :], src[:, 0:2, :])
                dve.tensor_copy(dst[:, 2:4, :], src[:, 2:4, ::-1]).then_inc(s_ssb, 1)

            w_fwd(0, 0)
            w_fwd(0, 1)
            with dve.Fori(0, PAIRS // 2 - 1) as i:
                s_copy(2 * i, 0)
                w_fwd(2 * i, 2)
                s_copy(2 * i, 1)
                w_fwd(2 * i, 3)
            s_copy(PAIRS - 2, 0)
            s_copy(PAIRS - 2, 1)
            dve.drain()

            a_re = A4R[:, :, :, :].rearrange("p d r q -> p (d r q)")
            a_im = A4I[:, :, :, :].rearrange("p d r q -> p (d r q)")
            swapped = sc2[:, :].rearrange("p (d r q) -> p d r q", d=DIRS, r=2)[:, :, ::-1, :]
            with dve.Fori(0, NCH - 1) as c:
                here = X[:, ds(c, 1), :, :].rearrange("p c r q -> p (c r q)")
                after = X[:, ds(c + 1, 1), :, :].rearrange("p c r q -> p (c r q)")
                after4 = X[:, ds(c + 1, 1), :, :].rearrange("p c (d r) q -> p (c d) r q", d=DIRS)
                mul(sc1[:, :], here, a_re)
                mul(sc2[:, :], here, a_im)
                dve.drain()
                dve.tensor_tensor(after, after, sc1[:, :], ALU.add)
                dve.drain()
                dve.tensor_tensor(after4, after4, swapped, ALU.add)
                dve.drain()
            dve.nop().then_inc(s_scan, 1)

            def g_fwd(p, k):
                if not (isinstance(p, int) and p + k < 2):
                    dve.wait_ge(s_yps, p + (k - 1))
                g_make(dve, p + k, k % 2, 0, t1v, t2v).then_inc(s_gd, 1)
                dve.drain()

            def y_copy(p, i, k):
                dve.wait_ge(s_yps, p + (k + 1))
                b = k % PB
                for j in range(CHUNK):
                    js = slice(32 * j, 32 * j + 32)
                    dst = yT[32 * b:32 * b + 32, ds(i, 1), :].rearrange("p a (c j) -> p j (a c)", j=CHUNK)[:, j, :]
                    last = dve.scalar_tensor_tensor(
                        out=dst, in0=U[js, ds(p + k, 1), :].rearrange("p a c -> p (a c)"), scalar=drep[js, ds(p + k, 1)],
                        in1=ps[js, 6 + k % 2, 0:NCH], op0=ALU.mult, op1=ALU.add)
                last.then_inc(s_ysb, 1)

            g_fwd(0, 0)
            g_fwd(0, 1)
            with dve.Fori(0, PAIRS // PB - 1) as i:
                for k in range(PB):
                    y_copy(PB * i, i, k)
                    g_fwd(PB * i, k + 2)
            last_b = PAIRS // PB - 1
            for k in range(PB):
                y_copy(PAIRS - PB, last_b, k)
                if k < PB - 2:
                    g_fwd(PAIRS - PB, k + 2)

            dve.wait_ge(s_ygh, 1)
            dve.tensor_tensor(ygl[:, :, :], yT[:, :, LIVE:L], ygh[:, :, :].bitcast(F), ALU.subtract).then_inc(s_ygl, 1)

            def att_scores(i, k):
                dve.wait_ge(s_qk, 4 * i + (k + 1))
                dve.wait_ge(s_bm, 4 * i + (k + 1))
                if k < 2:
                    dve.wait_ge(s_ptps, 4 * i + SEED)
                else:
                    dve.wait_ge(s_ptps, 4 * i + (k - 1) + SEED)
                bank = 2 * (k % 2)
                for t in range(2):
                    e0 = QROWS * (1 - t)
                    dve.scalar_tensor_tensor(
                        out=S[:, k % 2, t, N_META:L], in0=ps[:, bank + t, N_META:L], scalar=SCALE,
                        in1=bi[:, k, e0:e0 + GRID_ROWS, :].rearrange("p a b -> p (a b)"), op0=ALU.mult, op1=ALU.add)
                dve.tensor_scalar(S[:, k % 2, :, 0:N_META], ps[:, bank:bank + 2, 0:N_META], SCALE, None, ALU.mult)
                dve.drain()
                dve.reduce_max(stat[:, k, 0, :], S[:, k % 2, :, :], AX.X)
                dve.drain()
                dve.tensor_scalar(stat[:, k, 0, :], stat[:, k, 0, :], -1.0, None, ALU.mult).then_inc(s_nm, 1)

            def att_norm(i, k):
                dve.wait_ge(s_e, 4 * i + (k + 1))
                dve.reciprocal(stat[:, k, 1, :], stat[:, k, 1, :])
                dve.drain()
                for t in range(2):
                    last = dve.tensor_scalar(S[:, k % 2, t, :], S[:, k % 2, t, :], stat[:, k, 1, t:t + 1], None, ALU.mult)
                last.then_inc(s_p, 1)

            def att_lo(i, j):
                dve.wait_ge(s_ah, 2 * i + (j + 1))
                dve.tensor_tensor(anl[:, ds(2 * i + j, 1), 2:NL].rearrange("p k n -> p (k n)"), ps[:, 6 + j, 0:SEQ],
                                  anh[:, ds(2 * i + j, 1), 2:NL].rearrange("p k n -> p (k n)").bitcast(F),
                                  ALU.subtract).then_inc(s_al, 1)

            with dve.Fori(0, HEADS // 4) as i:
                att_scores(i, 0)
                att_scores(i, 1)
                att_norm(i, 0)
                att_scores(i, 2)
                att_norm(i, 1)
                att_lo(i, 0)
                att_scores(i, 3)
                att_norm(i, 2)
                att_norm(i, 3)
                att_lo(i, 1)

            dve.wait_ge(s_m1, 1)
            smf = sm[:, :, :, :].rearrange("p a b c -> p a (b c)")
            sm3 = sm[:, :, :, :].rearrange("p a b c -> p (a b) c")
            dve.tensor_scalar(smf, ps[0:2, 0:2, 0:P], SCALE, None, ALU.mult)
            dve.drain()
            dve.reduce_max(smx[:, 0, :], sm3, AX.X)
            dve.drain()
            dve.tensor_tensor(sm3, sm3, smx[:, 0, :].unsqueeze(2).to_broadcast([2, HEADS, N_META]), ALU.subtract)\
               .then_inc(s_m2, 1)
            dve.wait_ge(s_m3, 1)
            dve.reduce_sum(smx[:, 1, :], sm3, AX.X)
            dve.drain()
            dve.reciprocal(smx[:, 1, :], smx[:, 1, :])
            dve.drain()
            dve.tensor_tensor(sm3, sm3, smx[:, 1, :].unsqueeze(2).to_broadcast([2, HEADS, N_META]), ALU.mult)\
               .then_inc(s_m4, 1)
            dve.wait_ge(s_m8, 1)
            dve.tensor_tensor(anl[:, :, 0:2], ps[:, 3, 0:2 * KH].rearrange("p (b t) -> p b t", t=2),
                              anh[:, :, 0:2].bitcast(F), ALU.subtract).then_inc(s_al, 1)

            for n in range(KH):
                dve.wait_ge(s_sg, n + 1)
                if n >= 4:
                    dve.wait_ge(s_zl, n - 3)
                dve.tensor_tensor(mt[:, n % 4, :], yT[:, n, LIVE:L], gt[:, n % 4, :], ALU.mult).then_inc(s_z, 1)
                if n % 4 == 3:
                    for m in range(n - 3, n + 1):
                        dve.wait_ge(s_zh, m + 1)
                        dve.tensor_tensor(zl[:, m, :], mt[:, m % 4, :], zh[:, m, :].bitcast(F), ALU.subtract).then_inc(s_zl, 1)

            dve.wait_ge(s_g, 16 + SEED)
            dve.wait_ge(s_zl, KH)
            with dve.Fori(0, 4) as i:
                for k in range(2):
                    dve.wait_ge(s_used, 8 * i + (U_PROJ + 4 * (k + 1)))
                    for m in range(2):
                        f = 4 * i + (2 * k + m)
                        dve.tensor_tensor(mt[:, 2 * k + m, :], ps[:, 4 * k + m, 0:NL],
                                          gates[:, ds(f, 1), :].rearrange("p k n -> p (k n)"), ALU.mult)
                        dve.tensor_tensor(gt[:, 2 * k + m, :], ps[:, 4 * k + 2 + m, 0:NL],
                                          gates[:, ds(f + KT, 1), :].rearrange("p k n -> p (k n)"), ALU.mult)
                    dve.drain()
                    for m in range(2):
                        dve.tensor_tensor(mt[:, 2 * k + m, :], mt[:, 2 * k + m, :], gt[:, 2 * k + m, :], ALU.add).then_inc(s_mx, 1)
                    for m in range(2):
                        f = 4 * i + (2 * k + m)
                        dve.wait_ge(s_mh, f + 1)
                        dve.tensor_tensor(hnl[:, ds(f, 1), 0:NL].rearrange("p k n -> p (k n)"), mt[:, 2 * k + m, :],
                                          hnh[:, ds(f, 1), 0:NL].rearrange("p k n -> p (k n)").bitcast(F),
                                          ALU.subtract).then_inc(s_ml, 1)

            dve.wait_ge(s_xre, 16)
            with dve.Fori(0, 4) as i:
                for k in range(2):
                    dve.wait_ge(s_used, 8 * i + (U_OUT + 4 * (k + 1)))
                    for m in range(2):
                        h = xT[:, ds(4 * i + (2 * k + m), 1), LIVE:L].rearrange("p k n -> p (k n)")
                        last = dve.tensor_tensor(h, h, ps[:, 2 * k + m, 0:NL], ALU.add)
                    last.then_inc(s_h1, 1)
            norm(1, LIVE, NL)

            with dve.Fori(0, FT // 4) as i:
                for k in range(2):
                    for m in range(2):
                        f = 4 * i + (2 * k + m)
                        dve.wait_ge(s_c, f + 1)
                        c = cv[:, k, m, :]
                        dve.scalar_tensor_tensor(out=c, in0=ps[:, 4 * k + m, 1:NL - 1], scalar=cvw[:, ds(f, 1)], in1=c,
                                                 op0=ALU.mult, op1=ALU.add)
                        dve.drain()
                        dve.scalar_tensor_tensor(out=cv[:, k, m, 0:SEQ - 1], in0=ps[:, 4 * k + m, 3:NL],
                                                 scalar=cvw[:, ds(f + 2 * FT, 1)], in1=cv[:, k, m, 0:SEQ - 1],
                                                 op0=ALU.mult, op1=ALU.add).then_inc(s_cd, 1)
                    dve.wait_ge(s_used, 16 * i + (U_UP + 8 * (k + 1)))
                    for m in range(2):
                        dve.wait_ge(s_ge, 4 * i + (2 * k + m + 1) + SEED)
                        dve.tensor_tensor(ge[:, k, m, :], ge[:, k, m, :], ps[:, 4 * k + 2 + m, 0:SEQ], ALU.mult)\
                           .then_inc(s_fm, 1)
                    for m in range(2):
                        f = 4 * i + (2 * k + m)
                        dve.wait_ge(s_fh, f + 1)
                        dve.tensor_tensor(al[:, ds(f, 1), :].rearrange("p k n -> p (k n)"), ge[:, k, m, :],
                                          ah[:, ds(f, 1), :].rearrange("p k n -> p (k n)").bitcast(F),
                                          ALU.subtract).then_inc(s_fl, 1)

            dve.wait_ge(s_used, U_END)
            for m in range(0, KT, 2):
                h = xT[:, m:m + 2, N_META:L]
                last = dve.tensor_tensor(h, h, ps[:, m // 2, :].rearrange("p (a b) -> p a b", a=2), ALU.add)
            last.then_inc(s_h2, 1)
            norm(2, N_META, SEQ)
            for k in range(KT):
                if k >= DEPTH:
                    dve.wait_ge(s_ot, k // DEPTH)
                dve.scalar_tensor_tensor(out=tr[:, k % DEPTH, 0:SEQ], in0=xT[:, k, N_META:L],
                                         scalar=gains[:, 2 * KT + k:2 * KT + k + 1], in1=rstd[:, 0:SEQ],
                                         op0=ALU.mult, op1=ALU.mult).then_inc(s_nt, 1)
                if k % DEPTH == DEPTH - 1:
                    n = k // DEPTH
                    dve.wait_ge(s_ot, n + 1)
                    for t in range(2):
                        last = dve.tensor_copy(otok[:, t, 512 * n:512 * (n + 1)], ps[:, 2 * (n % 2) + t, :])
                    dve.drain()
                    dve.nop().then_inc(s_oc, 1)

        @block.tensor
        def _(pe):
            for seeded in (s_pv, s_sq_used, s_vtp, s_ptps):
                pe.sem_inc(seeded, SEED)
            mm = nc.tensor.matmul

            def product(base_u, k0, units, xh, xl, lo, n, banks, kt0=0, last_unit=True):
                kts = units * UKT
                for q in range(units):
                    k = k0 + q
                    pe.wait_ge(s_lo, base_u + (k + 1))
                    for m in range(2):
                        for t in range(UKT):
                            kt = q * UKT + t
                            cols = slice(t * CB + m * P, t * CB + (m + 1) * P)
                            o = ps[:, banks[m], 0:n]
                            mm(o, slot(whi, k)[:, cols], xh[:, kt, lo:lo + n], start=kt == 0, stop=False)
                            mm(o, slot(whi, k)[:, cols], xl[:, kt, lo:lo + n], start=False, stop=False)
                            ins = mm(o, slot(wlo, k)[:, cols], xh[:, kt, lo:lo + n], start=False, stop=kt == kts - 1)
                    ins.then_inc(s_used, 1)

            pe.wait_ge(s_x, 64)
            pe.wait_ge(s_const, 2)
            for k in range(KT):
                if k >= 4:
                    pe.wait_ge(s_xt, k - 3)
                cs = slice(k * P, (k + 1) * P)
                nc.tensor.transpose(ps[:, k % 4, 0:P], xtok[:, 0, cs], ident[:, :])
                nc.tensor.transpose(ps[:, k % 4, P:2 * P], xtok[:, 1, cs], ident[:, :])
                nc.tensor.transpose(ps[:, k % 4, 2 * P:L], xtok[0:N_META, 2, cs], ident[0:N_META, 0:N_META]).then_inc(s_xtp, 1)
            pe.wait_ge(s_par, 16 * 19)
            pe.wait_ge(s_rows, 1)
            nc.tensor.transpose(ps[:, 7, 0:48], grow[:, :], ident[0:48, 0:48])
            for n in range(2):
                nc.tensor.transpose(ps[:, 7, 48 + 88 * n:48 + 88 * (n + 1)], crow[:, n, :], ident[0:88, 0:88])
            for n in range(3):
                nc.tensor.transpose(ps[:, 7, 224 + 64 * n:224 + 64 * (n + 1)], rows[:, n, :], ident[0:64, 0:64])
            nc.tensor.transpose(ps[:, 7, 416:448], drow[:, :, :].rearrange("p a b -> p (a b)"), ident[0:32, 0:32])\
              .then_inc(s_ptp, 1)

            def norm_sums(which, n):
                for k in range(KT):
                    pe.wait_ge(s_sq, KT * which + k + 1)
                    ins = mm(ps[:, 6, 0:n], ones[:, :], sq[:, k % 2, 0:n], start=k == 0, stop=k == KT - 1)
                    ins.then_inc(s_sq_used, 1)
                pe.wait_ge(s_sq_used, KT * (which + 1) + SEED)
                pe.nop().then_inc(s_ss, 1)

            norm_sums(0, L)
            for n in range(4):
                d, q = n // 2, n % 2
                if n >= 2:
                    pe.wait_ge(s_ccp, n - 1)
                for b in range(4):
                    ins = nc.tensor.transpose(ps[:, 4 + n % 2, b * P:(b + 1) * P],
                                              cnat[:, d, 4 * q + b, :, :].rearrange("p r n -> p (r n)"), ident[:, :])
                ins.then_inc(s_ctp, 1)

            pe.wait_ge(s_nl, KT + SEED)
            for first, lo, n, name in ((U_U, 0, L, "u"), (U_K, 0, L, "k"), (U_V, 0, L, "v"), (U_Q, LIVE, NL, "q")):
                with pe.Fori(0, ITERS_IN) as i:
                    for k in range(2):
                        if name == "u":
                            pe.wait_ge(s_u, 2 * i + SEED)
                        elif name == "k":
                            pe.wait_ge(s_u, 4 + SEED)
                            pe.wait_ge(s_kev, 2 * i + SEED)
                        elif name == "v":
                            pe.wait_ge(s_kev, 4 + SEED)
                            pe.wait_ge(s_vtd, 2 * i + SEED)
                        else:
                            pe.wait_ge(s_vtd, 4 + SEED)
                            pe.wait_ge(s_kev, 2 * i + 4 + SEED)
                        product(first + 8 * i, 4 * k, 4, hnh, hnl, lo, n, (2 * k, 2 * k + 1))
                    if name == "v":
                        for k in range(2):
                            pe.wait_ge(s_vtd, 2 * i + (k + 1) + SEED)
                            pe.wait_ge(s_vcp, 2 * i + SEED)
                            for m in range(2):
                                for t in range(2):
                                    nc.tensor.transpose(ps[:, 4 + 2 * k, t * CB + m * P:t * CB + (m + 1) * P],
                                                        stg[:, k, m, t * P:(t + 1) * P], ident[:, :])
                                ins = nc.tensor.transpose(ps[0:N_META, 5 + 2 * k, m * P:(m + 1) * P],
                                                          stg[:, k, m, 2 * P:L], ident[:, :])
                            ins.then_inc(s_vtp, 1)

            def w_trans(p, k):
                pe.wait_ge(s_wd, p + (k + 1))
                pe.wait_ge(s_wp, p + (k + 1))
                if not (isinstance(p, int) and p + k < 2):
                    pe.wait_ge(s_wts, p + (k - 1))
                for d in range(DIRS):
                    for r in range(2):
                        n = 2 * d + r
                        ins = nc.tensor.transpose(ps[:, 4 + k % 2, n * P:(n + 1) * P], Wn[:, k % 2, d, r, :], ident[:, :])
                ins.then_inc(s_wtp, 1)

            def chunk_in(p, k):
                pe.wait_ge(s_wts, p + (k + 1))
                if not (isinstance(p, int) and p + k < 2):
                    pe.wait_ge(s_ssb, p + (k - 1))
                for n in range(2 * DIRS):
                    u = U[:, ds(p + k, 1), :].rearrange("p a c -> p (a c)")
                    ins = mm(ps[:, 6 + k % 2, n * NCH:(n + 1) * NCH], WT[:, k % 2, n, :], u, start=True, stop=True)
                ins.then_inc(s_sps, 1)

            w_trans(0, 0)
            w_trans(0, 1)
            chunk_in(0, 0)
            with pe.Fori(1, PAIRS // 2) as i:
                w_trans(2 * i, 0)
                chunk_in(2 * i - 2, 1)
                w_trans(2 * i, 1)
                chunk_in(2 * i, 0)
            chunk_in(PAIRS - 2, 1)

            def kernel(p, k):
                pe.wait_ge(s_gd, p + (k + 1))
                pe.wait_ge(s_gp, p + (k + 1))
                if not (isinstance(p, int) and p + k < 2):
                    pe.wait_ge(s_tm, p + (k - 1))
                g = lambda d, r, a, b: Gn[:, k % 2, d, r, 32 * a:32 * b]
                bm = lambda d, r: Bm[:, k % 2, d, r, :]
                o = lambda a, b: ps[0:32, 4 + k % 2, 32 * a:32 * b]
                for r in range(2):
                    mm(o(0, CHUNK - 1), bm(1, r), g(1, r, 1, CHUNK), start=r == 0, stop=r == 1)
                for n in range(4):
                    d, r = n // 2, n % 2
                    e = CHUNK * d
                    mm(o(CHUNK - 1, CHUNK), bm(d, r), g(d, r, e, e + 1), start=n == 0, stop=n == 3)
                for r in range(2):
                    ins = mm(o(CHUNK, 2 * CHUNK - 1), bm(0, r), g(0, r, 1, CHUNK), start=r == 0, stop=r == 1)
                ins.then_inc(s_kps, 1)

            def chunk_out(p, k):
                pe.wait_ge(s_tm, p + (k + 1))
                if not (isinstance(p, int) and p + k < 2):
                    pe.wait_ge(s_ysb, p + (k - 1))
                o = ps[:, 6 + k % 2, 0:NCH]
                mm(o, Tm[:, k % 2, :], U[:, ds(p + k, 1), :].rearrange("p a c -> p (a c)"), start=True, stop=False)
                for n in range(2 * DIRS):
                    d, r = n // 2, n % 2
                    st = X[:, 0:NCH, n, ds(p + k, 1)].rearrange("p c q -> p (c q)")
                    a = 32 * (1 - d)
                    ins = mm(o[:, ::-1] if d else o, Gn[:, k % 2, d, r, a:a + P], st, start=False, stop=n == 3)
                ins.then_inc(s_yps, 1)

            pe.wait_ge(s_ssb, PAIRS)
            kernel(0, 0)
            kernel(0, 1)
            pe.wait_ge(s_scan, 1)
            chunk_out(0, 0)
            with pe.Fori(1, PAIRS // 2) as i:
                kernel(2 * i, 0)
                chunk_out(2 * i - 2, 1)
                kernel(2 * i, 1)
                chunk_out(2 * i, 0)
            chunk_out(PAIRS - 2, 1)

            def scores(i, k):
                j, hh = k // 2, k % 2
                if hh == 0:
                    pe.wait_ge(s_qkv[j], 64 * i + 64)
                if k < 2:
                    pe.wait_ge(s_nm, 4 * i + SEED)
                    pe.wait_ge(s_ptsb, 4 * i + SEED)
                else:
                    pe.wait_ge(s_nm, 4 * i + (k - 1) + SEED)
                    pe.wait_ge(s_ptsb, 4 * i + (k - 1) + SEED)
                hs = slice(DH * hh, DH * (hh + 1))
                for t in range(2):
                    ins = mm(ps[:, 2 * hh + t, 0:L], qs[hs, j, 2 + t * P:2 + (t + 1) * P], ks[hs, j, :], start=True, stop=True)
                ins.then_inc(s_qk, 1)

            def probs_t(i, k):
                pe.wait_ge(s_p, 4 * i + (k + 1))
                pe.wait_ge(s_ptsb, 4 * i + (k - 1) + SEED) if k >= 2 else pe.wait_ge(s_ptsb, 4 * i + SEED)
                for t in range(2):
                    for c in range(2):
                        nc.tensor.transpose(ps[:, 4 + k % 2, c * SEQ + t * P:c * SEQ + (t + 1) * P],
                                            S[:, k % 2, t, c * P:(c + 1) * P], ident[:, :])
                    ins = nc.tensor.transpose(ps[0:N_META, 2 * (k % 2) + t, L:L + P], S[:, k % 2, t, 2 * P:L], ident[:, :])
                ins.then_inc(s_ptps, 1)

            def values(i, k):
                j, hh = k // 2, k % 2
                pe.wait_ge(s_ptsb, 4 * i + (k + 1) + SEED)
                if hh == 0:
                    pe.wait_ge(s_al, 2 * i + SEED)
                hs = slice(DH * hh, DH * (hh + 1))
                o = ps[hs, 6 + j, 0:SEQ]
                mm(o, vs[:, j, 0, hs], PT[:, k % 2, 0:SEQ], start=True, stop=False)
                mm(o, vs[:, j, 1, hs], PT[:, k % 2, SEQ:2 * SEQ], start=False, stop=False)
                mm(o, vs[0:N_META, j, 2, hs], PT2[:, k % 2, :], start=False, stop=True).then_inc(s_pv, 1)

            with pe.Fori(0, HEADS // 4) as i:
                scores(i, 0)
                scores(i, 1)
                probs_t(i, 0)
                values(i, 0)
                scores(i, 2)
                probs_t(i, 1)
                values(i, 1)
                scores(i, 3)
                probs_t(i, 2)
                values(i, 2)
                probs_t(i, 3)
                values(i, 3)
            pe.wait_ge(s_ptsb, HEADS + SEED)
            for h in range(HEADS):
                b, hh = h // 2, h % 2
                hs = slice(DH * hh, DH * (hh + 1))
                ins = mm(ps[0:2, hh, b * N_META:(b + 1) * N_META], qm[hs, b, :], km[hs, b, :], start=True, stop=True)
            ins.then_inc(s_m1, 1)
            pe.wait_ge(s_m4, 1)
            for h in range(HEADS):
                b, hh = h // 2, h % 2
                ins = nc.tensor.transpose(ps[0:N_META, 2, 2 * h:2 * h + 2], sm[:, hh, b, :], ident[0:2, 0:2])
            ins.then_inc(s_m5, 1)
            pe.wait_ge(s_m6, 1)
            for h in range(HEADS):
                b, hh = h // 2, h % 2
                hs = slice(DH * hh, DH * (hh + 1))
                ins = mm(ps[hs, 3, 2 * b:2 * b + 2], vm[:, b, hs], ptm[:, 2 * h:2 * h + 2], start=True, stop=True)
            ins.then_inc(s_m7, 1)
            pe.wait_ge(s_al, KH + 1 + SEED)

            with pe.Fori(0, 8) as i:
                for k in range(2):
                    pe.wait_ge(s_g, 2 * i + SEED)
                    product(U_G + 8 * i, 4 * k, 4, hnh, hnl, LIVE, NL, (2 * k, 2 * k + 1))
            pe.wait_ge(s_g, 16 + SEED)
            pe.wait_ge(s_ygl, 1)
            for k in range(4):
                product(U_GLU, 2 * k, 2, ygh, ygl, 0, NL, (2 * k, 2 * k + 1))
            pe.wait_ge(s_zl, KH)
            with pe.Fori(0, 4) as i:
                for k in range(2):
                    pe.wait_ge(s_mx, 4 * i + SEED)
                    product(U_PROJ + 8 * i, 4 * k, 2, anh, anl, 0, NL, (4 * k, 4 * k + 1))
                    product(U_PROJ + 8 * i, 4 * k + 2, 2, zh, zl, 0, NL, (4 * k + 2, 4 * k + 3))
            pe.wait_ge(s_ml, KT)
            with pe.Fori(0, 4) as i:
                for k in range(2):
                    pe.wait_ge(s_h1, 2 * i + SEED)
                    product(U_OUT + 8 * i, 4 * k, 4, hnh, hnl, 0, NL, (2 * k, 2 * k + 1))
            norm_sums(1, NL)
            pe.wait_ge(s_nl, 2 * KT + SEED)
            with pe.Fori(0, FT // 4) as i:
                for k in range(2):
                    pe.wait_ge(s_fm, 4 * i + SEED)
                    product(U_UP + 16 * i, 8 * k, 4, hnh, hnl, 0, NL, (4 * k, 4 * k + 1))
                    product(U_UP + 16 * i, 8 * k + 4, 4, hnh, hnl, 2, SEQ, (4 * k + 2, 4 * k + 3))

            def down(base_u, kt, k, first, final):
                pe.wait_ge(s_lo, base_u + (k + 1))
                xh = ah[:, kt, :] if isinstance(kt, int) else ah[:, ds(kt, 1), :].rearrange("p k n -> p (k n)")
                xl = al[:, kt, :] if isinstance(kt, int) else al[:, ds(kt, 1), :].rearrange("p k n -> p (k n)")
                for m in range(8):
                    g = 8 * (k % 2) + m
                    o = ps[:, g // 2, (g % 2) * SEQ:(g % 2 + 1) * SEQ]
                    cols = slice(m * P, (m + 1) * P)
                    mm(o, slot(whi, k)[:, cols], xh, start=first and g % 2 == 0, stop=False, skip_group_check=True)
                    mm(o, slot(whi, k)[:, cols], xl, start=False, stop=False, skip_group_check=True)
                    ins = mm(o, slot(wlo, k)[:, cols], xh, start=False, stop=final, skip_group_check=True)
                ins.then_inc(s_used, 1)

            pe.wait_ge(s_fl, FT + SEED)
            for k in range(4):
                down(U_DOWN, k // 2, k, k < 2, False)
            with pe.Fori(1, FT // 2 - 1) as i:
                for k in range(4):
                    down(U_DOWN + 4 * i, 2 * i + k // 2, k, False, False)
            for k in range(4):
                down(U_END - 4, FT - 2 + k // 2, k, False, k >= 2)

            norm_sums(2, SEQ)
            for n in range(KT // DEPTH):
                if n >= 2:
                    pe.wait_ge(s_oc, n - 1)
                for k in range(DEPTH):
                    pe.wait_ge(s_nt, 2 * KT + DEPTH * n + k + 1)
                    for t in range(2):
                        ins = nc.tensor.transpose(ps[:, 2 * (n % 2) + t, k * P:(k + 1) * P],
                                                  tr[:, k, t * P:(t + 1) * P], ident[:, :])
                ins.then_inc(s_ot, 1)


_INS = ["x", "meta_tokens", "norm1_g", "w_in", "na_rpb", "ssm_lam_re", "ssm_lam_im", "ssm_log_step", "ssm_b_re",
        "ssm_b_im", "ssm_c_re", "ssm_c_im", "ssm_d", "w_glu", "w_proj_na", "w_proj_ssm", "w_out", "norm2_g",
        "w_up", "conv_w", "conv_b", "w_down", "final_g"]


def kernel(**inputs):
    import numpy as _np
    import concourse.bacc as _bacc
    from concourse import mybir as _mybir
    from concourse.bass_utils import run_bass_kernel_spmd as _run

    nc = _bacc.Bacc("TRN2", target_bir_lowering=False, num_devices=1)
    arrays, args = {}, []
    for name in _INS:
        a = _np.ascontiguousarray(inputs[name])
        arrays[f"in_{name}"] = a
        args.append(nc.dram_tensor(f"in_{name}", a.shape, _mybir.dt.from_np(a.dtype), kind="ExternalInput").ap())
    args.append(nc.dram_tensor("out_h", (1, SEQ, D_MODEL), _mybir.dt.float32, kind="ExternalOutput").ap())
    encoder_block(nc, *args)
    r = _run(nc, [arrays], core_ids=[0])
    return r.results[0]["out_h"]
```

```python
import math
from contextlib import ExitStack

import numpy as np
import concourse.bass as bass
from concourse import mybir

D_MODEL = 2048
SEQ = 256
N_META = 16
GRID_W = 64
ROW_WIN = 8
COL_WIN = 16
DH = 64
HEADS = (D_MODEL // 2) // DH
HALF = D_MODEL // 2
GROUP = 16
GROUPS = HALF // GROUP
STATE = 64
D_FF = ((8 * D_MODEL // 3 + 255) // 256) * 256
EPS = 1e-6
SEED = 4
DIRS = 2

P = 128
L = N_META + SEQ
LIVE = N_META - 2
NL = L - LIVE
KT = D_MODEL // P
KH = HALF // P
FT = D_FF // P
DEPTH = 4
UNIT = 1024
CB = 256
UKT = UNIT // CB
G_SCAN = 2
G_SSM = 2
CHUNK = 4
NCH = L // CHUNK
PAIRS = GROUPS // 2
GSLOTS = 4
PB = P // (2 * GROUP)
GRID_ROWS = SEQ // GRID_W
SCALE = DH ** -0.5
MASKED = -1e30
PADW = 2 * GRID_W - 1
RPB_ROWS = 2 * ROW_WIN - 1
RPB_COLS = 2 * COL_WIN - 1
QROWS = P // GRID_W
DROWS = 2 * GRID_ROWS - 1
EWIN = GRID_ROWS + QROWS * (SEQ // P - 1)
TWO_PI_HI = 6.28125
TWO_PI_MID = 0.0019350051879882812
TWO_PI_LO = 2 * math.pi - TWO_PI_HI - TWO_PI_MID
ROUND = 1.5 * 2 ** 23
PI_BELOW = 3.1415925


def encoder_block(nc, x, meta, norm1_g, w_in, rpb, lam_re, lam_im, log_step, b_re, b_im, c_re, c_im,
                  ssm_d, w_glu, w_proj_na, w_proj_ssm, w_out, norm2_g, w_up, conv_w, conv_b, w_down,
                  final_g, out):
    F = mybir.dt.float32
    R = mybir.dt.float32r
    ACT = mybir.ActivationFunctionType
    ALU = mybir.AluOpType
    AX = mybir.AxisListType
    ds = bass.ds

    q_d = nc.dram_tensor("q_scratch", [KH, P, NL], F, kind="Internal").ap()
    k_d = nc.dram_tensor("k_scratch", [KH, P, L], F, kind="Internal").ap()
    v_d = nc.dram_tensor("v_scratch", [L, HALF], F, kind="Internal").ap()
    xT_d = nc.dram_tensor("xT_scratch", [P, KT * L], F, kind="Internal").ap()
    pad_d = nc.dram_tensor("rpb_scratch", [HEADS * DROWS, PADW], F, kind="Internal").ap()
    skew_d = nc.dram_tensor("skew_scratch", [GRID_W, HEADS * DROWS, GRID_W], F, kind="Internal").ap()

    ctx = ExitStack()
    with ctx:
        def sem(name):
            return ctx.enter_context(nc.semaphore(name))

        base = (nc.sbuf_base + 31) // 32 * 32
        cursor = [base]

        def keep(name, shape, dt=F):
            t = nc.alloc_sbuf_tensor_at(name, shape, dt, offset=cursor[0])
            cursor[0] += (int(np.prod(shape[1:])) * 4 + 31) // 32 * 32
            return t

        raw = keep("w_raw", [P, DEPTH, UNIT])
        whi = keep("w_hi", [P, DEPTH, UNIT], R)
        wlo = keep("w_lo", [P, DEPTH, UNIT], R)
        hnh = keep("act_hi", [P, KT, L], R)
        hnl = keep("act_lo", [P, KT, L], R)
        o_tr = cursor[0]
        tr = keep("norm_ring", [P, DEPTH, L])
        vm = nc.alloc_sbuf_tensor_at("v_meta", [N_META, KH, P], F, offset=o_tr)
        o_sq = cursor[0]
        sq = keep("square_ring", [P, 2, L])
        rstd = keep("rstd", [P, L])
        ident = keep("ident", [P, P])
        ones = keep("ones", [P, P])
        gains = keep("gains", [P, 3 * KT])
        cvw = keep("conv_params", [P, 4 * FT])
        mask = keep("col_mask", [P, GRID_W])
        stat = keep("att_stats", [P, 4, 2, 2])
        arena = (cursor[0] + 31) // 32 * 32

        def at(name, off, shape, dt=F):
            assert off % 32 == 0 and arena + off + int(np.prod(shape[1:])) * 4 <= nc.sbuf_usable_end, (name, off)
            return nc.alloc_sbuf_tensor_at(name, shape, dt, offset=arena + off)

        xtok = at("x_tokens", 0, [P, 3, D_MODEL])
        X = at("scan_states", 0, [P, NCH + 1, 2 * DIRS, PAIRS])
        gate_ssm = at("gate_ssm", 0, [P, KT, NL])
        ygh = at("gelu_hi", 16512, [P, KH, NL], R)
        ygl = at("gelu_lo", 16512 + 8256, [P, KH, NL], R)
        o_y = 35328
        yT = at("y_ssm", o_y, [P, KH, L])
        x0T = at("x_feature_major", o_y, [P, KT, L])
        braw = at("b_raw", 24576, [P, 2, DIRS * PAIRS, GROUP])
        o_u = o_y + KH * L * 4
        U = at("u_chunks", o_u, [P, PAIRS, NCH])
        stg = at("qkv_stage", o_u + 8704, [P, 2, 2, L])
        vst = at("v_stage", o_u + 8704 + 4352, [P, 3, CB])
        Gn = at("g_nat", o_u + 8704, [P, GSLOTS, DIRS, 2, 160])
        anh = at("attn_hi", o_u, [P, KH, NL], R)
        anl = at("attn_lo", o_u + 8256, [P, KH, NL], R)
        o_p = o_u + 8704 + 10240
        BB = at("b_bar", o_p, [P, DIRS * PAIRS, 3, GROUP])
        CC = at("c_slots", o_p + 12288, [P, DIRS * PAIRS, 3, GROUP])
        pwG = at("pow_out", o_p + 24576, [P, DIRS * PAIRS, 2, CHUNK + 1, 2])
        A4R = at("chunk_re", o_p + 29696, [P, DIRS, 2, PAIRS])
        A4I = at("chunk_im", o_p + 30208, [P, DIRS, 2, PAIRS])
        drep = at("d_skip", o_p + 30720, [P, PAIRS])
        o_r = o_p + 30848
        cnat = at("c_rows", o_r, [P, DIRS, KH, 2, STATE])
        prm = at("params", o_r + 8192, [P, 24, DIRS * PAIRS])
        pw = at("powers", o_r + 8192 + 6144, [P, CHUNK + 1, 2, DIRS * PAIRS])
        rows = at("param_rows", o_r + 8192 + 6144 + 2560, [DIRS * PAIRS, 3, P])
        lst = at("step_rows", o_r + 18432, [DIRS * PAIRS, 8])
        drow = at("d_rows", o_r + 18464, [PAIRS, CHUNK, 2 * GROUP])
        btmp = at("b_tmp", 0, [P, 2, UNIT])
        grow = at("gain_rows", o_r + 18976, [3 * KT, P])
        crow = at("conv_rows", o_r + 19488, [2 * FT, 2, P])
        padt = at("rpb_pad", o_u + 13056, [HEADS * DROWS, P])
        t1p = at("t1_p", o_r, [P, 2, 160])
        t2p = at("t2_p", o_r + 1280, [P, 2, 160])
        Tm = at("toeplitz", o_r + 2560, [P, 2, P])
        Bm = at("b_masked", o_r + 3584, [P, GSLOTS, DIRS, 2, 2 * GROUP])
        sc1 = at("scan_t1", o_r + 5632, [P, P])
        sc2 = at("scan_t2", o_r + 6144, [P, P])
        o_g = o_r + 6656
        Wn = at("w_nat", o_g, [P, 2, DIRS, 2, P])
        WT = at("w_tr", o_g + 4096, [P, 2, 2 * DIRS, P])
        pwW = at("pow_in", o_r + 21088, [P, DIRS * PAIRS, 2, CHUNK, 2])
        gate_na = at("gate_na", o_g, [P, KT, NL])
        t1v = nc.alloc_sbuf_tensor_at("t1_v", [P, 2, 160], F, offset=o_sq)
        t2v = nc.alloc_sbuf_tensor_at("t2_v", [P, 2, 160], F, offset=o_sq + 1280)
        qm = nc.alloc_sbuf_tensor_at("q_meta", [P, KH, 2], F, offset=o_sq + 2560)
        km = nc.alloc_sbuf_tensor_at("k_meta", [P, KH, N_META], F, offset=o_sq + 2624)
        o_a = o_p
        qs = at("q_ring", o_a, [P, 2, NL])
        ks = at("k_ring", o_a + 2080, [P, 2, L])
        vs = at("v_ring", o_a + 4256, [P, 2, 3, P])
        bi = at("bias_ring", o_a + 7328, [P, 4, EWIN, GRID_W])
        S = at("scores", o_a + 13472, [P, 2, 2, L])
        PT = at("probs_t", o_a + 17824, [P, 2, 2 * SEQ])
        PT2 = at("probs_t2", o_a + 21920, [N_META, 2, SEQ])
        sm = at("meta_scores", o_a + 23968, [2, 2, KH, N_META])
        smx = at("meta_stats", o_a + 24992, [2, 4, HEADS])
        ptm = at("meta_probs_t", o_a + 25248, [N_META, 2 * HEADS])
        zh = at("z_hi", o_a, [P, KH, NL], R)
        zl = at("z_lo", o_a + 8256, [P, KH, NL], R)
        gt = at("glu_ring", o_a + 16512, [P, 4, NL])
        mt = at("mix_ring", o_a + 16512 + 4128, [P, 4, NL])
        ah = at("hidden_hi", 0, [P, FT, SEQ], R)
        al = at("hidden_lo", 45056, [P, FT, SEQ], R)
        cv = at("conv_ring", 90112, [P, 2, 2, SEQ])
        ge = at("gelu_ring", 94208, [P, 2, 2, SEQ])
        o_x = 98304
        xT = at("xT", o_x, [P, KT, L])
        otok = at("out_tokens", 0, [P, SEQ // P, D_MODEL])

        ps = ctx.enter_context(nc.psum_tensor("ps", [P, 8, 512], F))

        s_x = sem("x_loaded")
        s_par = sem("params_loaded")
        s_raw = [sem(f"unit_loaded_{i}") for i in range(DEPTH)]
        s_hi = sem("unit_hi_made")
        s_lo = sem("unit_split")
        s_used = sem("unit_consumed")
        s_const = sem("constants_made")
        s_xtp = sem("x_transposed")
        s_xt = sem("xT_copied")
        s_sq = sem("squares_made")
        s_ss = sem("squares_summed")
        s_sq_used = sem("square_tile_summed")
        s_var = sem("variance_made")
        s_sd = sem("deviation_made")
        s_nt = sem("norm_tile_made")
        s_nh = sem("norm_hi_made")
        s_nl = sem("norm_lo_made")
        s_spill = sem("xT_spilled")
        s_xre = sem("xT_reloaded")
        s_rows = sem("rows_ready")
        s_ptp = sem("params_transposed")
        s_pcp = sem("params_copied")
        s_pd = sem("param_step_dve")
        s_pa = sem("param_step_act")
        s_ctp = sem("c_transposed")
        s_ccp = sem("c_copied")
        s_u = sem("u_chunks_ready")
        s_kev = sem("qkv_block_copied")
        s_kst = sem("qk_stored")
        s_vtd = sem("v_block_copied")
        s_vtp = sem("v_transposed")
        s_vcp = sem("v_copied")
        s_vst = sem("v_stored")
        s_wd = sem("w_fwd_made")
        s_wp = sem("w_bwd_made")
        s_wtp = sem("w_transposed")
        s_wts = sem("w_copied")
        s_sps = sem("chunk_inputs_summed")
        s_ssb = sem("chunk_inputs_copied")
        s_scan = sem("scan_done")
        s_gd = sem("g_fwd_made")
        s_gp = sem("g_bwd_made")
        s_kps = sem("kernel_summed")
        s_tm = sem("toeplitz_copied")
        s_yps = sem("y_summed")
        s_ysb = sem("y_copied")
        s_yg = sem("gelu_made")
        s_ygh = sem("gelu_hi_made")
        s_ygl = sem("gelu_lo_made")
        s_pad1 = sem("pad_zeroed")
        s_pad2 = sem("pad_filled")
        s_pad3 = sem("pad_skewed")
        s_qkv = [sem(f"qkv_loaded_{i}") for i in range(2)]
        s_bl = [sem(f"bias_loaded_{i}") for i in range(4)]
        s_bm = sem("bias_masked")
        s_qk = sem("scores_summed")
        s_nm = sem("row_max_ready")
        s_e = sem("exp_made")
        s_p = sem("probs_ready")
        s_ptps = sem("probs_transposed")
        s_ptsb = sem("probs_copied")
        s_pv = sem("pv_summed")
        s_ah = sem("attn_hi_made")
        s_al = sem("attn_lo_made")
        s_m1 = sem("meta_scores_summed")
        s_m2 = sem("meta_shifted")
        s_m3 = sem("meta_exp_made")
        s_m4 = sem("meta_probs_ready")
        s_m5 = sem("meta_probs_transposed")
        s_m6 = sem("meta_probs_copied")
        s_m7 = sem("meta_pv_summed")
        s_m8 = sem("meta_hi_made")
        s_g = sem("gates_made")
        s_sg = sem("glu_gate_made")
        s_z = sem("z_made")
        s_zh = sem("z_hi_made")
        s_zl = sem("z_lo_made")
        s_mx = sem("mix_made")
        s_mh = sem("mix_hi_made")
        s_ml = sem("mix_lo_made")
        s_h1 = sem("h1_block_added")
        s_c = sem("conv_started")
        s_cd = sem("conv_made")
        s_ge = sem("hidden_gelu_made")
        s_fm = sem("hidden_made")
        s_fh = sem("hidden_hi_made")
        s_fl = sem("hidden_lo_made")
        s_dn = sem("down_done")
        s_h2 = sem("h2_made")
        s_ot = sem("out_transposed")
        s_oc = sem("out_copied")
        s_out = sem("out_stored")

        block = ctx.enter_context(nc.Block())

        U_U, U_V, U_K, U_Q, U_G = 0, 16, 32, 48, 64
        U_GLU = U_G + 64
        U_PROJ = U_GLU + 8
        U_OUT = U_PROJ + 32
        U_UP = U_OUT + 32
        U_DOWN = U_UP + 4 * FT
        U_END = U_DOWN + 2 * FT
        ITERS_IN = 2

        def kblock(w, col, kq):
            return w[kq * UKT * P:(kq + 1) * UKT * P, ds(col, CB)].rearrange("(t p) c -> p t c", p=P)

        def slot(ring, k):
            return ring[:, k % DEPTH, :]

        @block.sync
        def _(sp):
            sp.dma_start(xtok[0:N_META, 0, :], meta).then_inc(s_x, 16)
            sp.dma_start(xtok[N_META:P, 0, :], x[0, 0:P - N_META, :]).then_inc(s_x, 16)
            sp.dma_start(xtok[:, 1, :], x[0, P - N_META:2 * P - N_META, :]).then_inc(s_x, 16)
            sp.dma_start(xtok[0:N_META, 2, :], x[0, 2 * P - N_META:SEQ, :]).then_inc(s_x, 16)

            def load(base_u, k, src):
                if isinstance(base_u, int) and base_u + k < DEPTH:
                    pass
                else:
                    sp.wait_ge(s_lo, base_u + (k - DEPTH + 1))
                dst = slot(raw, k)
                if len(src.shape) == 3:
                    dst = dst.rearrange("p (t c) -> p t c", t=src.shape[1])
                sp.dma_start(dst, src).then_inc(s_raw[k % DEPTH], 16)

            def load_in(first, col0, i, units=range(8)):
                for k in units:
                    load(first + 8 * i, k, kblock(w_in[0], i * (2 * CB) + (col0 + (k // 4) * CB), k % 4))

            load_in(U_U, 3 * HALF, 0)
            sp.wait_ge(s_xt, KT)
            sp.dma_start(xT_d, x0T[:, :, :].rearrange("p k t -> p (k t)")).then_inc(s_spill, 16)
            with sp.Fori(1, ITERS_IN) as i:
                load_in(U_U, 3 * HALF, i)
            sp.wait_ge(s_pad2, 16)
            with sp.Fori(0, GRID_W) as c:
                sp.dma_start(skew_d[ds(c, 1), :, :].rearrange("a r w -> (a r) w"),
                             pad_d[:, ds((GRID_W - 1) - c, GRID_W)]).then_inc(s_pad3, 16)
            for first, col0 in ((U_V, 2 * HALF), (U_K, HALF), (U_Q, 0)):
                with sp.Fori(0, ITERS_IN) as i:
                    load_in(first, col0, i)

            with sp.Fori(0, 8) as i:
                load_in(U_G, 4 * HALF, i)
            for k in range(8):
                load(U_GLU, k, kblock(w_glu[0], (k // 2) * CB, k % 2))
            with sp.Fori(0, 4) as i:
                for k in range(8):
                    w = (w_proj_na, w_proj_ssm)[k % 4 // 2]
                    load(U_PROJ + 8 * i, k, kblock(w[0], i * (2 * CB) + (k // 4) * CB, k % 2))
            with sp.Fori(0, 4) as i:
                for k in range(8):
                    load(U_OUT + 8 * i, k, kblock(w_out[0], i * (2 * CB) + (k // 4) * CB, k % 4))
            with sp.Fori(0, FT // 4) as i:
                for k in range(16):
                    col = i * (2 * CB) + ((k // 8) * CB + (k % 8 // 4) * D_FF)
                    load(U_UP + 16 * i, k, kblock(w_up[0], col, k % 4))
            with sp.Fori(0, FT // 2) as i:
                for k in range(4):
                    src = w_down[0][ds(i * (2 * P) + (k // 2) * P, P), (k % 2) * UNIT:(k % 2 + 1) * UNIT]
                    load(U_DOWN + 4 * i, k, src)
            for n in range(KT // DEPTH):
                sp.wait_ge(s_oc, n + 1)
                cs = slice(512 * n, 512 * (n + 1))
                sp.dma_start(out[0, :, cs].rearrange("(t p) c -> p t c", p=P), otok[:, :, cs]).then_inc(s_out, 16)
            sp.wait_ge(s_out, 16 * (KT // DEPTH))

        def hi_unit(act, base_u, k):
            act.wait_ge(s_raw[k % DEPTH], base_u * 4 + 16 * (k // DEPTH + 1))
            if not (isinstance(base_u, int) and base_u + k < DEPTH):
                act.wait_ge(s_used, base_u + (k - DEPTH + 1))
            act.activation(slot(whi, k), slot(raw, k), ACT.Copy).then_inc(s_hi, 1)

        def lo_unit(pool, base_u, k):
            pool.wait_ge(s_hi, base_u + (k + 1))
            pool.tensor_tensor(slot(wlo, k), slot(raw, k), slot(whi, k).bitcast(F), ALU.subtract).then_inc(s_lo, 1)

        def split_loop(eng, unit, first, iters, per):
            with eng.Fori(0, iters) as i:
                for k in range(per):
                    unit(eng, (first + DEPTH) + per * i, k)

        def norm_lo(pool, which, n):
            with pool.Fori(0, KT // DEPTH) as i:
                for k in range(DEPTH):
                    pool.wait_ge(s_nh, DEPTH * i + (KT * which + k + 1))
                    pool.tensor_tensor(hnl[:, ds(DEPTH * i + k, 1), 0:n].rearrange("p k n -> p (k n)"), tr[:, k, 0:n],
                                       hnh[:, ds(DEPTH * i + k, 1), 0:n].rearrange("p k n -> p (k n)").bitcast(F),
                                       ALU.subtract).then_inc(s_nl, 1)

        def w_make(eng, pair, sl, d, t1, t2):
            n = 2 * CHUNK
            dq = pair + d * PAIRS
            pr = pwW[:, ds(dq, 1), 0:1, :, :].rearrange("p q r k g -> p (q r) (k g)").unsqueeze(3)
            pi = pwW[:, ds(dq, 1), 1:2, :, :].rearrange("p q r k g -> p (q r) (k g)").unsqueeze(3)
            ri = BB[:, ds(dq, 1), 1:3, :].rearrange("p q r c -> p (q r) c").unsqueeze(2)
            nr = BB[:, ds(dq, 1), 0:2, :].rearrange("p q r c -> p (q r) c").unsqueeze(2)
            full = [P, 2, n, GROUP]
            a = t1[:, :, 0:n * GROUP].rearrange("p r (n c) -> p r n c", c=GROUP)
            b = t2[:, :, 0:n * GROUP].rearrange("p r (n c) -> p r n c", c=GROUP)
            eng.tensor_tensor(a, pr.to_broadcast(full), ri.to_broadcast(full), ALU.mult)
            eng.tensor_tensor(b, pi.to_broadcast(full), nr.to_broadcast(full), ALU.mult)
            eng.drain()
            ins = eng.tensor_tensor(Wn[:, sl, d, :, :], t1[:, :, 0:n * GROUP], t2[:, :, 0:n * GROUP], ALU.add)
            return ins

        def g_make(eng, pair, sl, d, t1, t2):
            n = 2 * (CHUNK + 1)
            dq = pair + d * PAIRS
            pr = pwG[:, ds(dq, 1), 0:1, :, :].rearrange("p q r k g -> p (q r) (k g)").unsqueeze(3)
            pi = pwG[:, ds(dq, 1), 1:2, :, :].rearrange("p q r k g -> p (q r) (k g)").unsqueeze(3)
            c0 = CC[:, ds(dq, 1), 0:2, :].rearrange("p q r c -> p (q r) c").unsqueeze(2)
            c1 = CC[:, ds(dq, 1), 1:3, :].rearrange("p q r c -> p (q r) c").unsqueeze(2)
            full = [P, 2, n, GROUP]
            a = t1[:, :, :].rearrange("p r (n c) -> p r n c", c=GROUP)
            b = t2[:, :, :].rearrange("p r (n c) -> p r n c", c=GROUP)
            eng.tensor_tensor(a, pr.to_broadcast(full), c0.to_broadcast(full), ALU.mult)
            eng.tensor_tensor(b, pi.to_broadcast(full), c1.to_broadcast(full), ALU.mult)
            eng.drain()
            return eng.tensor_tensor(Gn[:, sl, d, :, :], t1[:, :, :], t2[:, :, :], ALU.add)

        @block.gpsimd
        def _(pool):
            pool.sem_inc(s_nl, SEED)
            pool.memset(ones[:, :], 1.0).then_inc(s_const, 1)
            pool.memset(ident[:, :], 0.0)
            pool.memset(mask[:, :], 0.0)
            pool.memset(padt[:, :], 0.0)
            pool.drain()
            pool.affine_select(out=ident[:, :], in_=ident[:, :], compare_op=ALU.not_equal, fill=1.0,
                               base=0, pattern=[[-1, P]], channel_multiplier=1).then_inc(s_const, 1)
            pool.drain()
            far = GRID_W - COL_WIN
            for r in range(QROWS):
                m = mask[r * GRID_W:(r + 1) * GRID_W, 0:far]
                pool.affine_select(out=m, in_=m, compare_op=ALU.is_ge, fill=MASKED, base=COL_WIN // 2,
                                   pattern=[[1, far]], channel_multiplier=-1)
                pool.drain()
            pool.drain()
            for r in range(QROWS):
                m = mask[r * GRID_W:(r + 1) * GRID_W, COL_WIN:GRID_W]
                pool.affine_select(out=m, in_=m, compare_op=ALU.is_ge, fill=MASKED,
                                   base=COL_WIN // 2 - 1 - COL_WIN, pattern=[[-1, far]], channel_multiplier=1)
                pool.drain()
            pool.drain()
            for k in range(DEPTH):
                lo_unit(pool, 0, k)
            pool.dma_start(pad_d, padt[:, 0:PADW]).then_inc(s_pad1, 16)
            pool.wait_ge(s_pad1, 16)
            pool.dma_start(pad_d[:, GRID_W - COL_WIN:GRID_W - COL_WIN + RPB_COLS].rearrange("(h d) c -> h d c", h=HEADS),
                           rpb[0, :, ROW_WIN - GRID_ROWS:ROW_WIN - GRID_ROWS + DROWS, :]).then_inc(s_pad2, 16)
            norm_lo(pool, 0, L)

            split_loop(pool, lo_unit, U_U, ITERS_IN, 8)
            split_loop(pool, lo_unit, U_V, ITERS_IN, 8)

            def w_bwd(p, k):
                pool.wait_ge(s_wtp, p + (k - 1 + SEED))
                w_make(pool, p + k, k % 2, 1, t1p, t2p).then_inc(s_wp, 1)
                pool.drain()

            pool.wait_ge(s_pd, 1)
            pool.wait_ge(s_ccp, 4)
            pool.memset(Bm[:, :, :, :, :], 0.0)
            w_bwd(0, 0)
            w_bwd(0, 1)
            with pool.Fori(0, ITERS_IN - 1) as i:
                for k in range(8):
                    w_bwd(16 * i, 2 * k + 2)
                    w_bwd(16 * i, 2 * k + 3)
                    lo_unit(pool, (U_K + DEPTH) + 8 * i, k)
            for k in range(8):
                if k < 7:
                    w_bwd(PAIRS - 16, 2 * k + 2)
                    w_bwd(PAIRS - 16, 2 * k + 3)
                lo_unit(pool, U_Q - 8 + DEPTH, k)
            split_loop(pool, lo_unit, U_Q, ITERS_IN, 8)
            split_loop(pool, lo_unit, U_G, G_SCAN, 8)

            def g_bwd(p, k):
                pool.wait_ge(s_yps, p + (k - GSLOTS + 1 + SEED))
                for h in range(2):
                    hs = slice(64 * h, 64 * h + 64)
                    src = BB[hs, :, 1:3, :].rearrange("p (d q) r c -> p d q r c", d=DIRS)[:, :, ds(p + k, 1), :, :]
                    pool.tensor_copy(Bm[hs, k % GSLOTS, :, :, GROUP * h:GROUP * (h + 1)],
                                     src.rearrange("p d q r c -> p d (q r) c"))
                    pool.drain()
                g_make(pool, p + k, k % GSLOTS, 1, t1p, t2p).then_inc(s_gp, 1)
                pool.drain()

            pool.wait_ge(s_kst, 16 * 16)
            pool.wait_ge(s_vst, 16 * 8)
            for k in range(GSLOTS):
                g_bwd(0, k)
            with pool.Fori(0, G_SSM - 1) as i:
                for k in range(8):
                    lo_unit(pool, (U_G + DEPTH + 8 * G_SCAN) + 8 * i, k)
                    g_bwd(16 * i, 2 * k + 4)
                    g_bwd(16 * i, 2 * k + 5)
            for k in range(8):
                lo_unit(pool, U_G + DEPTH + 8 * (G_SCAN + G_SSM - 1), k)
                if k < 6:
                    g_bwd(PAIRS - 16, 2 * k + 4)
                    g_bwd(PAIRS - 16, 2 * k + 5)

            with pool.Fori(0, HEADS // 4) as i:
                for k in range(4):
                    if k % 2 == 0:
                        for hh in range(2):
                            pool.wait_ge(s_bl[k + hh], 32 * i + 32)
                            pool.tensor_tensor(bi[:, k + hh, :, :], bi[:, k + hh, :, :],
                                               mask[:, :].unsqueeze(1).to_broadcast([P, EWIN, GRID_W]), ALU.add)\
                                .then_inc(s_bm, 1)
                    lo_unit(pool, (U_G + DEPTH + 8 * (G_SCAN + G_SSM)) + 8 * i, 2 * k)
                    lo_unit(pool, (U_G + DEPTH + 8 * (G_SCAN + G_SSM)) + 8 * i, 2 * k + 1)
            for k in range(8):
                lo_unit(pool, U_GLU + DEPTH, k)
            split_loop(pool, lo_unit, U_PROJ, 4, 8)
            split_loop(pool, lo_unit, U_OUT, 4, 8)
            norm_lo(pool, 1, NL)
            split_loop(pool, lo_unit, U_UP, FT // 4, 16)
            split_loop(pool, lo_unit, U_DOWN, FT // 2 - 1, 4)

        @block.scalar
        def _(act):
            for seeded in (s_ptsb, s_g, s_ge, s_u, s_kev, s_vtd, s_vcp, s_wts, s_tm):
                act.sem_inc(seeded, SEED)
            act.dma_start(rows[:, 0, :], lam_re[0].rearrange("d (q g) n -> (d q) (g n)", g=2)).then_inc(s_par, 16)
            act.dma_start(rows[:, 1, :], lam_im[0].rearrange("d (q g) n -> (d q) (g n)", g=2)).then_inc(s_par, 16)
            act.dma_start(lst[:, 0:2], log_step[0].rearrange("d (q g) -> (d q) g", g=2)).then_inc(s_par, 16)
            act.dma_start(drow[:, 0, :], ssm_d[0].rearrange("(q c) -> q c", q=PAIRS)).then_inc(s_par, 16)
            for n, g in enumerate((norm1_g[0], norm2_g[0], final_g)):
                act.dma_start(grow[n * KT:(n + 1) * KT, :], g.rearrange("(k p) -> k p", p=P)).then_inc(s_par, 16)
            for n in range(3):
                act.dma_start(crow[n % 2 * FT:(n % 2 + 1) * FT, n // 2, :],
                              conv_w[0, n].rearrange("(k p) -> k p", p=P)).then_inc(s_par, 16)
            act.dma_start(crow[FT:2 * FT, 1, :], conv_b[0].rearrange("(k p) -> k p", p=P)).then_inc(s_par, 16)
            for r, b in enumerate((b_re, b_im)):
                for d in range(DIRS):
                    act.dma_start(braw[:, r, d * PAIRS:(d + 1) * PAIRS, :],
                                  b[0, d].rearrange("(q g) n c -> (g n) q c", g=2)).then_inc(s_par, 16)
            for r, c in enumerate((c_re, c_im)):
                for d in range(DIRS):
                    act.dma_start(cnat[:, d, :, r, :],
                                  c[0, d].rearrange("(k g) c n -> (g c) k n", k=KH)).then_inc(s_par, 16)
            for k in range(DEPTH):
                hi_unit(act, 0, k)

            def norm_squares(which, lo, n):
                src = xT if which else x0T
                with act.Fori(0, KT // 2) as i:
                    for k in range(2):
                        if which == 0:
                            act.wait_ge(s_xt, 2 * i + (k + 1))
                        act.wait_ge(s_sq_used, 2 * i + (KT * which + k - 1 + SEED))
                        act.activation(sq[:, k, 0:n], src[:, ds(2 * i + k, 1), lo:lo + n].rearrange("p k n -> p (k n)"),
                                       ACT.Square).then_inc(s_sq, 1)
                act.wait_ge(s_var, which + 1)
                act.activation(rstd[:, 0:n], rstd[:, 0:n], ACT.Sqrt).then_inc(s_sd, 1)

            def norm_hi(which, n):
                with act.Fori(0, KT // DEPTH) as i:
                    for k in range(DEPTH):
                        act.wait_ge(s_nt, DEPTH * i + (KT * which + k + 1))
                        act.activation(hnh[:, ds(DEPTH * i + k, 1), 0:n].rearrange("p k n -> p (k n)"),
                                       tr[:, k, 0:n], ACT.Copy).then_inc(s_nh, 1)

            norm_squares(0, 0, L)
            norm_hi(0, L)

            v = lambda n: prm[:, n, :]
            act.wait_ge(s_pcp, 1)
            act.activation(v(3), v(2), ACT.Exp).then_inc(s_pa, 1)
            act.wait_ge(s_pcp, 2)
            act.activation(v(6), v(4), ACT.Exp).then_inc(s_pa, 1)
            act.wait_ge(s_pcp, 3)
            act.activation(v(8), v(7), ACT.Sin)
            act.activation(v(9), v(7), ACT.Sin, scale=0.5).then_inc(s_pa, 1)
            for d in range(DIRS):
                for q in range(2):
                    n = 2 * d + q
                    act.wait_ge(s_ctp, n + 1)
                    for h in range(2):
                        hs = slice(64 * h, 64 * h + 64)
                        for sl, part, sign in ((0, 0, 1.0), (1, 1, -1.0), (2, 0, -1.0)):
                            src = ps[64 * part:64 * part + 64, 4 + n % 2, :].rearrange("p (q g c) -> p q g c", g=2, c=GROUP)
                            last = act.activation(CC[hs, d * PAIRS + 16 * q:d * PAIRS + 16 * (q + 1), sl, :],
                                                  src[:, :, h, :], ACT.Copy, scale=sign)
                    last.then_inc(s_ccp, 1)

            act.wait_ge(s_spill, 16)
            with act.Fori(0, ITERS_IN) as i:
                for k in range(2):
                    for n in range(4):
                        hi_unit(act, (U_U + DEPTH) + 8 * i, 4 * k + n)
                    act.wait_ge(s_used, 8 * i + (U_U + 4 * (k + 1)))
                    for m in range(2):
                        for b in range(PB):
                            for j in range(CHUNK):
                                src = ps[32 * b:32 * b + 32, 2 * k + m, 0:L].rearrange("p (c j) -> p j c", j=CHUNK)
                                pair = i * (4 * PB) + ((2 * k + m) * PB + b)
                                last = act.activation(U[32 * j:32 * j + 32, ds(pair, 1), :].rearrange("p a c -> p (a c)"),
                                                      src[:, j, :], ACT.Copy)
                    last.then_inc(s_u, 1)

            def v_blocks(i, start):
                for k in range(2):
                    for n in range(4):
                        hi_unit(act, (U_V + DEPTH) + 8 * i, 4 * k + n)
                    act.wait_ge(s_used, 8 * i + (U_V + 4 * (k + 1)))
                    act.wait_ge(s_vtp, 2 * i + SEED)
                    act.activation(stg[:, k, :, :], ps[:, 2 * k:2 * k + 2, 0:L], ACT.Copy).then_inc(s_vtd, 1)
                for k in range(2):
                    act.wait_ge(s_vtp, 2 * i + (k + 1 + SEED))
                    if k or not start:
                        act.wait_ge(s_vst, 64 * i + 32 * k)
                    act.activation(vst[:, 0:2, :], ps[:, 4 + 2 * k, :].rearrange("p (a b) -> p a b", a=2), ACT.Copy)
                    act.activation(vst[0:N_META, 2, :], ps[0:N_META, 5 + 2 * k, 0:CB], ACT.Copy)
                    act.activation(vm[:, ds(4 * i + 2 * k, 2), :].rearrange("p a b -> p (a b)"),
                                   ps[0:N_META, 4 + 2 * k, 0:CB], ACT.Copy).then_inc(s_vcp, 1)
                    act.wait_ge(s_vcp, 2 * i + (k + 1 + SEED))
                    col = i * (2 * CB) + k * CB
                    act.dma_start(v_d[0:2 * P, ds(col, CB)].rearrange("(k p) c -> p k c", p=P),
                                  vst[:, 0:2, :]).then_inc(s_vst, 16)
                    act.dma_start(v_d[2 * P:L, ds(col, CB)], vst[0:N_META, 2, :]).then_inc(s_vst, 16)

            v_blocks(0, True)
            with act.Fori(1, ITERS_IN) as i:
                v_blocks(i, False)

            def store_block(i, k, n, before, dst, meta, width):
                act.activation(stg[:, k, :, 0:n], ps[:, 2 * k:2 * k + 2, 0:n], ACT.Copy)
                act.activation(meta[:, ds(4 * i + 2 * k, 2), :], ps[:, 2 * k:2 * k + 2, 0:width], ACT.Copy).then_inc(s_kev, 1)
                act.wait_ge(s_kev, 2 * i + (before + k + 1 + SEED))
                for m in range(2):
                    act.dma_start(dst[ds(4 * i + (2 * k + m), 1), :, :].rearrange("b p t -> p (b t)"),
                                  stg[:, k, m, 0:n]).then_inc(s_kst, 16)

            def wt_copy(p, k):
                act.wait_ge(s_wtp, p + (k + 1 + SEED))
                act.wait_ge(s_sps, p + (k - 1 + SEED))
                act.activation(WT[:, k % 2, :, :].rearrange("p a b -> p (a b)"), ps[:, 4 + k % 2, :], ACT.Copy)\
                   .then_inc(s_wts, 1)

            def k_blocks(i, start):
                for k in range(8):
                    wt_copy(16 * i, 2 * k)
                    wt_copy(16 * i, 2 * k + 1)
                    hi_unit(act, (U_K + DEPTH) + 8 * i, k)
                    if k % 4 == 3:
                        act.wait_ge(s_used, 8 * i + (U_K + k + 1))
                        act.wait_ge(s_vtp, 4 + SEED)
                        if not start:
                            act.wait_ge(s_kst, 64 * i)
                        store_block(i, k // 4, L, 0, k_d, km, N_META)

            k_blocks(0, True)
            with act.Fori(1, ITERS_IN) as i:
                k_blocks(i, False)
            with act.Fori(0, ITERS_IN) as i:
                for k in range(2):
                    for n in range(4):
                        hi_unit(act, (U_Q + DEPTH) + 8 * i, 4 * k + n)
                    act.wait_ge(s_used, 8 * i + (U_Q + 4 * (k + 1)))
                    act.wait_ge(s_kst, 64 * i + 128)
                    store_block(i, k, NL, 4, q_d, qm, 2)

            def gate_block(gate, f, base_u, used, banks):
                act.wait_ge(s_used, base_u + used)
                act.activation(gate[:, ds(f, 2), :], ps[:, banks:banks + 2, 0:NL], ACT.Sigmoid).then_inc(s_g, 1)

            with act.Fori(0, G_SCAN) as i:
                for k in range(2):
                    for n in range(4):
                        hi_unit(act, (U_G + DEPTH) + 8 * i, 4 * k + n)
                    if k == 0:
                        act.wait_ge(s_ssb, PAIRS + SEED)
                    gate_block(gate_na, 4 * i + 2 * k, 8 * i, U_G + 4 * (k + 1), 2 * k)

            def tm_copy(p, k):
                act.wait_ge(s_kps, p + (k + 1))
                act.wait_ge(s_yps, p + (k - 1 + SEED))
                for j in range(CHUNK):
                    lo = (CHUNK - 1 - j) * 2 * GROUP
                    last = act.activation(Tm[32 * j:32 * j + 32, k % 2, :], ps[0:32, 4 + k % 2, lo:lo + P], ACT.Copy)
                last.then_inc(s_tm, 1)

            with act.Fori(0, G_SSM) as i:
                for k in range(8):
                    tm_copy(16 * i, 2 * k)
                    tm_copy(16 * i, 2 * k + 1)
                    hi_unit(act, (U_G + DEPTH + 8 * G_SCAN) + 8 * i, k)
                    if k % 4 == 3:
                        gate_block(gate_na, 4 * i + (4 * G_SCAN + k // 2 - 1), 8 * i, U_G + 8 * G_SCAN + k + 1, k // 4 * 2)

            def att_load(b, j):
                act.dma_start(qs[:, j, :], q_d[ds(b, 1), :, :].rearrange("b p t -> p (b t)")).then_inc(s_qkv[j], 16)
                act.dma_start(ks[:, j, :], k_d[ds(b, 1), :, :].rearrange("b p t -> p (b t)")).then_inc(s_qkv[j], 16)
                act.dma_start(vs[:, j, 0:2, :],
                              v_d[0:2 * P, ds(b * P, P)].rearrange("(k p) c -> p k c", p=P)).then_inc(s_qkv[j], 16)
                act.dma_start(vs[0:N_META, j, 2, :], v_d[2 * P:L, ds(b * P, P)]).then_inc(s_qkv[j], 16)
                for hh in range(2):
                    for r in range(QROWS):
                        row = b * (2 * DROWS) + (hh * DROWS + GRID_ROWS - 1 - QROWS - r)
                        act.dma_start(bi[GRID_W * r:GRID_W * (r + 1), 2 * j + hh, :, :], skew_d[:, ds(row, EWIN), :])\
                           .then_inc(s_bl[2 * j + hh], 16)

            def att_exp(i, k):
                act.wait_ge(s_nm, 4 * i + (k + 1 + SEED))
                for t in range(2):
                    last = act.activation(S[:, k % 2, t, :], S[:, k % 2, t, :], ACT.Exp,
                                          bias=stat[:, k, 0, t:t + 1], accum_out=stat[:, k, 1, t:t + 1])
                last.then_inc(s_e, 1)

            def att_pt(i, k):
                act.wait_ge(s_ptps, 4 * i + (k + 1 + SEED))
                act.wait_ge(s_pv, 4 * i + (k - 1 + SEED))
                act.activation(PT[:, k % 2, :], ps[:, 4, :], ACT.Copy)
                two = ps[0:N_META, 2 * (k % 2):2 * (k % 2) + 2, L:L + P]
                act.activation(PT2[:, k % 2, :].rearrange("p (t q) -> p t q", t=2), two, ACT.Copy).then_inc(s_ptsb, 1)

            def att_hi(i, j):
                act.wait_ge(s_pv, 4 * i + (2 * (j + 1) + SEED))
                act.activation(anh[:, ds(2 * i + j, 1), 2:NL].rearrange("p k n -> p (k n)"),
                               ps[:, 5, 0:SEQ], ACT.Copy).then_inc(s_ah, 1)

            G_ATT = G_SCAN + G_SSM
            def att_iteration(i, start, last):
                for k in range(4):
                    att_exp(i, k)
                    hi_unit(act, (U_G + DEPTH + 8 * G_ATT) + 8 * i, 2 * k)
                    if k % 2 == 0 and (k or not start):
                        att_hi(i, k // 2 - 1)
                        if not (last and k):
                            att_load(2 * i + (k // 2 + 1), (k // 2 + 1) % 2)
                    hi_unit(act, (U_G + DEPTH + 8 * G_ATT) + 8 * i, 2 * k + 1)
                    if k % 2 == 1:
                        gate_block(gate_ssm, 4 * i + (k - 1), 8 * i, U_G + 8 * G_ATT + 2 * (k + 1), 6)
                    att_pt(i, k)

            act.wait_ge(s_pad3, 16 * GRID_W)
            act.wait_ge(s_kst, 16 * 16)
            act.wait_ge(s_vst, 16 * 8)
            act.wait_ge(s_ysb, PAIRS + SEED)
            att_load(0, 0)
            att_load(1, 1)
            act.activation(yT[:, :, LIVE:L], yT[:, :, LIVE:L], ACT.Gelu_apprx_tanh).then_inc(s_yg, 1)
            act.drain()
            act.activation(ygh[:, :, :], yT[:, :, LIVE:L], ACT.Copy).then_inc(s_ygh, 1)
            att_iteration(0, True, False)
            with act.Fori(1, HEADS // 4 - 1) as i:
                att_iteration(i, False, False)
            att_iteration(HEADS // 4 - 1, False, True)
            att_hi(HEADS // 4 - 1, 1)
            act.wait_ge(s_m2, 1)
            act.activation(sm[:, :, :, :], sm[:, :, :, :], ACT.Exp).then_inc(s_m3, 1)
            act.wait_ge(s_m5, 1)
            act.activation(ptm[:, :], ps[0:N_META, 2, 0:2 * HEADS], ACT.Copy).then_inc(s_m6, 1)
            act.wait_ge(s_m7, 1)
            act.activation(anh[:, :, 0:2], ps[:, 3, 0:2 * KH].rearrange("p (b t) -> p b t", t=2), ACT.Copy)\
               .then_inc(s_m8, 1)

            for q in range(2):
                for n in range(4):
                    hi_unit(act, U_GLU + DEPTH, 4 * q + n)
                act.wait_ge(s_used, U_GLU + 4 * (q + 1))
                if q:
                    act.wait_ge(s_z, 4)
                for m in range(4):
                    act.activation(gt[:, m, :], ps[:, 4 * q + m, 0:NL], ACT.Sigmoid).then_inc(s_sg, 1)
                for m in range(4):
                    act.wait_ge(s_z, 4 * q + m + 1)
                    act.activation(zh[:, 4 * q + m, :], mt[:, m, :], ACT.Copy).then_inc(s_zh, 1)

            with act.Fori(0, 4) as i:
                for k in range(2):
                    for n in range(4):
                        hi_unit(act, (U_PROJ + DEPTH) + 8 * i, 4 * k + n)
                    for m in range(2):
                        act.wait_ge(s_mx, 4 * i + (2 * k + m + 1) + SEED)
                        act.activation(hnh[:, ds(4 * i + (2 * k + m), 1), 0:NL].rearrange("p k n -> p (k n)"),
                                       mt[:, 2 * k + m, :], ACT.Copy).then_inc(s_mh, 1)
            act.wait_ge(s_mx, KT + SEED)
            act.dma_start(xT[:, :, :].rearrange("p k t -> p (k t)"), xT_d).then_inc(s_xre, 16)
            split_loop(act, hi_unit, U_OUT, 4, 8)
            act.wait_ge(s_h1, KT // 2 + SEED)
            norm_squares(1, LIVE, NL)
            norm_hi(1, NL)

            with act.Fori(0, FT // 4) as i:
                for k in range(2):
                    for n in range(4):
                        hi_unit(act, (U_UP + DEPTH) + 16 * i, 8 * k + n)
                    act.wait_ge(s_used, 16 * i + (U_UP + 8 * k + 4))
                    if k == 0:
                        act.wait_ge(s_ge, 4 * i + SEED)
                    for m in range(2):
                        f = 4 * i + (2 * k + m)
                        act.activation(cv[:, k, m, :], ps[:, 4 * k + m, 2:NL], ACT.Identity,
                                       scale=cvw[:, ds(f + FT, 1)], bias=cvw[:, ds(f + 3 * FT, 1)]).then_inc(s_c, 1)
                    for n in range(4, 8):
                        hi_unit(act, (U_UP + DEPTH) + 16 * i, 8 * k + n)
                    if k == 0:
                        act.wait_ge(s_fl, 4 * i + SEED)
                    for m in range(2):
                        act.wait_ge(s_cd, 4 * i + (2 * k + m + 1))
                        act.activation(ge[:, k, m, :], cv[:, k, m, :], ACT.Gelu_apprx_tanh).then_inc(s_ge, 1)
                    for m in range(2):
                        act.wait_ge(s_fm, 4 * i + (2 * k + m + 1) + SEED)
                        act.activation(ah[:, ds(4 * i + (2 * k + m), 1), :].rearrange("p k n -> p (k n)"),
                                       ge[:, k, m, :], ACT.Copy).then_inc(s_fh, 1)
            split_loop(act, hi_unit, U_DOWN, FT // 2 - 1, 4)
            act.wait_ge(s_h2, 1)
            norm_squares(2, N_META, SEQ)

        @block.vector
        def _(dve):
            for seeded in (s_nm, s_al, s_mx, s_h1, s_fm, s_fl, s_ssb, s_ysb):
                dve.sem_inc(seeded, SEED)
            dve.wait_ge(s_par, 16 * 19)
            dve.tensor_copy(rows[:, 2, :].rearrange("p (g n) -> p g n", g=2),
                            lst[:, 0:2].unsqueeze(2).to_broadcast([DIRS * PAIRS, 2, STATE]))
            for j in range(1, CHUNK):
                last = dve.tensor_copy(drow[:, j, :], drow[:, 0, :])
            last.then_inc(s_rows, 1)
            for k in range(KT):
                dve.wait_ge(s_xtp, k + 1)
                dve.tensor_copy(x0T[:, k, :], ps[:, k % 4, 0:L]).then_inc(s_xt, 1)
            dve.wait_ge(s_ptp, 1)
            dve.tensor_copy(gains[:, :], ps[:, 7, 0:3 * KT])
            dve.tensor_copy(cvw[:, :], ps[:, 7, 48:48 + 4 * FT])
            dve.tensor_copy(drep[:, :], ps[:, 7, 416:448])
            dve.tensor_copy(prm[:, 0:3, :], ps[:, 7, 224:416].rearrange("p (a b) -> p a b", a=3)).then_inc(s_pcp, 1)
            dve.drain()

            def norm(which, lo, n):
                dve.wait_ge(s_ss, which + 1)
                dve.tensor_scalar(rstd[:, 0:n], ps[:, 6, 0:n], 1.0 / D_MODEL, EPS, ALU.mult, ALU.add).then_inc(s_var, 1)
                dve.wait_ge(s_sd, which + 1)
                dve.reciprocal(rstd[:, 0:n], rstd[:, 0:n])
                dve.drain()
                src = xT if which else x0T
                if which < 2:
                    with dve.Fori(0, KT // DEPTH) as i:
                        for k in range(DEPTH):
                            dve.wait_ge(s_nl, DEPTH * i + (KT * which + SEED))
                            dve.scalar_tensor_tensor(
                                out=tr[:, k, 0:n], in0=src[:, ds(DEPTH * i + k, 1), lo:lo + n].rearrange("p k n -> p (k n)"),
                                scalar=gains[:, ds(DEPTH * i + (KT * which + k), 1)], in1=rstd[:, 0:n],
                                op0=ALU.mult, op1=ALU.mult).then_inc(s_nt, 1)

            norm(0, 0, L)

            v = lambda n: prm[:, n, :]

            def mul(o, a, b):
                dve.tensor_tensor(o, a, b, ALU.mult)

            def cmul(o, a, b, t):
                mul(t[0], a[0], b[0])
                mul(t[1], a[1], b[1])
                mul(t[2], a[0], b[1])
                mul(t[3], a[1], b[0])
                dve.drain()
                dve.tensor_tensor(o[0], t[0], t[1], ALU.subtract)
                dve.tensor_tensor(o[1], t[2], t[3], ALU.add)
                dve.drain()

            dve.wait_ge(s_pa, 1)
            mul(v(4), v(0), v(3))
            mul(v(5), v(1), v(3))
            dve.drain()
            dve.tensor_scalar(v(10), v(5), 1.0 / (2 * math.pi), ROUND, ALU.mult, ALU.add).then_inc(s_pcp, 1)
            dve.drain()
            dve.tensor_scalar(v(10), v(10), ROUND, None, ALU.subtract)
            for c in (TWO_PI_HI, TWO_PI_MID, TWO_PI_LO):
                dve.drain()
                dve.scalar_tensor_tensor(out=v(5), in0=v(10), scalar=-c, in1=v(5), op0=ALU.mult, op1=ALU.add)
            dve.drain()
            dve.tensor_scalar(v(7), v(5), PI_BELOW, -PI_BELOW, ALU.min, ALU.max).then_inc(s_pcp, 1)
            dve.wait_ge(s_pa, 3)
            mul(v(10), v(9), v(9))
            dve.drain()
            dve.tensor_scalar(v(10), v(10), -2.0, 1.0, ALU.mult, ALU.add)
            dve.memset(pw[:, 0, 0, :], 1.0)
            dve.memset(pw[:, 0, 1, :], 0.0)
            dve.drain()
            a1 = (pw[:, 1, 0, :], pw[:, 1, 1, :])
            a2 = (pw[:, 2, 0, :], pw[:, 2, 1, :])
            tmp = [v(n) for n in (11, 12, 13, 14)]
            mul(a1[0], v(6), v(10))
            mul(a1[1], v(6), v(8))
            dve.drain()
            cmul(a2, a1, a1, tmp)
            cmul((pw[:, 3, 0, :], pw[:, 3, 1, :]), a2, a1, tmp)
            cmul((pw[:, 4, 0, :], pw[:, 4, 1, :]), a2, a2, tmp)
            dve.tensor_scalar(v(15), a1[0], 1.0, None, ALU.subtract)
            mul(v(16), v(0), v(0))
            mul(v(17), v(1), v(1))
            dve.drain()
            dve.tensor_tensor(v(16), v(16), v(17), ALU.add)
            mul(v(18), v(15), v(0))
            mul(v(19), a1[1], v(1))
            mul(v(20), a1[1], v(0))
            mul(v(21), v(15), v(1))
            dve.drain()
            dve.reciprocal(v(16), v(16))
            dve.tensor_tensor(v(18), v(18), v(19), ALU.add)
            dve.tensor_tensor(v(20), v(20), v(21), ALU.subtract)
            dve.drain()
            mul(v(18), v(18), v(16))
            mul(v(20), v(20), v(16))
            dve.drain()
            full = [P, DIRS * PAIRS, GROUP]
            qr = v(18).unsqueeze(2).to_broadcast(full)
            qi = v(20).unsqueeze(2).to_broadcast(full)
            ta = btmp[:, 0, :].rearrange("p (a b) -> p a b", b=GROUP)
            tb = btmp[:, 1, :].rearrange("p (a b) -> p a b", b=GROUP)
            mul(ta, qr, braw[:, 0, :, :])
            mul(tb, qi, braw[:, 1, :, :])
            dve.drain()
            dve.tensor_tensor(BB[:, :, 1, :], ta, tb, ALU.subtract)
            dve.drain()
            mul(ta, qr, braw[:, 1, :, :])
            mul(tb, qi, braw[:, 0, :, :])
            dve.drain()
            dve.tensor_tensor(BB[:, :, 2, :], ta, tb, ALU.add)
            dve.drain()
            dve.tensor_scalar(BB[:, :, 0, :], BB[:, :, 2, :], -1.0, None, ALU.mult)
            dve.memset(pwW[:, :, :, :, :], 0.0)
            dve.memset(pwG[:, :, :, :, :], 0.0)
            dve.drain()
            for h in range(2):
                hs = slice(64 * h, 64 * h + 64)
                for d in range(DIRS):
                    dq = slice(d * PAIRS, (d + 1) * PAIRS)
                    kin = pw[hs, 0:CHUNK, :, dq] if d else pw[hs, CHUNK - 1::-1, :, dq]
                    kout = pw[hs, CHUNK::-1, :, dq] if d else pw[hs, :, :, dq]
                    for r in range(2):
                        dve.tensor_copy(pwW[hs, dq, r, :, h], kin[:, :, r, :].rearrange("p k q -> p q k"))
                        dve.tensor_copy(pwG[hs, dq, r, :, h], kout[:, :, r, :].rearrange("p k q -> p q k"))
            a4r = pw[:, CHUNK, 0, :].rearrange("p (d q) -> p d q", d=DIRS)
            a4i = pw[:, CHUNK, 1, :].rearrange("p (d q) -> p d q", d=DIRS)
            for r in range(2):
                dve.tensor_copy(A4R[:, :, r, :], a4r)
            dve.tensor_copy(A4I[:, :, 0, :], a4i)
            dve.tensor_scalar(A4I[:, :, 1, :], a4i, -1.0, None, ALU.mult)
            dve.drain()
            dve.nop().then_inc(s_pd, 1)

            dve.memset(X[:, 0, :, :], 0.0)

            def w_fwd(p, k):
                dve.wait_ge(s_wtp, p + (k - 1 + SEED))
                w_make(dve, p + k, k % 2, 0, t1v, t2v).then_inc(s_wd, 1)
                dve.drain()

            def s_copy(p, k):
                dve.wait_ge(s_sps, p + (k + 1 + SEED))
                dst = X[:, 1:NCH + 1, :, ds(p + k, 1)].rearrange("p c r q -> p (r q) c")
                src = ps[:, 6 + k % 2, 0:4 * NCH].rearrange("p (r c) -> p r c", c=NCH)
                dve.tensor_copy(dst[:, 0:2, :], src[:, 0:2, :])
                dve.tensor_copy(dst[:, 2:4, :], src[:, 2:4, ::-1]).then_inc(s_ssb, 1)

            dve.wait_ge(s_ccp, 4)
            w_fwd(0, 0)
            w_fwd(0, 1)
            with dve.Fori(0, PAIRS // 2 - 1) as i:
                w_fwd(2 * i, 2)
                w_fwd(2 * i, 3)
                s_copy(2 * i, 0)
                s_copy(2 * i, 1)
            s_copy(PAIRS - 2, 0)
            s_copy(PAIRS - 2, 1)
            dve.drain()

            a_re = A4R[:, :, :, :].rearrange("p d r q -> p (d r q)")
            a_im = A4I[:, :, :, :].rearrange("p d r q -> p (d r q)")
            swapped = sc2[:, :].rearrange("p (d r q) -> p d r q", d=DIRS, r=2)[:, :, ::-1, :]
            with dve.Fori(0, NCH - 1) as c:
                here = X[:, ds(c, 1), :, :].rearrange("p c r q -> p (c r q)")
                after = X[:, ds(c + 1, 1), :, :].rearrange("p c r q -> p (c r q)")
                after4 = X[:, ds(c + 1, 1), :, :].rearrange("p c (d r) q -> p (c d) r q", d=DIRS)
                mul(sc1[:, :], here, a_re)
                mul(sc2[:, :], here, a_im)
                dve.drain()
                dve.tensor_tensor(after, after, sc1[:, :], ALU.add)
                dve.drain()
                dve.tensor_tensor(after4, after4, swapped, ALU.add)
                dve.drain()
            dve.nop().then_inc(s_scan, 1)

            def g_fwd(p, k):
                dve.wait_ge(s_yps, p + (k - GSLOTS + 1 + SEED))
                g_make(dve, p + k, k % GSLOTS, 0, t1v, t2v).then_inc(s_gd, 1)
                dve.drain()

            def y_copy(p, i, k):
                dve.wait_ge(s_yps, p + (k + 1 + SEED))
                b = k % PB
                for j in range(CHUNK):
                    js = slice(32 * j, 32 * j + 32)
                    dst = yT[32 * b:32 * b + 32, ds(i, 1), :].rearrange("p a (c j) -> p j (a c)", j=CHUNK)[:, j, :]
                    last = dve.scalar_tensor_tensor(
                        out=dst, in0=U[js, ds(p + k, 1), :].rearrange("p a c -> p (a c)"), scalar=drep[js, ds(p + k, 1)],
                        in1=ps[js, 6 + k % 2, 0:NCH], op0=ALU.mult, op1=ALU.add)
                last.then_inc(s_ysb, 1)

            dve.wait_ge(s_kst, 16 * 16)
            dve.wait_ge(s_vst, 16 * 8)
            for k in range(GSLOTS):
                g_fwd(0, k)
            with dve.Fori(0, PAIRS // PB - 1) as i:
                for k in range(PB):
                    y_copy(PB * i, i, k)
                    g_fwd(PB * i, k + GSLOTS)
            for k in range(PB):
                y_copy(PAIRS - PB, PAIRS // PB - 1, k)

            dve.wait_ge(s_ygh, 1)
            dve.tensor_tensor(ygl[:, :, :], yT[:, :, LIVE:L], ygh[:, :, :].bitcast(F), ALU.subtract).then_inc(s_ygl, 1)

            def att_scores(i, k):
                dve.wait_ge(s_qk, 4 * i + (k + 1))
                dve.wait_ge(s_bm, 4 * i + (k + 1))
                dve.wait_ge(s_ptps, 4 * i + (k - 1 + SEED))
                bank = 2 * (k % 2)
                for t in range(2):
                    e0 = QROWS * (1 - t)
                    dve.scalar_tensor_tensor(
                        out=S[:, k % 2, t, N_META:L], in0=ps[:, bank + t, N_META:L], scalar=SCALE,
                        in1=bi[:, k, e0:e0 + GRID_ROWS, :].rearrange("p a b -> p (a b)"), op0=ALU.mult, op1=ALU.add)
                dve.tensor_scalar(S[:, k % 2, :, 0:N_META], ps[:, bank:bank + 2, 0:N_META], SCALE, None, ALU.mult)
                dve.drain()
                dve.reduce_max(stat[:, k, 0, :], S[:, k % 2, :, :], AX.X)
                dve.drain()
                dve.tensor_scalar(stat[:, k, 0, :], stat[:, k, 0, :], -1.0, None, ALU.mult).then_inc(s_nm, 1)

            def att_norm(i, k):
                dve.wait_ge(s_e, 4 * i + (k + 1))
                dve.reciprocal(stat[:, k, 1, :], stat[:, k, 1, :])
                dve.drain()
                for t in range(2):
                    last = dve.tensor_scalar(S[:, k % 2, t, :], S[:, k % 2, t, :], stat[:, k, 1, t:t + 1], None, ALU.mult)
                last.then_inc(s_p, 1)

            def att_lo(i, j):
                dve.wait_ge(s_ah, 2 * i + (j + 1))
                dve.tensor_tensor(anl[:, ds(2 * i + j, 1), 2:NL].rearrange("p k n -> p (k n)"),
                                  ps[:, 5, 0:SEQ],
                                  anh[:, ds(2 * i + j, 1), 2:NL].rearrange("p k n -> p (k n)").bitcast(F),
                                  ALU.subtract).then_inc(s_al, 1)

            def att_iteration(i, start):
                for k in range(4):
                    att_scores(i, k)
                    att_norm(i, k)
                    if k % 2 == 0 and (k or not start):
                        att_lo(i, k // 2 - 1)

            att_iteration(0, True)
            with dve.Fori(1, HEADS // 4) as i:
                att_iteration(i, False)
            att_lo(HEADS // 4 - 1, 1)

            dve.wait_ge(s_m1, 1)
            smf = sm[:, :, :, :].rearrange("p a b c -> p a (b c)")
            sm3 = sm[:, :, :, :].rearrange("p a b c -> p (a b) c")
            dve.tensor_scalar(smf, ps[0:2, 0:2, 0:P], SCALE, None, ALU.mult)
            dve.drain()
            dve.reduce_max(smx[:, 0, :], sm3, AX.X)
            dve.drain()
            dve.tensor_tensor(sm3, sm3, smx[:, 0, :].unsqueeze(2).to_broadcast([2, HEADS, N_META]), ALU.subtract)\
               .then_inc(s_m2, 1)
            dve.wait_ge(s_m3, 1)
            dve.reduce_sum(smx[:, 1, :], sm3, AX.X)
            dve.drain()
            dve.reciprocal(smx[:, 1, :], smx[:, 1, :])
            dve.drain()
            dve.tensor_tensor(sm3, sm3, smx[:, 1, :].unsqueeze(2).to_broadcast([2, HEADS, N_META]), ALU.mult)\
               .then_inc(s_m4, 1)
            dve.wait_ge(s_m8, 1)
            dve.tensor_tensor(anl[:, :, 0:2], ps[:, 3, 0:2 * KH].rearrange("p (b t) -> p b t", t=2),
                              anh[:, :, 0:2].bitcast(F), ALU.subtract).then_inc(s_al, 1)

            for n in range(KH):
                dve.wait_ge(s_sg, n + 1)
                if n >= 4:
                    dve.wait_ge(s_zl, n - 3)
                dve.tensor_tensor(mt[:, n % 4, :], yT[:, n, LIVE:L], gt[:, n % 4, :], ALU.mult).then_inc(s_z, 1)
                if n % 4 == 3:
                    for m in range(n - 3, n + 1):
                        dve.wait_ge(s_zh, m + 1)
                        dve.tensor_tensor(zl[:, m, :], mt[:, m % 4, :], zh[:, m, :].bitcast(F), ALU.subtract).then_inc(s_zl, 1)

            dve.wait_ge(s_g, 16 + SEED)
            dve.wait_ge(s_zl, KH)
            with dve.Fori(0, 4) as i:
                for k in range(2):
                    dve.wait_ge(s_used, 8 * i + (U_PROJ + 4 * (k + 1)))
                    for m in range(2):
                        f = 4 * i + (2 * k + m)
                        dve.tensor_tensor(mt[:, 2 * k + m, :], ps[:, 4 * k + m, 0:NL],
                                          gate_na[:, ds(f, 1), :].rearrange("p k n -> p (k n)"), ALU.mult)
                        dve.tensor_tensor(gt[:, 2 * k + m, :], ps[:, 4 * k + 2 + m, 0:NL],
                                          gate_ssm[:, ds(f, 1), :].rearrange("p k n -> p (k n)"), ALU.mult)
                    dve.drain()
                    for m in range(2):
                        dve.tensor_tensor(mt[:, 2 * k + m, :], mt[:, 2 * k + m, :], gt[:, 2 * k + m, :], ALU.add).then_inc(s_mx, 1)
                    for m in range(2):
                        f = 4 * i + (2 * k + m)
                        dve.wait_ge(s_mh, f + 1)
                        dve.tensor_tensor(hnl[:, ds(f, 1), 0:NL].rearrange("p k n -> p (k n)"), mt[:, 2 * k + m, :],
                                          hnh[:, ds(f, 1), 0:NL].rearrange("p k n -> p (k n)").bitcast(F),
                                          ALU.subtract).then_inc(s_ml, 1)

            dve.wait_ge(s_xre, 16)
            with dve.Fori(0, 4) as i:
                for k in range(2):
                    dve.wait_ge(s_used, 8 * i + (U_OUT + 4 * (k + 1)))
                    for m in range(2):
                        h = xT[:, ds(4 * i + (2 * k + m), 1), LIVE:L].rearrange("p k n -> p (k n)")
                        last = dve.tensor_tensor(h, h, ps[:, 2 * k + m, 0:NL], ALU.add)
                    last.then_inc(s_h1, 1)
            norm(1, LIVE, NL)

            with dve.Fori(0, FT // 4) as i:
                for k in range(2):
                    for m in range(2):
                        f = 4 * i + (2 * k + m)
                        dve.wait_ge(s_c, f + 1)
                        c = cv[:, k, m, :]
                        dve.scalar_tensor_tensor(out=c, in0=ps[:, 4 * k + m, 1:NL - 1], scalar=cvw[:, ds(f, 1)], in1=c,
                                                 op0=ALU.mult, op1=ALU.add)
                        dve.drain()
                        dve.scalar_tensor_tensor(out=cv[:, k, m, 0:SEQ - 1], in0=ps[:, 4 * k + m, 3:NL],
                                                 scalar=cvw[:, ds(f + 2 * FT, 1)], in1=cv[:, k, m, 0:SEQ - 1],
                                                 op0=ALU.mult, op1=ALU.add).then_inc(s_cd, 1)
                    dve.wait_ge(s_used, 16 * i + (U_UP + 8 * (k + 1)))
                    for m in range(2):
                        dve.wait_ge(s_ge, 4 * i + (2 * k + m + 1) + SEED)
                        dve.tensor_tensor(ge[:, k, m, :], ge[:, k, m, :], ps[:, 4 * k + 2 + m, 0:SEQ], ALU.mult)\
                           .then_inc(s_fm, 1)
                    for m in range(2):
                        f = 4 * i + (2 * k + m)
                        dve.wait_ge(s_fh, f + 1)
                        dve.tensor_tensor(al[:, ds(f, 1), :].rearrange("p k n -> p (k n)"), ge[:, k, m, :],
                                          ah[:, ds(f, 1), :].rearrange("p k n -> p (k n)").bitcast(F),
                                          ALU.subtract).then_inc(s_fl, 1)

            dve.wait_ge(s_used, U_END)
            for m in range(0, KT, 2):
                h = xT[:, m:m + 2, N_META:L]
                last = dve.tensor_tensor(h, h, ps[:, m // 2, :].rearrange("p (a b) -> p a b", a=2), ALU.add)
            last.then_inc(s_h2, 1)
            norm(2, N_META, SEQ)
            for k in range(KT):
                if k >= DEPTH:
                    dve.wait_ge(s_ot, k // DEPTH)
                dve.scalar_tensor_tensor(out=tr[:, k % DEPTH, 0:SEQ], in0=xT[:, k, N_META:L],
                                         scalar=gains[:, 2 * KT + k:2 * KT + k + 1], in1=rstd[:, 0:SEQ],
                                         op0=ALU.mult, op1=ALU.mult).then_inc(s_nt, 1)
                if k % DEPTH == DEPTH - 1:
                    n = k // DEPTH
                    dve.wait_ge(s_ot, n + 1)
                    for t in range(2):
                        last = dve.tensor_copy(otok[:, t, 512 * n:512 * (n + 1)], ps[:, 2 * (n % 2) + t, :])
                    dve.drain()
                    dve.nop().then_inc(s_oc, 1)

        @block.tensor
        def _(pe):
            for seeded in (s_pv, s_sq_used, s_vtp, s_ptps, s_wtp, s_sps, s_yps):
                pe.sem_inc(seeded, SEED)
            mm = nc.tensor.matmul

            def half_unit(base_u, k, q, units, m, xh, xl, lo, n, bank):
                if m == 0:
                    pe.wait_ge(s_lo, base_u + (k + 1))
                for t in range(UKT):
                    kt = q * UKT + t
                    cols = slice(t * CB + m * P, t * CB + (m + 1) * P)
                    o = ps[:, bank, 0:n]
                    mm(o, slot(whi, k)[:, cols], xh[:, kt, lo:lo + n], start=kt == 0, stop=False)
                    mm(o, slot(whi, k)[:, cols], xl[:, kt, lo:lo + n], start=False, stop=False)
                    ins = mm(o, slot(wlo, k)[:, cols], xh[:, kt, lo:lo + n], start=False, stop=kt == units * UKT - 1)
                if m == 1:
                    ins.then_inc(s_used, 1)

            def product(base_u, k0, units, xh, xl, lo, n, banks):
                for q in range(units):
                    for m in range(2):
                        half_unit(base_u, k0 + q, q, units, m, xh, xl, lo, n, banks[m])

            pe.wait_ge(s_x, 64)
            pe.wait_ge(s_const, 2)
            for k in range(KT):
                if k >= 4:
                    pe.wait_ge(s_xt, k - 3)
                cs = slice(k * P, (k + 1) * P)
                nc.tensor.transpose(ps[:, k % 4, 0:P], xtok[:, 0, cs], ident[:, :])
                nc.tensor.transpose(ps[:, k % 4, P:2 * P], xtok[:, 1, cs], ident[:, :])
                nc.tensor.transpose(ps[:, k % 4, 2 * P:L], xtok[0:N_META, 2, cs], ident[0:N_META, 0:N_META]).then_inc(s_xtp, 1)
            pe.wait_ge(s_par, 16 * 19)
            pe.wait_ge(s_rows, 1)
            nc.tensor.transpose(ps[:, 7, 0:48], grow[:, :], ident[0:48, 0:48])
            for n in range(2):
                nc.tensor.transpose(ps[:, 7, 48 + 88 * n:48 + 88 * (n + 1)], crow[:, n, :], ident[0:88, 0:88])
            for n in range(3):
                nc.tensor.transpose(ps[:, 7, 224 + 64 * n:224 + 64 * (n + 1)], rows[:, n, :], ident[0:64, 0:64])
            nc.tensor.transpose(ps[:, 7, 416:448], drow[:, :, :].rearrange("p a b -> p (a b)"), ident[0:32, 0:32])\
              .then_inc(s_ptp, 1)

            def norm_sums(which, n):
                for k in range(KT):
                    pe.wait_ge(s_sq, KT * which + k + 1)
                    ins = mm(ps[:, 6, 0:n], ones[:, :], sq[:, k % 2, 0:n], start=k == 0, stop=k == KT - 1)
                    ins.then_inc(s_sq_used, 1)
                pe.wait_ge(s_sq_used, KT * (which + 1) + SEED)
                pe.nop().then_inc(s_ss, 1)

            norm_sums(0, L)
            for n in range(4):
                d, q = n // 2, n % 2
                if n >= 2:
                    pe.wait_ge(s_ccp, n - 1)
                for b in range(4):
                    ins = nc.tensor.transpose(ps[:, 4 + n % 2, b * P:(b + 1) * P],
                                              cnat[:, d, 4 * q + b, :, :].rearrange("p r n -> p (r n)"), ident[:, :])
                ins.then_inc(s_ctp, 1)

            pe.wait_ge(s_nl, KT + SEED)
            with pe.Fori(0, ITERS_IN) as i:
                for k in range(2):
                    pe.wait_ge(s_u, 2 * i + SEED)
                    product(U_U + 8 * i, 4 * k, 4, hnh, hnl, 0, L, (2 * k, 2 * k + 1))
            pe.wait_ge(s_u, 4 + SEED)
            with pe.Fori(0, ITERS_IN) as i:
                for k in range(2):
                    pe.wait_ge(s_vtd, 2 * i + SEED)
                    product(U_V + 8 * i, 4 * k, 4, hnh, hnl, 0, L, (2 * k, 2 * k + 1))
                for k in range(2):
                    pe.wait_ge(s_vtd, 2 * i + (k + 1 + SEED))
                    pe.wait_ge(s_vcp, 2 * i + SEED)
                    for m in range(2):
                        for t in range(2):
                            nc.tensor.transpose(ps[:, 4 + 2 * k, t * CB + m * P:t * CB + (m + 1) * P],
                                                stg[:, k, m, t * P:(t + 1) * P], ident[:, :])
                        ins = nc.tensor.transpose(ps[0:N_META, 5 + 2 * k, m * P:(m + 1) * P],
                                                  stg[:, k, m, 2 * P:L], ident[:, :])
                    ins.then_inc(s_vtp, 1)

            def w_trans(p, k):
                pe.wait_ge(s_wd, p + (k + 1))
                pe.wait_ge(s_wp, p + (k + 1))
                pe.wait_ge(s_wts, p + (k - 1 + SEED))
                for d in range(DIRS):
                    for r in range(2):
                        n = 2 * d + r
                        ins = nc.tensor.transpose(ps[:, 4 + k % 2, n * P:(n + 1) * P], Wn[:, k % 2, d, r, :], ident[:, :])
                ins.then_inc(s_wtp, 1)

            def chunk_in(p, k):
                pe.wait_ge(s_wts, p + (k + 1 + SEED))
                pe.wait_ge(s_ssb, p + (k - 1 + SEED))
                for n in range(2 * DIRS):
                    u = U[:, ds(p + k, 1), :].rearrange("p a c -> p (a c)")
                    ins = mm(ps[:, 6 + k % 2, n * NCH:(n + 1) * NCH], WT[:, k % 2, n, :], u, start=True, stop=True)
                ins.then_inc(s_sps, 1)

            def beside(base_u, k, n, lo, first, second, p, bank):
                for m, step in ((0, first), (1, second)):
                    step(p, 2 * k)
                    step(p, 2 * k + 1)
                    half_unit(base_u, k, k % 4, 4, m, hnh, hnl, lo, n, bank + m)

            pe.wait_ge(s_vtd, 4 + SEED)
            pe.wait_ge(s_vcp, 4 + SEED)
            with pe.Fori(0, ITERS_IN) as i:
                for k in range(8):
                    if k % 4 == 0:
                        pe.wait_ge(s_kev, 2 * i + SEED)
                    beside(U_K + 8 * i, k, L, 0, w_trans, chunk_in, 16 * i, k // 4 * 2)
            with pe.Fori(0, ITERS_IN) as i:
                for k in range(2):
                    pe.wait_ge(s_kev, 2 * i + (4 + SEED))
                    product(U_Q + 8 * i, 4 * k, 4, hnh, hnl, LIVE, NL, (2 * k, 2 * k + 1))
            pe.wait_ge(s_kev, 8 + SEED)
            with pe.Fori(0, G_SCAN) as i:
                for k in range(2):
                    pe.wait_ge(s_g, 2 * i + SEED)
                    product(U_G + 8 * i, 4 * k, 4, hnh, hnl, LIVE, NL, (2 * k, 2 * k + 1))

            def kernel(p, k):
                pe.wait_ge(s_gd, p + (k + 1))
                pe.wait_ge(s_gp, p + (k + 1))
                pe.wait_ge(s_tm, p + (k - 1 + SEED))
                g = lambda d, r, a, b: Gn[:, k % GSLOTS, d, r, 32 * a:32 * b]
                bm = lambda d, r: Bm[:, k % GSLOTS, d, r, :]
                o = lambda a, b: ps[0:32, 4 + k % 2, 32 * a:32 * b]
                for r in range(2):
                    mm(o(0, CHUNK - 1), bm(1, r), g(1, r, 1, CHUNK), start=r == 0, stop=r == 1)
                for n in range(4):
                    d, r = n // 2, n % 2
                    e = CHUNK * d
                    mm(o(CHUNK - 1, CHUNK), bm(d, r), g(d, r, e, e + 1), start=n == 0, stop=n == 3)
                for r in range(2):
                    ins = mm(o(CHUNK, 2 * CHUNK - 1), bm(0, r), g(0, r, 1, CHUNK), start=r == 0, stop=r == 1)
                ins.then_inc(s_kps, 1)

            def chunk_out(p, k):
                pe.wait_ge(s_tm, p + (k + 1 + SEED))
                pe.wait_ge(s_ysb, p + (k - 1 + SEED))
                o = ps[:, 6 + k % 2, 0:NCH]
                mm(o, Tm[:, k % 2, :], U[:, ds(p + k, 1), :].rearrange("p a c -> p (a c)"), start=True, stop=False)
                for n in range(2 * DIRS):
                    d, r = n // 2, n % 2
                    st = X[:, 0:NCH, n, ds(p + k, 1)].rearrange("p c q -> p (c q)")
                    a = 32 * (1 - d)
                    ins = mm(o[:, ::-1] if d else o, Gn[:, k % GSLOTS, d, r, a:a + P], st, start=False, stop=n == 3)
                ins.then_inc(s_yps, 1)

            pe.wait_ge(s_ssb, PAIRS + SEED)
            pe.wait_ge(s_scan, 1)
            with pe.Fori(0, G_SSM) as i:
                for k in range(8):
                    if k % 4 == 0:
                        pe.wait_ge(s_g, 2 * i + (2 * G_SCAN + SEED))
                    beside(U_G + 8 * G_SCAN + 8 * i, k, NL, LIVE, kernel, chunk_out, 16 * i, k // 4 * 2)
            pe.wait_ge(s_g, 2 * (G_SCAN + G_SSM) + SEED)
            pe.wait_ge(s_ysb, PAIRS + SEED)

            def scores(i, k):
                j, hh = k // 2, k % 2
                if hh == 0:
                    pe.wait_ge(s_qkv[j], 64 * i + 64)
                pe.wait_ge(s_nm, 4 * i + (k - 1 + SEED))
                pe.wait_ge(s_ptsb, 4 * i + (k - 1 + SEED))
                hs = slice(DH * hh, DH * (hh + 1))
                for t in range(2):
                    ins = mm(ps[:, 2 * hh + t, 0:L], qs[hs, j, 2 + t * P:2 + (t + 1) * P], ks[hs, j, :], start=True, stop=True)
                ins.then_inc(s_qk, 1)

            def probs_t(i, k):
                pe.wait_ge(s_p, 4 * i + (k + 1))
                pe.wait_ge(s_ptsb, 4 * i + (k + SEED))
                for t in range(2):
                    for c in range(2):
                        nc.tensor.transpose(ps[:, 4, c * SEQ + t * P:c * SEQ + (t + 1) * P],
                                            S[:, k % 2, t, c * P:(c + 1) * P], ident[:, :])
                    ins = nc.tensor.transpose(ps[0:N_META, 2 * (k % 2) + t, L:L + P], S[:, k % 2, t, 2 * P:L], ident[:, :])
                ins.then_inc(s_ptps, 1)

            def values(i, k):
                j, hh = k // 2, k % 2
                pe.wait_ge(s_ptsb, 4 * i + (k + 1 + SEED))
                if hh == 0:
                    pe.wait_ge(s_al, 2 * i + (j + SEED))
                hs = slice(DH * hh, DH * (hh + 1))
                o = ps[hs, 5, 0:SEQ]
                mm(o, vs[:, j % 2, 0, hs], PT[:, k % 2, 0:SEQ], start=True, stop=False)
                mm(o, vs[:, j % 2, 1, hs], PT[:, k % 2, SEQ:2 * SEQ], start=False, stop=False)
                mm(o, vs[0:N_META, j % 2, 2, hs], PT2[:, k % 2, :], start=False, stop=True).then_inc(s_pv, 1)

            def att_iteration(i, start):
                for k in range(4):
                    base_u = U_G + 8 * (G_SCAN + G_SSM) + 8 * i
                    scores(i, k)
                    if k % 2 == 0:
                        pe.wait_ge(s_g, 2 * i + (2 * (G_SCAN + G_SSM) + k // 2 + SEED))
                    for q in range(2):
                        for m in range(2):
                            half_unit(base_u, 2 * k + q, 2 * (k % 2) + q, 4, m, hnh, hnl, LIVE, NL, 6 + m)
                        if q == 0 and (k or not start):
                            values(i, k - 1)
                    probs_t(i, k)

            att_iteration(0, True)
            with pe.Fori(1, HEADS // 4) as i:
                att_iteration(i, False)
            values(HEADS // 4 - 1, 3)
            pe.wait_ge(s_ptsb, HEADS + SEED)
            for h in range(HEADS):
                b, hh = h // 2, h % 2
                hs = slice(DH * hh, DH * (hh + 1))
                ins = mm(ps[0:2, hh, b * N_META:(b + 1) * N_META], qm[hs, b, :], km[hs, b, :], start=True, stop=True)
            ins.then_inc(s_m1, 1)
            pe.wait_ge(s_m4, 1)
            for h in range(HEADS):
                b, hh = h // 2, h % 2
                ins = nc.tensor.transpose(ps[0:N_META, 2, 2 * h:2 * h + 2], sm[:, hh, b, :], ident[0:2, 0:2])
            ins.then_inc(s_m5, 1)
            pe.wait_ge(s_m6, 1)
            for h in range(HEADS):
                b, hh = h // 2, h % 2
                hs = slice(DH * hh, DH * (hh + 1))
                ins = mm(ps[hs, 3, 2 * b:2 * b + 2], vm[:, b, hs], ptm[:, 2 * h:2 * h + 2], start=True, stop=True)
            ins.then_inc(s_m7, 1)
            pe.wait_ge(s_al, KH + 1 + SEED)

            pe.wait_ge(s_g, 16 + SEED)
            pe.wait_ge(s_ygl, 1)
            for k in range(4):
                product(U_GLU, 2 * k, 2, ygh, ygl, 0, NL, (2 * k, 2 * k + 1))
            pe.wait_ge(s_zl, KH)
            with pe.Fori(0, 4) as i:
                for k in range(2):
                    pe.wait_ge(s_mx, 4 * i + SEED)
                    product(U_PROJ + 8 * i, 4 * k, 2, anh, anl, 0, NL, (4 * k, 4 * k + 1))
                    product(U_PROJ + 8 * i, 4 * k + 2, 2, zh, zl, 0, NL, (4 * k + 2, 4 * k + 3))
            pe.wait_ge(s_ml, KT)
            with pe.Fori(0, 4) as i:
                for k in range(2):
                    pe.wait_ge(s_h1, 2 * i + SEED)
                    product(U_OUT + 8 * i, 4 * k, 4, hnh, hnl, 0, NL, (2 * k, 2 * k + 1))
            norm_sums(1, NL)
            pe.wait_ge(s_nl, 2 * KT + SEED)
            with pe.Fori(0, FT // 4) as i:
                for k in range(2):
                    pe.wait_ge(s_fm, 4 * i + SEED)
                    product(U_UP + 16 * i, 8 * k, 4, hnh, hnl, 0, NL, (4 * k, 4 * k + 1))
                    product(U_UP + 16 * i, 8 * k + 4, 4, hnh, hnl, 2, SEQ, (4 * k + 2, 4 * k + 3))

            def down(base_u, kt, k, first, final):
                pe.wait_ge(s_lo, base_u + (k + 1))
                xh = ah[:, kt, :] if isinstance(kt, int) else ah[:, ds(kt, 1), :].rearrange("p k n -> p (k n)")
                xl = al[:, kt, :] if isinstance(kt, int) else al[:, ds(kt, 1), :].rearrange("p k n -> p (k n)")
                for m in range(8):
                    g = 8 * (k % 2) + m
                    o = ps[:, g // 2, (g % 2) * SEQ:(g % 2 + 1) * SEQ]
                    cols = slice(m * P, (m + 1) * P)
                    mm(o, slot(whi, k)[:, cols], xh, start=first and g % 2 == 0, stop=False, skip_group_check=True)
                    mm(o, slot(whi, k)[:, cols], xl, start=False, stop=False, skip_group_check=True)
                    ins = mm(o, slot(wlo, k)[:, cols], xh, start=False, stop=final, skip_group_check=True)
                ins.then_inc(s_used, 1)

            pe.wait_ge(s_fl, FT + SEED)
            for k in range(4):
                down(U_DOWN, k // 2, k, k < 2, False)
            with pe.Fori(1, FT // 2 - 1) as i:
                for k in range(4):
                    down(U_DOWN + 4 * i, 2 * i + k // 2, k, False, False)
            for k in range(4):
                down(U_END - 4, FT - 2 + k // 2, k, False, k >= 2)

            norm_sums(2, SEQ)
            for n in range(KT // DEPTH):
                if n >= 2:
                    pe.wait_ge(s_oc, n - 1)
                for k in range(DEPTH):
                    pe.wait_ge(s_nt, 2 * KT + DEPTH * n + k + 1)
                    for t in range(2):
                        ins = nc.tensor.transpose(ps[:, 2 * (n % 2) + t, k * P:(k + 1) * P],
                                                  tr[:, k, t * P:(t + 1) * P], ident[:, :])
                ins.then_inc(s_ot, 1)


_INS = ["x", "meta_tokens", "norm1_g", "w_in", "na_rpb", "ssm_lam_re", "ssm_lam_im", "ssm_log_step", "ssm_b_re",
        "ssm_b_im", "ssm_c_re", "ssm_c_im", "ssm_d", "w_glu", "w_proj_na", "w_proj_ssm", "w_out", "norm2_g",
        "w_up", "conv_w", "conv_b", "w_down", "final_g"]


def kernel(**inputs):
    import numpy as _np
    import concourse.bacc as _bacc
    from concourse import mybir as _mybir
    from concourse.bass_utils import run_bass_kernel_spmd as _run

    nc = _bacc.Bacc("TRN2", target_bir_lowering=False, num_devices=1)
    arrays, args = {}, []
    for name in _INS:
        a = _np.ascontiguousarray(inputs[name])
        arrays[f"in_{name}"] = a
        args.append(nc.dram_tensor(f"in_{name}", a.shape, _mybir.dt.from_np(a.dtype), kind="ExternalInput").ap())
    args.append(nc.dram_tensor("out_h", (1, SEQ, D_MODEL), _mybir.dt.float32, kind="ExternalOutput").ap())
    encoder_block(nc, *args)
    r = _run(nc, [arrays], core_ids=[0])
    return r.results[0]["out_h"]
```

```python
import math
from contextlib import ExitStack

import numpy as np
import concourse.bass as bass
from concourse import mybir

D_MODEL = 2048
SEQ = 256
N_META = 16
GRID_W = 64
ROW_WIN = 8
COL_WIN = 16
DH = 64
HEADS = (D_MODEL // 2) // DH
HALF = D_MODEL // 2
GROUP = 16
GROUPS = HALF // GROUP
STATE = 64
D_FF = ((8 * D_MODEL // 3 + 255) // 256) * 256
EPS = 1e-6
SEED = 4
DIRS = 2

P = 128
L = N_META + SEQ
LIVE = N_META - 2
NL = L - LIVE
KT = D_MODEL // P
KH = HALF // P
FT = D_FF // P
DEPTH = 4
UNIT = 1024
CB = 256
UKT = UNIT // CB
G_SCAN = 6
G_SSM = 2
G_ATT = 2 * KT // 2 - G_SCAN - G_SSM
CHUNK = 4
NCH = L // CHUNK
PAIRS = GROUPS // 2
SCAN_STEPS = 6
WSLOTS = 4
GSLOTS = 4
PB = P // (2 * GROUP)
PPU = PAIRS // (4 * G_SSM)
GRID_ROWS = SEQ // GRID_W
SCALE = DH ** -0.5
MASKED = -1e30
PADW = 2 * GRID_W - 1
RPB_COLS = 2 * COL_WIN - 1
QROWS = P // GRID_W
DROWS = 2 * GRID_ROWS - 1
EWIN = GRID_ROWS + QROWS * (SEQ // P - 1)
TWO_PI_HI = 6.28125
TWO_PI_MID = 0.0019350051879882812
TWO_PI_LO = 2 * math.pi - TWO_PI_HI - TWO_PI_MID
ROUND = 1.5 * 2 ** 23
PI_BELOW = 3.1415925


def encoder_block(nc, x, meta, norm1_g, w_in, rpb, lam_re, lam_im, log_step, b_re, b_im, c_re, c_im,
                  ssm_d, w_glu, w_proj_na, w_proj_ssm, w_out, norm2_g, w_up, conv_w, conv_b, w_down,
                  final_g, out):
    F = mybir.dt.float32
    R = mybir.dt.float32r
    ACT = mybir.ActivationFunctionType
    ALU = mybir.AluOpType
    AX = mybir.AxisListType
    ds = bass.ds

    q_d = nc.dram_tensor("q_scratch", [KH, P, NL], F, kind="Internal").ap()
    k_d = nc.dram_tensor("k_scratch", [KH, P, L], F, kind="Internal").ap()
    v_d = nc.dram_tensor("v_scratch", [L, HALF], F, kind="Internal").ap()
    xT_d = nc.dram_tensor("xT_scratch", [P, KT * L], F, kind="Internal").ap()
    pad_d = nc.dram_tensor("rpb_scratch", [HEADS * DROWS, PADW], F, kind="Internal").ap()
    skew_d = nc.dram_tensor("skew_scratch", [GRID_W, HEADS * DROWS, GRID_W], F, kind="Internal").ap()

    ctx = ExitStack()
    with ctx:
        def sem(name):
            return ctx.enter_context(nc.semaphore(name))

        base = (nc.sbuf_base + 31) // 32 * 32
        cursor = [base]

        def keep(name, shape, dt=F):
            t = nc.alloc_sbuf_tensor_at(name, shape, dt, offset=cursor[0])
            cursor[0] += (int(np.prod(shape[1:])) * 4 + 31) // 32 * 32
            return t

        raw = keep("w_raw", [P, DEPTH, UNIT])
        whi = keep("w_hi", [P, DEPTH, UNIT], R)
        wlo = keep("w_lo", [P, DEPTH, UNIT], R)
        hnh = keep("act_hi", [P, KT, L], R)
        hnl = keep("act_lo", [P, KT, L], R)
        o_tr = cursor[0]
        tr = keep("norm_ring", [P, DEPTH, L])
        vm = nc.alloc_sbuf_tensor_at("v_meta", [N_META, KH, P], F, offset=o_tr)
        o_sq = cursor[0]
        sq = keep("square_ring", [P, 2, L])
        rstd = keep("rstd", [P, L])
        ident = keep("ident", [P, P])
        ones = keep("ones", [P, P])
        gains = keep("gains", [P, 2 * KT])
        cvw = keep("conv_params", [P, 4 * FT])
        mask = keep("col_mask", [P, GRID_W])
        stat = keep("att_stats", [P, 4, 2, 2])
        arena = (cursor[0] + 31) // 32 * 32

        def at(name, off, shape, dt=F):
            assert off % 32 == 0 and arena + off + int(np.prod(shape[1:])) * 4 <= nc.sbuf_usable_end, (name, off)
            return nc.alloc_sbuf_tensor_at(name, shape, dt, offset=arena + off)

        xtok = at("x_tokens", 0, [P, 3, D_MODEL])
        X = at("scan_states", 0, [P, NCH + 1, 2 * DIRS, PAIRS])
        gate_ssm = at("gate_ssm", 0, [P, KT, NL])
        ygh = at("gelu_hi", 16512, [P, KH, NL], R)
        ygl = at("gelu_lo", 16512 + 8256, [P, KH, NL], R)
        o_y = 35328
        yT = at("y_ssm", o_y, [P, KH, L])
        x0T = at("x_feature_major", o_y, [P, KT, L])
        braw = at("b_raw", 24576, [P, 2, DIRS * PAIRS, GROUP])
        o_u = o_y + KH * L * 4
        U = at("u_chunks", o_u, [P, PAIRS, NCH])
        stg = at("qkv_stage", o_u + 8704, [P, 2, 2, L])
        vst = at("v_stage", o_u + 8704 + 4352, [P, 3, CB])
        Gn = at("g_nat", o_u + 8704, [P, GSLOTS, DIRS, 2, 160])
        anh = at("attn_hi", o_u, [P, KH, NL], R)
        anl = at("attn_lo", o_u + 8256, [P, KH, NL], R)
        o_p = o_u + 8704 + 10240
        BB = at("b_bar", o_p, [P, DIRS * PAIRS, 3, GROUP])
        CC = at("c_slots", o_p + 12288, [P, DIRS * PAIRS, 3, GROUP])
        pwG = at("pow_out", o_p + 24576, [P, DIRS * PAIRS, 2, CHUNK + 1])
        A4R = at("chunk_re", o_p + 27136, [P, DIRS, 2, PAIRS])
        A4I = at("chunk_im", o_p + 27648, [P, DIRS, 2, PAIRS])
        dD = at("d_diagonal", o_p + 28160, [P, PAIRS, 2 * GROUP])
        o_r = o_p + 32256
        cnat = at("c_rows", o_r, [P, DIRS, KH, 2, STATE])
        prm = at("params", o_r + 8192, [P, 24, DIRS * PAIRS])
        pw = at("powers", o_r + 8192 + 6144, [P, CHUNK + 1, 2, DIRS * PAIRS])
        rows = at("param_rows", o_r + 8192 + 6144 + 2560, [DIRS * PAIRS, 3, P])
        lst = at("step_rows", o_r + 18432, [DIRS * PAIRS, 8])
        drow = at("d_rows", o_r + 18464, [PAIRS, 2 * GROUP])
        btmp = at("b_tmp", 0, [P, 2, UNIT])
        grow = at("gain_rows", o_r + 18976, [2 * KT, P])
        crow = at("conv_rows", o_r + 19488, [2 * FT, 2, P])
        padt = at("rpb_pad", o_u + 13056, [HEADS * DROWS, P])
        t1p = at("t1_p", o_r, [P, 320])
        t2p = at("t2_p", o_r + 1280, [P, 320])
        Tm = at("toeplitz", o_r + 2560, [P, 2, P])
        Bm = at("b_masked", o_r + 3584, [P, GSLOTS, DIRS, 2, 2 * GROUP])
        sc1 = at("scan_t1", o_r + 5632, [P, P])
        sc2 = at("scan_t2", o_r + 6144, [P, P])
        o_g = o_r + 6656
        Wn = at("w_nat", o_g, [P, WSLOTS, DIRS, 2, P])
        WT = at("w_tr", o_g + 8192, [P, 2, 2 * DIRS, P])
        pwW = at("pow_in", o_r + 21088, [P, DIRS * PAIRS, 2, CHUNK])
        gate_na = at("gate_na", o_g, [P, KT, NL])
        t1v = nc.alloc_sbuf_tensor_at("t1_v", [P, 320], F, offset=o_sq)
        t2v = nc.alloc_sbuf_tensor_at("t2_v", [P, 320], F, offset=o_sq + 1280)
        qm = nc.alloc_sbuf_tensor_at("q_meta", [P, KH, 2], F, offset=o_sq + 2560)
        km = nc.alloc_sbuf_tensor_at("k_meta", [P, KH, N_META], F, offset=o_sq + 2624)
        o_a = o_p
        qs = at("q_ring", o_a, [P, 2, NL])
        ks = at("k_ring", o_a + 2080, [P, 2, L])
        vs = at("v_ring", o_a + 4256, [P, 2, 3, P])
        bi = at("bias_ring", o_a + 7328, [P, 4, EWIN, GRID_W])
        S = at("scores", o_a + 13472, [P, 2, 2, L])
        PT = at("probs_t", o_a + 17824, [P, 2, 2 * SEQ])
        PT2 = at("probs_t2", o_a + 21920, [N_META, 2, SEQ])
        sm = at("meta_scores", o_r + 5632, [2, 2, KH, N_META])
        smx = nc.alloc_sbuf_tensor_at("meta_stats", [2, 4, HEADS], F, offset=o_tr + 4096)
        ptm = at("meta_probs_t", o_a + 25248, [N_META, 2 * HEADS])
        zh = at("z_hi", o_a, [P, KH, NL], R)
        zl = at("z_lo", o_a + 8256, [P, KH, NL], R)
        gt = at("glu_ring", o_a + 16512, [P, 4, NL])
        mt = at("mix_ring", o_a + 16512 + 4128, [P, 4, NL])
        ah = at("hidden_hi", 0, [P, FT, SEQ], R)
        al = at("hidden_lo", 45056, [P, FT, SEQ], R)
        cv = at("conv_ring", 90112, [P, 2, 2, SEQ])
        ge = at("gelu_ring", 94208, [P, 2, 2, SEQ])
        o_x = 98304
        xT = at("xT", o_x, [P, KT, L])
        otok = at("out_tokens", 0, [P, SEQ // P, D_MODEL])
        grep = at("final_gain", 90112, [P, D_MODEL])
        sqt = at("token_squares", 16384, [P, 2, 512])
        fin = at("final_stats", 20480, [P, 2, KT // 2])

        ps = ctx.enter_context(nc.psum_tensor("ps", [P, 8, 512], F))

        s_x = [sem(f"x_loaded_{h}") for h in range(2)]
        s_gain = sem("gains_loaded")
        s_gtp = sem("gains_transposed")
        s_gcp = sem("gains_copied")
        s_par = sem("params_loaded")
        s_fg = sem("final_gain_loaded")
        s_raw = [sem(f"unit_loaded_{i}") for i in range(DEPTH)]
        s_hi = sem("unit_hi_made")
        s_lo = sem("unit_split")
        s_used = sem("unit_consumed")
        s_const = sem("constants_made")
        s_xtp = sem("x_transposed")
        s_xt = sem("xT_copied")
        s_sq = sem("squares_made")
        s_ss = sem("squares_summed")
        s_sq_used = sem("square_tile_summed")
        s_var = sem("variance_made")
        s_sd = sem("deviation_made")
        s_nt = sem("norm_tile_made")
        s_nh = sem("norm_hi_made")
        s_nl = sem("norm_lo_made")
        s_spill = sem("xT_spilled")
        s_xre = sem("xT_reloaded")
        s_rows = sem("rows_ready")
        s_ptp = sem("params_transposed")
        s_pcp = sem("params_copied")
        s_pd = sem("param_step_dve")
        s_pa = sem("param_step_act")
        s_ctp = sem("c_transposed")
        s_ccp = sem("c_copied")
        s_u = sem("u_chunks_ready")
        s_kev = sem("qkv_block_copied")
        s_kst = sem("qk_stored")
        s_vtd = sem("v_block_copied")
        s_vtp = sem("v_transposed")
        s_vcp = sem("v_copied")
        s_vst = sem("v_stored")
        s_wd = sem("w_fwd_made")
        s_wp = sem("w_bwd_made")
        s_wtp = sem("w_transposed")
        s_wts = sem("w_copied")
        s_sps = sem("chunk_inputs_summed")
        s_ssb = sem("chunk_inputs_copied")
        s_scan = sem("scan_done")
        s_bz = sem("b_masked_zeroed")
        s_bb = sem("b_masked_filled")
        s_gd = sem("g_fwd_made")
        s_gp = sem("g_bwd_made")
        s_kps = sem("kernel_summed")
        s_tm = sem("toeplitz_copied")
        s_yps = sem("y_summed")
        s_ysb = sem("y_copied")
        s_ysa = sem("y_copied_by_act")
        s_ygh = sem("gelu_hi_made")
        s_ygl = sem("gelu_lo_made")
        s_pad1 = sem("pad_zeroed")
        s_pad2 = sem("pad_filled")
        s_pad3 = sem("pad_skewed")
        s_qkv = [sem(f"qkv_loaded_{i}") for i in range(2)]
        s_bl = [sem(f"bias_loaded_{i}") for i in range(4)]
        s_bm = sem("bias_masked")
        s_qk = sem("scores_summed")
        s_nm = sem("row_max_ready")
        s_e = sem("exp_made")
        s_p = sem("probs_ready")
        s_ptps = sem("probs_transposed")
        s_ptsb = sem("probs_copied")
        s_pv = sem("pv_summed")
        s_ah = sem("attn_hi_made")
        s_al = sem("attn_lo_made")
        s_m1 = sem("meta_scores_summed")
        s_m2 = sem("meta_shifted")
        s_m3 = sem("meta_exp_made")
        s_m4 = sem("meta_probs_ready")
        s_m5 = sem("meta_probs_transposed")
        s_m6 = sem("meta_probs_copied")
        s_m7 = sem("meta_pv_summed")
        s_m8 = sem("meta_hi_made")
        s_mal = sem("meta_lo_made")
        s_g = sem("gates_made")
        s_gs = sem("gate_sigmoid_made")
        s_sg = sem("glu_gate_made")
        s_z = sem("z_made")
        s_zh = sem("z_hi_made")
        s_zl = sem("z_lo_made")
        s_mx = sem("mix_made")
        s_mh = sem("mix_hi_made")
        s_ml = sem("mix_lo_made")
        s_h1 = sem("h1_block_added")
        s_c = sem("conv_started")
        s_cd = sem("conv_made")
        s_ge = sem("hidden_gelu_made")
        s_fm = sem("hidden_made")
        s_fh = sem("hidden_hi_made")
        s_fl = sem("hidden_lo_made")
        s_h2 = sem("h2_made")
        s_ot = sem("out_transposed")
        s_oc = sem("out_copied")
        s_oc1 = sem("out_half_made")
        s_sum = sem("token_squares_summed")
        s_rs = sem("final_scale_made")
        s_out = sem("out_stored")

        block = ctx.enter_context(nc.Block())

        U_U, U_V, U_K, U_Q, U_G = 0, 16, 32, 48, 64
        U_GLU = U_G + 64
        U_PROJ = U_GLU + 8
        U_OUT = U_PROJ + 32
        U_UP = U_OUT + 32
        U_DOWN = U_UP + 4 * FT
        U_END = U_DOWN + 2 * FT
        ITERS_IN = 2

        def kblock(w, col, kq):
            return w[kq * UKT * P:(kq + 1) * UKT * P, ds(col, CB)].rearrange("(t p) c -> p t c", p=P)

        def slot(ring, k):
            return ring[:, k % DEPTH, :]

        @block.sync
        def _(sp):
            for h in range(2):
                cs = slice(h * HALF, (h + 1) * HALF)
                sp.dma_start(xtok[0:N_META, 0, cs], meta[:, cs]).then_inc(s_x[h], 16)
                sp.dma_start(xtok[N_META:P, 0, cs], x[0, 0:P - N_META, cs]).then_inc(s_x[h], 16)
                sp.dma_start(xtok[:, 1, cs], x[0, P - N_META:2 * P - N_META, cs]).then_inc(s_x[h], 16)
                sp.dma_start(xtok[0:N_META, 2, cs], x[0, 2 * P - N_META:SEQ, cs]).then_inc(s_x[h], 16)

            def load(base_u, k, src):
                if isinstance(base_u, int) and base_u + k < DEPTH:
                    pass
                else:
                    sp.wait_ge(s_lo, base_u + (k - DEPTH + 1))
                dst = slot(raw, k)
                if len(src.shape) == 3:
                    dst = dst.rearrange("p (t c) -> p t c", t=src.shape[1])
                sp.dma_start(dst, src).then_inc(s_raw[k % DEPTH], 16)

            def load_in(first, col0, i, units=range(8)):
                for k in units:
                    load(first + 8 * i, k, kblock(w_in[0], i * (2 * CB) + (col0 + (k // 4) * CB), k % 4))

            load_in(U_U, 3 * HALF, 0, range(DEPTH))
            sp.wait_ge(s_xt, KT)
            sp.dma_start(xT_d, x0T[:, :, :].rearrange("p k t -> p (k t)")).then_inc(s_spill, 16)
            load_in(U_U, 3 * HALF, 0, range(DEPTH, 8))
            with sp.Fori(1, ITERS_IN) as i:
                load_in(U_U, 3 * HALF, i)
            with sp.Fori(0, ITERS_IN) as i:
                load_in(U_V, 2 * HALF, i)
            sp.wait_ge(s_pad2, 16)
            with sp.Fori(0, ITERS_IN) as i:
                for k in range(8):
                    load_in(U_K, HALF, i, (k,))
                    for n in range(GRID_W // (8 * ITERS_IN)):
                        c = i * (GRID_W // ITERS_IN) + (k * (GRID_W // (8 * ITERS_IN)) + n)
                        sp.dma_start(skew_d[ds(c, 1), :, :].rearrange("a r w -> (a r) w"),
                                     pad_d[:, ds((GRID_W - 1) - c, GRID_W)]).then_inc(s_pad3, 16)
            with sp.Fori(0, ITERS_IN) as i:
                load_in(U_Q, 0, i)

            with sp.Fori(0, 8) as i:
                load_in(U_G, 4 * HALF, i)
            for k in range(8):
                load(U_GLU, k, kblock(w_glu[0], (k // 2) * CB, k % 2))
            with sp.Fori(0, 4) as i:
                for k in range(8):
                    w = (w_proj_na, w_proj_ssm)[k % 4 // 2]
                    load(U_PROJ + 8 * i, k, kblock(w[0], i * (2 * CB) + (k // 4) * CB, k % 2))
            with sp.Fori(0, 4) as i:
                for k in range(8):
                    load(U_OUT + 8 * i, k, kblock(w_out[0], i * (2 * CB) + (k // 4) * CB, k % 4))
            with sp.Fori(0, FT // 4) as i:
                for k in range(16):
                    col = i * (2 * CB) + ((k // 8) * CB + (k % 8 // 4) * D_FF)
                    load(U_UP + 16 * i, k, kblock(w_up[0], col, k % 4))
            with sp.Fori(0, FT // 2) as i:
                for k in range(4):
                    src = w_down[0][ds(i * (2 * P) + (k // 2) * P, P), (k % 2) * UNIT:(k % 2 + 1) * UNIT]
                    load(U_DOWN + 4 * i, k, src)
            for n in range(SEQ // P):
                sp.wait_ge((s_oc, s_oc1)[n], 1)
                sp.dma_start(out[0, n * P:(n + 1) * P, :], otok[:, n, :]).then_inc(s_out, 16)
            sp.wait_ge(s_out, 32)

        def hi_unit(act, base_u, k):
            act.wait_ge(s_raw[k % DEPTH], base_u * 4 + 16 * (k // DEPTH + 1))
            if not (isinstance(base_u, int) and base_u + k < DEPTH):
                act.wait_ge(s_used, base_u + (k - DEPTH + 1))
            act.activation(slot(whi, k), slot(raw, k), ACT.Copy).then_inc(s_hi, 1)

        def lo_unit(pool, base_u, k):
            pool.wait_ge(s_hi, base_u + (k + 1))
            pool.tensor_tensor(slot(wlo, k), slot(raw, k), slot(whi, k).bitcast(F), ALU.subtract).then_inc(s_lo, 1)

        def split_loop(eng, unit, first, iters, per):
            with eng.Fori(0, iters) as i:
                for k in range(per):
                    unit(eng, (first + DEPTH) + per * i, k)

        def norm_lo(pool, which, n):
            with pool.Fori(0, KT // DEPTH) as i:
                for k in range(DEPTH):
                    pool.wait_ge(s_nh, DEPTH * i + (KT * which + k + 1))
                    pool.tensor_tensor(hnl[:, ds(DEPTH * i + k, 1), 0:n].rearrange("p k n -> p (k n)"), tr[:, k, 0:n],
                                       hnh[:, ds(DEPTH * i + k, 1), 0:n].rearrange("p k n -> p (k n)").bitcast(F),
                                       ALU.subtract).then_inc(s_nl, 1)

        def matrices(eng, dst, powers, tab, first, second, pair, sl, d, t1, t2):
            n = powers.shape[3]
            dq = ds(pair + d * PAIRS, 2)
            full = [P, 2, n, GROUP]
            a = t1[:, 0:4 * n * GROUP].rearrange("p (q r n c) -> p q r n c", q=2, r=2, c=GROUP)
            b = t2[:, 0:4 * n * GROUP].rearrange("p (q r n c) -> p q r n c", q=2, r=2, c=GROUP)
            for o, part, at_slot in ((a, 0, first), (b, 1, second)):
                for r in range(2):
                    eng.tensor_tensor(o[:, :, r, :, :], powers[:, dq, part, :].unsqueeze(3).to_broadcast(full),
                                      tab[:, dq, at_slot + r, :].unsqueeze(2).to_broadcast(full), ALU.mult)
            eng.drain()
            for h in range(2):
                hs = slice(64 * h, 64 * h + 64)
                o = dst[hs, sl:sl + 2, d, :, :].rearrange("p q r (n g c) -> p q r n g c", g=2, c=GROUP)[:, :, :, :, h, :]
                last = eng.tensor_tensor(o, a[hs], b[hs], ALU.add)
            return last

        def w_make(eng, pair, sl, d, t1, t2):
            return matrices(eng, Wn, pwW, BB, 1, 0, pair, sl, d, t1, t2)

        def g_make(eng, pair, sl, d, t1, t2):
            return matrices(eng, Gn, pwG, CC, 0, 1, pair, sl, d, t1, t2)

        def y_copy(copy, eng, p, i, k, half, done):
            eng.wait_ge(s_yps, p + (k + 1 + SEED))
            b = k % PB
            for j in range(half * CHUNK // 2, (half + 1) * CHUNK // 2):
                dst = yT[32 * b:32 * b + 32, ds(i + k // PB, 1), :].rearrange("p a (c j) -> p j (a c)", j=CHUNK)[:, j, :]
                last = copy(dst, ps[32 * j:32 * j + 32, 6 + k % 2, 0:NCH])
            last.then_inc(done, 1)

        @block.gpsimd
        def _(pool):
            pool.sem_inc(s_nl, SEED)
            pool.memset(ones[:, :], 1.0).then_inc(s_const, 1)
            pool.memset(ident[:, :], 0.0)
            pool.memset(mask[:, :], 0.0)
            pool.memset(padt[:, :], 0.0)
            pool.drain()
            pool.affine_select(out=ident[:, :], in_=ident[:, :], compare_op=ALU.not_equal, fill=1.0,
                               base=0, pattern=[[-1, P]], channel_multiplier=1).then_inc(s_const, 1)
            pool.drain()
            far = GRID_W - COL_WIN
            for r in range(QROWS):
                m = mask[r * GRID_W:(r + 1) * GRID_W, 0:far]
                pool.affine_select(out=m, in_=m, compare_op=ALU.is_ge, fill=MASKED, base=COL_WIN // 2,
                                   pattern=[[1, far]], channel_multiplier=-1)
                pool.drain()
            pool.drain()
            for r in range(QROWS):
                m = mask[r * GRID_W:(r + 1) * GRID_W, COL_WIN:GRID_W]
                pool.affine_select(out=m, in_=m, compare_op=ALU.is_ge, fill=MASKED,
                                   base=COL_WIN // 2 - 1 - COL_WIN, pattern=[[-1, far]], channel_multiplier=1)
                pool.drain()
            pool.drain()
            for k in range(DEPTH - 1):
                lo_unit(pool, 0, k)
            norm_lo(pool, 0, L)
            lo_unit(pool, 0, DEPTH - 1)
            pool.dma_start(pad_d, padt[:, 0:PADW]).then_inc(s_pad1, 16)
            pool.wait_ge(s_pad1, 16)
            pool.dma_start(pad_d[:, GRID_W - COL_WIN:GRID_W - COL_WIN + RPB_COLS].rearrange("(h d) c -> h d c", h=HEADS),
                           rpb[0, :, ROW_WIN - GRID_ROWS:ROW_WIN - GRID_ROWS + DROWS, :]).then_inc(s_pad2, 16)

            split_loop(pool, lo_unit, U_U, ITERS_IN, 8)
            split_loop(pool, lo_unit, U_V, ITERS_IN - 1, 8)

            def w_bwd(p, k):
                pool.wait_ge(s_wtp, p + (k - WSLOTS + 2 + SEED))
                w_make(pool, p + k, k % WSLOTS, 1, t1p, t2p).then_inc(s_wp, 2)
                pool.drain()

            pool.wait_ge(s_pd, 1)
            pool.wait_ge(s_ccp, 4)
            pool.memset(Wn[:, :, :, :, :], 0.0)
            pool.memset(Bm[:, :, :, :, :], 0.0).then_inc(s_bz, 1)
            pool.drain()
            for k in range(8):
                if k in (3, 5):
                    w_bwd(0, k - 3)
                lo_unit(pool, U_K - 8 + DEPTH, k)
            with pool.Fori(0, ITERS_IN - 1) as i:
                for k in range(8):
                    w_bwd(16 * i, 2 * k + 4)
            for k in range(6):
                w_bwd(PAIRS - 16, 2 * k + 4)
            pool.wait_ge(s_lo, U_Q + DEPTH)
            split_loop(pool, lo_unit, U_Q, ITERS_IN, 8)
            split_loop(pool, lo_unit, U_G, G_SCAN // 2 - 1, 8)

            def g_bwd(p, k):
                pool.wait_ge(s_yps, p + (k - GSLOTS + 2 + SEED))
                g_make(pool, p + k, k % GSLOTS, 1, t1p, t2p).then_inc(s_gp, 2)
                pool.drain()

            pool.wait_ge(s_kst, 16 * 16)
            pool.wait_ge(s_vst, 16 * 8)
            pool.memset(Gn[:, :, :, :, :], 0.0).then_inc(s_bz, 1)
            pool.drain()
            for k in range(0, GSLOTS, 2):
                g_bwd(0, k)
                for n in range(4):
                    lo_unit(pool, U_G + 4 * G_SCAN - 8 + DEPTH, 2 * k + n)
            with pool.Fori(0, G_SSM - 1) as i:
                for k in range(4):
                    for n in range(0, PPU, 2):
                        g_bwd(4 * PPU * i, PPU * k + n + GSLOTS)
            for k in range(3):
                for n in range(0, PPU, 2):
                    g_bwd(PAIRS - 4 * PPU, PPU * k + n + GSLOTS)
            pool.wait_ge(s_lo, U_G + 4 * (G_SCAN + G_SSM) + DEPTH)

            with pool.Fori(0, HEADS // 4) as i:
                for k in range(4):
                    if k % 2 == 0:
                        for hh in range(2):
                            pool.wait_ge(s_bl[k + hh], 32 * i + 32)
                            pool.tensor_tensor(bi[:, k + hh, :, :], bi[:, k + hh, :, :],
                                               mask[:, :].unsqueeze(1).to_broadcast([P, EWIN, GRID_W]), ALU.add)\
                                .then_inc(s_bm, 1)
                    lo_unit(pool, (U_G + DEPTH + 4 * (G_SCAN + G_SSM)) + 8 * i, 2 * k)
                    lo_unit(pool, (U_G + DEPTH + 4 * (G_SCAN + G_SSM)) + 8 * i, 2 * k + 1)
            for k in range(8):
                lo_unit(pool, U_GLU + DEPTH, k)
            split_loop(pool, lo_unit, U_PROJ, 4, 8)
            split_loop(pool, lo_unit, U_OUT, 4, 8)
            norm_lo(pool, 1, NL)
            split_loop(pool, lo_unit, U_UP, FT // 4, 16)
            split_loop(pool, lo_unit, U_DOWN, FT // 2 - 1, 4)

        @block.scalar
        def _(act):
            for seeded in (s_ptsb, s_g, s_ge, s_u, s_kev, s_vtd, s_vcp, s_wts, s_tm, s_ysa):
                act.sem_inc(seeded, SEED)
            for n, g in enumerate((norm1_g[0], norm2_g[0])):
                act.dma_start(grow[n * KT:(n + 1) * KT, :], g.rearrange("(k p) -> k p", p=P)).then_inc(s_gain, 16)
            def squares(src, tile, t, ring, k, lo, n):
                act.wait_ge(s_sq_used, t + (SEED - ring.shape[1]))
                act.activation(ring[:, k, 0:n], src[:, ds(tile, 1), lo:lo + n].rearrange("p k n -> p (k n)"),
                               ACT.Square).then_inc(s_sq, 1)

            def norm_root(which, n):
                act.wait_ge(s_var, which + 1)
                act.activation(rstd[:, 0:n], rstd[:, 0:n], ACT.Sqrt).then_inc(s_sd, 1)

            def norm_hi(which, n):
                with act.Fori(0, KT // DEPTH) as i:
                    for k in range(DEPTH):
                        act.wait_ge(s_nt, DEPTH * i + (KT * which + k + 1))
                        act.activation(hnh[:, ds(DEPTH * i + k, 1), 0:n].rearrange("p k n -> p (k n)"),
                                       tr[:, k, 0:n], ACT.Copy).then_inc(s_nh, 1)

            act.wait_ge(s_const, 1)
            act.activation(stat[:, 0, 0, 0:1], ones[:, 0:1], ACT.Sqrt)
            with act.Fori(0, KT // DEPTH) as i:
                for k in range(DEPTH):
                    act.wait_ge(s_xt, DEPTH * i + (k + 1))
                    squares(x0T, DEPTH * i + k, DEPTH * i + (k + 1), tr, k, 0, L)
            for k in range(DEPTH - 1):
                hi_unit(act, 0, k)
            norm_root(0, L)
            norm_hi(0, L)
            hi_unit(act, 0, DEPTH - 1)
            act.dma_start(rows[:, 0, :], lam_re[0].rearrange("d (q g) n -> (d q) (g n)", g=2)).then_inc(s_par, 16)
            act.dma_start(rows[:, 1, :], lam_im[0].rearrange("d (q g) n -> (d q) (g n)", g=2)).then_inc(s_par, 16)
            act.dma_start(lst[:, 0:2], log_step[0].rearrange("d (q g) -> (d q) g", g=2)).then_inc(s_par, 16)
            act.dma_start(drow[:, :], ssm_d[0].rearrange("(q c) -> q c", q=PAIRS)).then_inc(s_par, 16)
            for n in range(3):
                act.dma_start(crow[n % 2 * FT:(n % 2 + 1) * FT, n // 2, :],
                              conv_w[0, n].rearrange("(k p) -> k p", p=P)).then_inc(s_par, 16)
            act.dma_start(crow[FT:2 * FT, 1, :], conv_b[0].rearrange("(k p) -> k p", p=P)).then_inc(s_par, 16)
            for r, b in enumerate((b_re, b_im)):
                for d in range(DIRS):
                    act.dma_start(braw[:, r, d * PAIRS:(d + 1) * PAIRS, :],
                                  b[0, d].rearrange("(q g) n c -> (g n) q c", g=2)).then_inc(s_par, 16)
            for r, c in enumerate((c_re, c_im)):
                for d in range(DIRS):
                    act.dma_start(cnat[:, d, :, r, :],
                                  c[0, d].rearrange("(k g) c n -> (g c) k n", k=KH)).then_inc(s_par, 16)

            act.wait_ge(s_spill, 16)
            with act.Fori(0, ITERS_IN) as i:
                for k in range(2):
                    for n in range(4):
                        hi_unit(act, (U_U + DEPTH) + 8 * i, 4 * k + n)
                    act.wait_ge(s_used, 8 * i + (U_U + 4 * (k + 1)))
                    for m in range(2):
                        for b in range(PB):
                            for j in range(CHUNK):
                                src = ps[32 * b:32 * b + 32, 2 * k + m, 0:L].rearrange("p (c j) -> p j c", j=CHUNK)
                                pair = i * (4 * PB) + ((2 * k + m) * PB + b)
                                last = act.activation(U[32 * j:32 * j + 32, ds(pair, 1), :].rearrange("p a c -> p (a c)"),
                                                      src[:, j, :], ACT.Copy)
                    last.then_inc(s_u, 1)

            v = lambda n: prm[:, n, :]
            act.wait_ge(s_pcp, 1)
            act.activation(v(3), v(2), ACT.Exp).then_inc(s_pa, 1)
            act.wait_ge(s_pcp, 2)
            act.activation(v(6), v(4), ACT.Exp).then_inc(s_pa, 1)
            act.wait_ge(s_pcp, 3)
            act.activation(v(8), v(7), ACT.Sin)
            act.activation(v(9), v(7), ACT.Sin, scale=0.5).then_inc(s_pa, 1)
            for d in range(DIRS):
                for q in range(2):
                    n = 2 * d + q
                    act.wait_ge(s_ctp, n + 1)
                    for h in range(2):
                        hs = slice(64 * h, 64 * h + 64)
                        for sl, part, sign in ((0, 0, 1.0), (1, 1, -1.0), (2, 0, -1.0)):
                            src = ps[64 * part:64 * part + 64, 4 + n, :].rearrange("p (q g c) -> p q g c", g=2, c=GROUP)
                            last = act.activation(CC[hs, d * PAIRS + 16 * q:d * PAIRS + 16 * (q + 1), sl, :],
                                                  src[:, :, h, :], ACT.Copy, scale=sign)
                    last.then_inc(s_ccp, 1)

            def v_copy(i, k, start):
                act.wait_ge(s_vtp, 2 * i + (k + 1 + SEED))
                if not start:
                    act.wait_ge(s_vst, 64 * i + 32 * k)
                b = 4 + 2 * (k % 2)
                act.activation(vst[:, 0:2, :], ps[:, b, :].rearrange("p (a b) -> p a b", a=2), ACT.Copy)
                act.activation(vst[0:N_META, 2, :], ps[0:N_META, b + 1, 0:CB], ACT.Copy)
                act.activation(vm[:, ds(4 * i + 2 * k, 2), :].rearrange("p a b -> p (a b)"),
                               ps[0:N_META, b, 0:CB], ACT.Copy).then_inc(s_vcp, 1)
                act.wait_ge(s_vcp, 2 * i + (k + 1 + SEED))
                col = i * (2 * CB) + k * CB
                act.dma_start(v_d[0:2 * P, ds(col, CB)].rearrange("(k p) c -> p k c", p=P),
                              vst[:, 0:2, :]).then_inc(s_vst, 16)
                act.dma_start(v_d[2 * P:L, ds(col, CB)], vst[0:N_META, 2, :]).then_inc(s_vst, 16)

            def v_blocks(i, start):
                for k in range(2):
                    for n in range(4):
                        hi_unit(act, (U_V + DEPTH) + 8 * i, 4 * k + n)
                    act.wait_ge(s_used, 8 * i + (U_V + 4 * (k + 1)))
                    act.wait_ge(s_vtp, 2 * i + (k - 1 + SEED))
                    act.activation(stg[:, k, :, :], ps[:, 2 * k:2 * k + 2, 0:L], ACT.Copy).then_inc(s_vtd, 1)
                    if k or not start:
                        v_copy(i, k - 1, start)

            v_blocks(0, True)
            with act.Fori(1, ITERS_IN) as i:
                v_blocks(i, False)
            v_copy(ITERS_IN - 1, 1, False)

            def store_block(i, k, n, before, dst, meta, width):
                act.activation(stg[:, k, :, 0:n], ps[:, 2 * k:2 * k + 2, 0:n], ACT.Copy)
                act.activation(meta[:, ds(4 * i + 2 * k, 2), :], ps[:, 2 * k:2 * k + 2, 0:width], ACT.Copy).then_inc(s_kev, 1)
                act.wait_ge(s_kev, 2 * i + (before + k + 1 + SEED))
                for m in range(2):
                    act.dma_start(dst[ds(4 * i + (2 * k + m), 1), :, :].rearrange("b p t -> p (b t)"),
                                  stg[:, k, m, 0:n]).then_inc(s_kst, 16)

            def wt_copy(p, k):
                act.wait_ge(s_wtp, p + (k + 1 + SEED))
                act.wait_ge(s_sps, p + (k - 1 + SEED))
                act.activation(WT[:, k % 2, :, :].rearrange("p a b -> p (a b)"), ps[:, 4 + k % 2, :], ACT.Copy)\
                   .then_inc(s_wts, 1)

            def k_blocks(i, start):
                for k in range(8):
                    wt_copy(16 * i, 2 * k)
                    wt_copy(16 * i, 2 * k + 1)
                    hi_unit(act, (U_K + DEPTH) + 8 * i, k)
                    if k % 4 == 3:
                        act.wait_ge(s_used, 8 * i + (U_K + k + 1))
                        act.wait_ge(s_vtp, 4 + SEED)
                        if not start:
                            act.wait_ge(s_kst, 64 * i)
                        store_block(i, k // 4, L, 0, k_d, km, N_META)

            k_blocks(0, True)
            with act.Fori(1, ITERS_IN) as i:
                k_blocks(i, False)
            with act.Fori(0, ITERS_IN) as i:
                for k in range(2):
                    for n in range(4):
                        hi_unit(act, (U_Q + DEPTH) + 8 * i, 4 * k + n)
                    act.wait_ge(s_used, 8 * i + (U_Q + 4 * (k + 1)))
                    act.wait_ge(s_kst, 64 * i + 128)
                    store_block(i, k, NL, 4, q_d, qm, 2)

            def gate_block(gate, f, base_u, used, banks):
                act.wait_ge(s_used, base_u + used)
                act.activation(gate[:, ds(f, 2), :], ps[:, banks:banks + 2, 0:NL], ACT.Copy).then_inc(s_g, 1)

            with act.Fori(0, G_SCAN // 2) as i:
                for k in range(2):
                    for n in range(4):
                        hi_unit(act, (U_G + DEPTH) + 8 * i, 4 * k + n)
                    if k == 0:
                        act.wait_ge(s_ssb, PAIRS + SEED)
                    gate_block(gate_na, 4 * i + 2 * k, 8 * i, U_G + 4 * (k + 1), 2 * k)

            def b_copy(p, k):
                for h in range(2):
                    hs = slice(64 * h, 64 * h + 64)
                    src = BB[hs, :, 1:3, :].rearrange("p (d q) r c -> p d q r c", d=DIRS)[:, :, ds(p + k, 1), :, :]
                    last = act.activation(Bm[hs, k % GSLOTS, :, :, GROUP * h:GROUP * (h + 1)],
                                          src.rearrange("p d q r c -> p d (q r) c"), ACT.Copy)
                last.then_inc(s_bb, 1)

            act.wait_ge(s_bz, 1)
            for k in range(GSLOTS):
                b_copy(0, k)
            act.wait_ge(s_m2, 1)
            act.activation(sm[:, :, :, :], sm[:, :, :, :], ACT.Exp).then_inc(s_m3, 1)
            def tm_copy(p, k):
                act.wait_ge(s_kps, p + (k + 1))
                act.wait_ge(s_yps, p + (k - 1 + SEED))
                for j in range(CHUNK):
                    lo = (CHUNK - 1 - j) * 2 * GROUP
                    last = act.activation(Tm[32 * j:32 * j + 32, k % 2, :], ps[0:32, 4 + k % 2, lo:lo + P], ACT.Copy)
                last.then_inc(s_tm, 1)

            def act_copy(dst, src):
                return act.activation(dst, src, ACT.Copy)

            def tm_block(i, last):
                for k in range(4):
                    for n in range(PPU * k, PPU * (k + 1), 2):
                        for pair in (n, n + 1):
                            tm_copy(4 * PPU * i, pair)
                            if not (last and pair >= 4 * PPU - GSLOTS):
                                b_copy(4 * PPU * i, pair + GSLOTS)
                        for pair in (n, n + 1):
                            y_copy(act_copy, act, 4 * PPU * i, 4 * PPU // PB * i, pair, 1, s_ysa)
                    hi_unit(act, (U_G + DEPTH + 4 * G_SCAN) + 4 * i, k)
                gate_block(gate_na, 2 * i + 2 * G_SCAN, 4 * i, U_G + 4 * G_SCAN + 4, 0)

            with act.Fori(0, G_SSM - 1) as i:
                tm_block(i, False)
            tm_block(G_SSM - 1, True)

            def att_load(b, j):
                act.dma_start(qs[:, j, :], q_d[ds(b, 1), :, :].rearrange("b p t -> p (b t)")).then_inc(s_qkv[j], 16)
                act.dma_start(ks[:, j, :], k_d[ds(b, 1), :, :].rearrange("b p t -> p (b t)")).then_inc(s_qkv[j], 16)
                act.dma_start(vs[:, j, 0:2, :],
                              v_d[0:2 * P, ds(b * P, P)].rearrange("(k p) c -> p k c", p=P)).then_inc(s_qkv[j], 16)
                act.dma_start(vs[0:N_META, j, 2, :], v_d[2 * P:L, ds(b * P, P)]).then_inc(s_qkv[j], 16)
                for hh in range(2):
                    for r in range(QROWS):
                        row = b * (2 * DROWS) + (hh * DROWS + GRID_ROWS - 1 - QROWS - r)
                        act.dma_start(bi[GRID_W * r:GRID_W * (r + 1), 2 * j + hh, :, :], skew_d[:, ds(row, EWIN), :])\
                           .then_inc(s_bl[2 * j + hh], 16)

            def att_exp(i, k):
                act.wait_ge(s_nm, 4 * i + (k + 1 + SEED))
                for t in range(2):
                    last = act.activation(S[:, k % 2, t, :], S[:, k % 2, t, :], ACT.Exp,
                                          bias=stat[:, k, 0, t:t + 1], accum_out=stat[:, k, 1, t:t + 1])
                last.then_inc(s_e, 1)

            def att_pt(i, k):
                act.wait_ge(s_ptps, 4 * i + (k + 1 + SEED))
                act.wait_ge(s_pv, 4 * i + (k - 1 + SEED))
                act.activation(PT[:, k % 2, :], ps[:, 4, :], ACT.Copy)
                two = ps[0:N_META, 2 * (k % 2):2 * (k % 2) + 2, L:L + P]
                act.activation(PT2[:, k % 2, :].rearrange("p (t q) -> p t q", t=2), two, ACT.Copy).then_inc(s_ptsb, 1)

            def att_hi(i, j):
                act.wait_ge(s_pv, 4 * i + (2 * (j + 1) + SEED))
                act.activation(anh[:, ds(2 * i + j, 1), 2:NL].rearrange("p k n -> p (k n)"),
                               ps[:, 5, 0:SEQ], ACT.Copy).then_inc(s_ah, 1)

            att_u = U_G + 4 * (G_SCAN + G_SSM)
            def att_iteration(i, start, last):
                for k in range(4):
                    att_exp(i, k)
                    if start and k == 0:
                        att_load(1, 1)
                    hi_unit(act, (att_u + DEPTH) + 8 * i, 2 * k)
                    if k % 2 == 0 and (k or not start):
                        att_hi(i, k // 2 - 1)
                        if not (last and k):
                            att_load(2 * i + (k // 2 + 1), (k // 2 + 1) % 2)
                    hi_unit(act, (att_u + DEPTH) + 8 * i, 2 * k + 1)
                    if k % 2 == 1:
                        gate_block(gate_ssm, 4 * i + (k - 1), 8 * i, att_u + 2 * (k + 1), 6)
                    att_pt(i, k)

            act.wait_ge(s_pad3, 16 * GRID_W)
            act.wait_ge(s_kst, 16 * 16)
            act.wait_ge(s_vst, 16 * 8)
            act.wait_ge(s_ysb, PAIRS + SEED)
            att_load(0, 0)
            act.drain()
            act.activation(yT[:, :, LIVE:L], yT[:, :, LIVE:L], ACT.Gelu_apprx_tanh)
            act.drain()
            act.activation(ygh[:, :, :], yT[:, :, LIVE:L], ACT.Copy).then_inc(s_ygh, 1)
            att_iteration(0, True, False)
            with act.Fori(1, HEADS // 4 - 1) as i:
                att_iteration(i, False, False)
            att_iteration(HEADS // 4 - 1, False, True)
            att_hi(HEADS // 4 - 1, 1)
            act.wait_ge(s_m5, 1)
            act.activation(ptm[:, :], ps[0:N_META, 2, 0:2 * HEADS], ACT.Copy).then_inc(s_m6, 1)
            for q in range(2):
                for n in range(4):
                    hi_unit(act, U_GLU + DEPTH, 4 * q + n)
                    if 4 * q + n == 1:
                        act.wait_ge(s_m7, 1)
                        act.activation(anh[:, :, 0:2], ps[:, 3, 0:2 * KH].rearrange("p (b t) -> p b t", t=2), ACT.Copy)\
                           .then_inc(s_m8, 1)
                    if q:
                        gate = (gate_na, gate_ssm)[n % 2][:, KT // 2 * (n // 2):KT // 2 * (n // 2 + 1), :]
                        act.activation(gate, gate, ACT.Sigmoid).then_inc(s_gs, 1)
                act.wait_ge(s_used, U_GLU + 4 * (q + 1))
                if q:
                    act.wait_ge(s_z, 4)
                else:
                    act.wait_ge(s_g, 16 + SEED)
                for m in range(4):
                    act.activation(gt[:, m, :], ps[:, 4 * q + m, 0:NL], ACT.Sigmoid).then_inc(s_sg, 1)
                for m in range(4):
                    act.wait_ge(s_z, 4 * q + m + 1)
                    act.activation(zh[:, 4 * q + m, :], mt[:, m, :], ACT.Copy).then_inc(s_zh, 1)

            with act.Fori(0, 4) as i:
                for k in range(2):
                    for n in range(4):
                        hi_unit(act, (U_PROJ + DEPTH) + 8 * i, 4 * k + n)
                    for m in range(2):
                        act.wait_ge(s_mx, 4 * i + (2 * k + m + 1) + SEED)
                        act.activation(hnh[:, ds(4 * i + (2 * k + m), 1), 0:NL].rearrange("p k n -> p (k n)"),
                                       mt[:, 2 * k + m, :], ACT.Copy).then_inc(s_mh, 1)
            act.wait_ge(s_mx, KT + SEED)
            act.dma_start(xT[:, :, :].rearrange("p k t -> p (k t)"), xT_d).then_inc(s_xre, 16)
            with act.Fori(0, 4) as i:
                for k in range(2):
                    for n in range(4):
                        hi_unit(act, (U_OUT + DEPTH) + 8 * i, 4 * k + n)
                    act.wait_ge(s_h1, 2 * i + (k + 1 + SEED))
                    for m in range(2):
                        tile = 4 * i + (2 * k + m)
                        squares(xT, tile, tile + (KT + 1), sq, m, LIVE, NL)
            norm_root(1, NL)
            norm_hi(1, NL)

            with act.Fori(0, FT // 4) as i:
                for k in range(2):
                    for n in range(4):
                        hi_unit(act, (U_UP + DEPTH) + 16 * i, 8 * k + n)
                    act.wait_ge(s_used, 16 * i + (U_UP + 8 * k + 4))
                    if k == 0:
                        act.wait_ge(s_ge, 4 * i + SEED)
                    for m in range(2):
                        f = 4 * i + (2 * k + m)
                        act.activation(cv[:, k, m, :], ps[:, 4 * k + m, 2:NL], ACT.Identity,
                                       scale=cvw[:, ds(f + FT, 1)], bias=cvw[:, ds(f + 3 * FT, 1)]).then_inc(s_c, 1)
                    for n in range(4, 8):
                        hi_unit(act, (U_UP + DEPTH) + 16 * i, 8 * k + n)
                    if k == 0:
                        act.wait_ge(s_fl, 4 * i + SEED)
                    for m in range(2):
                        act.wait_ge(s_cd, 4 * i + (2 * k + m + 1))
                        act.activation(ge[:, k, m, :], cv[:, k, m, :], ACT.Gelu_apprx_tanh).then_inc(s_ge, 1)
                    for m in range(2):
                        act.wait_ge(s_fm, 4 * i + (2 * k + m + 1) + SEED)
                        act.activation(ah[:, ds(4 * i + (2 * k + m), 1), :].rearrange("p k n -> p (k n)"),
                                       ge[:, k, m, :], ACT.Copy).then_inc(s_fh, 1)
            act.wait_ge(s_fl, FT + SEED)
            act.dma_start(grep[:, :], final_g.rearrange("(a n) -> a n", a=1).to_broadcast([P, D_MODEL])).then_inc(s_fg, 16)
            split_loop(act, hi_unit, U_DOWN, FT // 2 - 1, 4)
            for n in range(KT // 2):
                act.wait_ge(s_ot, n + 1)
                act.activation(sqt[:, n % 2, :], ps[:, n, :], ACT.Square, accum_out=fin[:, 0, n:n + 1]).then_inc(s_sum, 1)
                act.drain()
            act.wait_ge(s_var, 3)
            act.activation(fin[:, 1, 4:6], fin[:, 1, 2:4], ACT.Sqrt).then_inc(s_sd, 1)
            act.wait_ge(s_rs, 1)
            act.activation(otok[:, 1, :], otok[:, 1, :], ACT.Copy, scale=fin[:, 1, 7:8]).then_inc(s_oc1, 1)

        @block.vector
        def _(dve):
            for seeded in (s_nm, s_al, s_mx, s_h1, s_fm, s_fl, s_ssb, s_ysb):
                dve.sem_inc(seeded, SEED)
            for k in range(KT):
                dve.wait_ge(s_xtp, k + 1)
                dve.tensor_copy(x0T[:, k, :], ps[:, k % 4, 0:L]).then_inc(s_xt, 1)
            def norm(which, lo, n):
                dve.wait_ge(s_ss, which + 1)
                dve.tensor_scalar(rstd[:, 0:n], ps[:, 6, 0:n], 1.0 / D_MODEL, EPS, ALU.mult, ALU.add).then_inc(s_var, 1)
                if which == 0:
                    dve.wait_ge(s_gtp, 1)
                    dve.tensor_copy(gains[:, :], ps[:, 7, 0:2 * KT]).then_inc(s_gcp, 1)
                dve.wait_ge(s_sd, which + 1)
                dve.reciprocal(rstd[:, 0:n], rstd[:, 0:n])
                dve.drain()
                src = xT if which else x0T
                if which < 2:
                    with dve.Fori(0, KT // DEPTH) as i:
                        for k in range(DEPTH):
                            dve.wait_ge(s_nl, DEPTH * i + (KT * which + SEED))
                            dve.scalar_tensor_tensor(
                                out=tr[:, k, 0:n], in0=src[:, ds(DEPTH * i + k, 1), lo:lo + n].rearrange("p k n -> p (k n)"),
                                scalar=gains[:, ds(DEPTH * i + (KT * which + k), 1)], in1=rstd[:, 0:n],
                                op0=ALU.mult, op1=ALU.mult).then_inc(s_nt, 1)

            norm(0, 0, L)

            dve.wait_ge(s_par, 16 * 16)
            dve.tensor_copy(rows[:, 2, :].rearrange("p (g n) -> p g n", g=2),
                            lst[:, 0:2].unsqueeze(2).to_broadcast([DIRS * PAIRS, 2, STATE])).then_inc(s_rows, 1)
            dve.wait_ge(s_ptp, 1)
            dve.tensor_copy(cvw[:, :], ps[:, 7, 48:48 + 4 * FT])
            full = [2 * GROUP, PAIRS, 2 * GROUP]
            dve.memset(dD[:, :, :], 0.0)
            dve.drain()
            dve.tensor_tensor(dD[0:2 * GROUP, :, :], ident[0:2 * GROUP, 0:2 * GROUP].unsqueeze(1).to_broadcast(full),
                              ps[0:2 * GROUP, 7, 416:448].unsqueeze(2).to_broadcast(full), ALU.mult)
            dve.tensor_copy(prm[:, 0:3, :], ps[:, 7, 224:416].rearrange("p (a b) -> p a b", a=3)).then_inc(s_pcp, 1)
            dve.drain()

            v = lambda n: prm[:, n, :]

            def mul(o, a, b):
                dve.tensor_tensor(o, a, b, ALU.mult)

            def cmul(o, a, b, t):
                mul(t[0], a[0], b[0])
                mul(t[1], a[1], b[1])
                mul(t[2], a[0], b[1])
                mul(t[3], a[1], b[0])
                dve.drain()
                dve.tensor_tensor(o[0], t[0], t[1], ALU.subtract)
                dve.tensor_tensor(o[1], t[2], t[3], ALU.add)
                dve.drain()

            dve.wait_ge(s_pa, 1)
            mul(v(4), v(0), v(3))
            mul(v(5), v(1), v(3))
            dve.drain()
            dve.tensor_scalar(v(10), v(5), 1.0 / (2 * math.pi), ROUND, ALU.mult, ALU.add).then_inc(s_pcp, 1)
            dve.drain()
            dve.tensor_scalar(v(10), v(10), ROUND, None, ALU.subtract)
            for c in (TWO_PI_HI, TWO_PI_MID, TWO_PI_LO):
                dve.drain()
                dve.scalar_tensor_tensor(out=v(5), in0=v(10), scalar=-c, in1=v(5), op0=ALU.mult, op1=ALU.add)
            dve.drain()
            dve.tensor_scalar(v(7), v(5), PI_BELOW, -PI_BELOW, ALU.min, ALU.max).then_inc(s_pcp, 1)
            dve.wait_ge(s_pa, 3)
            mul(v(10), v(9), v(9))
            dve.drain()
            dve.tensor_scalar(v(10), v(10), -2.0, 1.0, ALU.mult, ALU.add)
            dve.memset(pw[:, 0, 0, :], 1.0)
            dve.memset(pw[:, 0, 1, :], 0.0)
            dve.drain()
            a1 = (pw[:, 1, 0, :], pw[:, 1, 1, :])
            a2 = (pw[:, 2, 0, :], pw[:, 2, 1, :])
            tmp = [v(n) for n in (11, 12, 13, 14)]
            mul(a1[0], v(6), v(10))
            mul(a1[1], v(6), v(8))
            dve.drain()
            cmul(a2, a1, a1, tmp)
            cmul((pw[:, 3, 0, :], pw[:, 3, 1, :]), a2, a1, tmp)
            cmul((pw[:, 4, 0, :], pw[:, 4, 1, :]), a2, a2, tmp)
            dve.tensor_scalar(v(15), a1[0], 1.0, None, ALU.subtract)
            mul(v(16), v(0), v(0))
            mul(v(17), v(1), v(1))
            dve.drain()
            dve.tensor_tensor(v(16), v(16), v(17), ALU.add)
            mul(v(18), v(15), v(0))
            mul(v(19), a1[1], v(1))
            mul(v(20), a1[1], v(0))
            mul(v(21), v(15), v(1))
            dve.drain()
            dve.reciprocal(v(16), v(16))
            dve.tensor_tensor(v(18), v(18), v(19), ALU.add)
            dve.tensor_tensor(v(20), v(20), v(21), ALU.subtract)
            dve.drain()
            mul(v(18), v(18), v(16))
            mul(v(20), v(20), v(16))
            dve.drain()
            full = [P, DIRS * PAIRS, GROUP]
            qr = v(18).unsqueeze(2).to_broadcast(full)
            qi = v(20).unsqueeze(2).to_broadcast(full)
            ta = btmp[:, 0, :].rearrange("p (a b) -> p a b", b=GROUP)
            tb = btmp[:, 1, :].rearrange("p (a b) -> p a b", b=GROUP)
            mul(ta, qr, braw[:, 0, :, :])
            mul(tb, qi, braw[:, 1, :, :])
            dve.drain()
            dve.tensor_tensor(BB[:, :, 1, :], ta, tb, ALU.subtract)
            dve.drain()
            mul(ta, qr, braw[:, 1, :, :])
            mul(tb, qi, braw[:, 0, :, :])
            dve.drain()
            dve.tensor_tensor(BB[:, :, 2, :], ta, tb, ALU.add)
            dve.drain()
            dve.tensor_scalar(BB[:, :, 0, :], BB[:, :, 2, :], -1.0, None, ALU.mult)
            for d in range(DIRS):
                dq = slice(d * PAIRS, (d + 1) * PAIRS)
                kin = pw[:, 0:CHUNK, :, dq] if d else pw[:, CHUNK - 1::-1, :, dq]
                kout = pw[:, CHUNK::-1, :, dq] if d else pw[:, :, :, dq]
                for r in range(2):
                    dve.tensor_copy(pwW[:, dq, r, :], kin[:, :, r, :].rearrange("p k q -> p q k"))
                    dve.tensor_copy(pwG[:, dq, r, :], kout[:, :, r, :].rearrange("p k q -> p q k"))
            a4r = pw[:, CHUNK, 0, :].rearrange("p (d q) -> p d q", d=DIRS)
            a4i = pw[:, CHUNK, 1, :].rearrange("p (d q) -> p d q", d=DIRS)
            for r in range(2):
                dve.tensor_copy(A4R[:, :, r, :], a4r)
            dve.tensor_copy(A4I[:, :, 0, :], a4i)
            dve.tensor_scalar(A4I[:, :, 1, :], a4i, -1.0, None, ALU.mult)
            dve.drain()
            dve.nop().then_inc(s_pd, 1)

            dve.memset(X[:, 0, :, :], 0.0)

            def w_fwd(p, k):
                dve.wait_ge(s_wtp, p + (k - WSLOTS + 2 + SEED))
                w_make(dve, p + k, k % WSLOTS, 0, t1v, t2v).then_inc(s_wd, 2)
                dve.drain()

            def s_copy(p, k):
                dve.wait_ge(s_sps, p + (k + 1 + SEED))
                dst = X[:, 1:NCH + 1, :, ds(p + k, 1)].rearrange("p c r q -> p (r q) c")
                src = ps[:, 6 + k % 2, 0:4 * NCH].rearrange("p (r c) -> p r c", c=NCH)
                dve.tensor_copy(dst[:, 0:2, :], src[:, 0:2, :])
                dve.tensor_copy(dst[:, 2:4, :], src[:, 2:4, ::-1]).then_inc(s_ssb, 1)

            dve.wait_ge(s_bz, 1)
            w_fwd(0, 0)
            w_fwd(0, 2)
            def in_block(i, last):
                for k in range(0, 8, 2):
                    s_copy(8 * i, k)
                    s_copy(8 * i, k + 1)
                    if not (last and k >= 8 - WSLOTS):
                        w_fwd(8 * i, k + WSLOTS)
                    lo_unit(dve, (U_K + DEPTH) + 4 * i, k // 2)

            dve.wait_ge(s_lo, U_K + DEPTH)
            with dve.Fori(0, PAIRS // 8 - 1) as i:
                in_block(i, False)
            in_block(PAIRS // 8 - 1, True)
            dve.drain()

            a_re = A4R[:, :, :, :].rearrange("p d r q -> p (d r q)")
            a_im = A4I[:, :, :, :].rearrange("p d r q -> p (d r q)")
            swapped = sc2[:, :].rearrange("p (d r q) -> p d r q", d=DIRS, r=2)[:, :, ::-1, :]

            def scan_step(c):
                here = X[:, ds(c, 1), :, :].rearrange("p c r q -> p (c r q)")
                after = X[:, ds(c + 1, 1), :, :].rearrange("p c r q -> p (c r q)")
                after4 = X[:, ds(c + 1, 1), :, :].rearrange("p c (d r) q -> p (c d) r q", d=DIRS)
                mul(sc1[:, :], here, a_re)
                mul(sc2[:, :], here, a_im)
                dve.drain()
                dve.tensor_tensor(after, after, sc1[:, :], ALU.add)
                dve.drain()
                dve.tensor_tensor(after4, after4, swapped, ALU.add)
                dve.drain()

            for c in range((NCH - 1) % SCAN_STEPS):
                scan_step(c)
            with dve.Fori(0, (NCH - 1) // SCAN_STEPS) as i:
                for c in range(SCAN_STEPS):
                    scan_step(SCAN_STEPS * i + (c + (NCH - 1) % SCAN_STEPS))
            dve.nop().then_inc(s_scan, 1)

            def g_fwd(p, k):
                dve.wait_ge(s_yps, p + (k - GSLOTS + 2 + SEED))
                g_make(dve, p + k, k % GSLOTS, 0, t1v, t2v).then_inc(s_gd, 2)
                dve.drain()

            dve.wait_ge(s_bz, 2)
            for k in range(0, GSLOTS, 2):
                g_fwd(0, k)
            dve.wait_ge(s_m1, 1)
            smf = sm[:, :, :, :].rearrange("p a b c -> p a (b c)")
            sm3 = sm[:, :, :, :].rearrange("p a b c -> p (a b) c")
            dve.tensor_scalar(smf, ps[0:2, 2:4, 0:P], SCALE, None, ALU.mult)
            dve.drain()
            dve.reduce_max(smx[:, 0, :], sm3, AX.X)
            dve.drain()
            dve.tensor_tensor(sm3, sm3, smx[:, 0, :].unsqueeze(2).to_broadcast([2, HEADS, N_META]), ALU.subtract)\
               .then_inc(s_m2, 1)
            dve.wait_ge(s_m3, 1)
            dve.reduce_sum(smx[:, 1, :], sm3, AX.X)
            dve.drain()
            dve.reciprocal(smx[:, 1, :], smx[:, 1, :])
            dve.drain()
            dve.tensor_tensor(sm3, sm3, smx[:, 1, :].unsqueeze(2).to_broadcast([2, HEADS, N_META]), ALU.mult)\
               .then_inc(s_m4, 1)
            def out_block(i, last):
                for k in range(0, 4 * PPU, 2):
                    for n in (k, k + 1):
                        y_copy(dve.tensor_copy, dve, 4 * PPU * i, 4 * PPU // PB * i, n, 0, s_ysb)
                    if not (last and k >= 4 * PPU - GSLOTS):
                        g_fwd(4 * PPU * i, k + GSLOTS)
                    if k % PPU == PPU - 2:
                        lo_unit(dve, (U_G + DEPTH + 4 * G_SCAN) + 4 * i, k // PPU)

            dve.wait_ge(s_lo, U_G + DEPTH + 4 * G_SCAN)
            with dve.Fori(0, G_SSM - 1) as i:
                out_block(i, False)
            out_block(G_SSM - 1, True)

            def att_scores(i, k):
                dve.wait_ge(s_qk, 4 * i + (k + 1))
                dve.wait_ge(s_bm, 4 * i + (k + 1))
                dve.wait_ge(s_ptps, 4 * i + (k - 1 + SEED))
                bank = 2 * (k % 2)
                for t in range(2):
                    e0 = QROWS * (1 - t)
                    dve.scalar_tensor_tensor(
                        out=S[:, k % 2, t, N_META:L], in0=ps[:, bank + t, N_META:L], scalar=SCALE,
                        in1=bi[:, k, e0:e0 + GRID_ROWS, :].rearrange("p a b -> p (a b)"), op0=ALU.mult, op1=ALU.add)
                dve.tensor_scalar(S[:, k % 2, :, 0:N_META], ps[:, bank:bank + 2, 0:N_META], SCALE, None, ALU.mult)
                dve.drain()
                dve.reduce_max(stat[:, k, 0, :], S[:, k % 2, :, :], AX.X)
                dve.drain()
                dve.tensor_scalar(stat[:, k, 0, :], stat[:, k, 0, :], -1.0, None, ALU.mult).then_inc(s_nm, 1)

            def att_norm(i, k):
                dve.wait_ge(s_e, 4 * i + (k + 1))
                dve.reciprocal(stat[:, k, 1, :], stat[:, k, 1, :])
                dve.drain()
                for t in range(2):
                    last = dve.tensor_scalar(S[:, k % 2, t, :], S[:, k % 2, t, :], stat[:, k, 1, t:t + 1], None, ALU.mult)
                last.then_inc(s_p, 1)

            def att_lo(i, j):
                dve.wait_ge(s_ah, 2 * i + (j + 1))
                dve.tensor_tensor(anl[:, ds(2 * i + j, 1), 2:NL].rearrange("p k n -> p (k n)"),
                                  ps[:, 5, 0:SEQ],
                                  anh[:, ds(2 * i + j, 1), 2:NL].rearrange("p k n -> p (k n)").bitcast(F),
                                  ALU.subtract).then_inc(s_al, 1)

            def att_iteration(i, start):
                for k in range(4):
                    att_scores(i, k)
                    if start and k == 0:
                        dve.wait_ge(s_ysa, PAIRS + SEED)
                        dve.wait_ge(s_ygh, 1)
                        dve.tensor_tensor(ygl[:, :, :], yT[:, :, LIVE:L], ygh[:, :, :].bitcast(F), ALU.subtract).then_inc(s_ygl, 1)
                    att_norm(i, k)
                    if k % 2 == 0 and (k or not start):
                        att_lo(i, k // 2 - 1)

            att_iteration(0, True)
            with dve.Fori(1, G_ATT // 2) as i:
                att_iteration(i, False)
            att_lo(HEADS // 4 - 1, 1)

            dve.wait_ge(s_m8, 1)
            dve.tensor_tensor(anl[:, :, 0:2], ps[:, 3, 0:2 * KH].rearrange("p (b t) -> p b t", t=2),
                              anh[:, :, 0:2].bitcast(F), ALU.subtract).then_inc(s_mal, 1)

            for n in range(KH):
                dve.wait_ge(s_sg, n + 1)
                if n >= 4:
                    dve.wait_ge(s_zl, n - 3)
                dve.tensor_tensor(mt[:, n % 4, :], yT[:, n, LIVE:L], gt[:, n % 4, :], ALU.mult).then_inc(s_z, 1)
                if n % 4 == 3:
                    for m in range(n - 3, n + 1):
                        dve.wait_ge(s_zh, m + 1)
                        dve.tensor_tensor(zl[:, m, :], mt[:, m % 4, :], zh[:, m, :].bitcast(F), ALU.subtract).then_inc(s_zl, 1)

            dve.wait_ge(s_gs, 4)
            dve.wait_ge(s_zl, KH)
            with dve.Fori(0, 4) as i:
                for k in range(2):
                    dve.wait_ge(s_used, 8 * i + (U_PROJ + 4 * (k + 1)))
                    for m in range(2):
                        f = 4 * i + (2 * k + m)
                        dve.tensor_tensor(mt[:, 2 * k + m, :], ps[:, 4 * k + m, 0:NL],
                                          gate_na[:, ds(f, 1), :].rearrange("p k n -> p (k n)"), ALU.mult)
                        dve.tensor_tensor(gt[:, 2 * k + m, :], ps[:, 4 * k + 2 + m, 0:NL],
                                          gate_ssm[:, ds(f, 1), :].rearrange("p k n -> p (k n)"), ALU.mult)
                    dve.drain()
                    for m in range(2):
                        dve.tensor_tensor(mt[:, 2 * k + m, :], mt[:, 2 * k + m, :], gt[:, 2 * k + m, :], ALU.add).then_inc(s_mx, 1)
                    for m in range(2):
                        f = 4 * i + (2 * k + m)
                        dve.wait_ge(s_mh, f + 1)
                        dve.tensor_tensor(hnl[:, ds(f, 1), 0:NL].rearrange("p k n -> p (k n)"), mt[:, 2 * k + m, :],
                                          hnh[:, ds(f, 1), 0:NL].rearrange("p k n -> p (k n)").bitcast(F),
                                          ALU.subtract).then_inc(s_ml, 1)

            dve.wait_ge(s_xre, 16)
            with dve.Fori(0, 4) as i:
                for k in range(2):
                    dve.wait_ge(s_used, 8 * i + (U_OUT + 4 * (k + 1)))
                    for m in range(2):
                        h = xT[:, ds(4 * i + (2 * k + m), 1), LIVE:L].rearrange("p k n -> p (k n)")
                        last = dve.tensor_tensor(h, h, ps[:, 2 * k + m, 0:NL], ALU.add)
                    last.then_inc(s_h1, 1)
            norm(1, LIVE, NL)

            with dve.Fori(0, FT // 4) as i:
                for k in range(2):
                    for m in range(2):
                        f = 4 * i + (2 * k + m)
                        dve.wait_ge(s_c, f + 1)
                        c = cv[:, k, m, :]
                        dve.scalar_tensor_tensor(out=c, in0=ps[:, 4 * k + m, 1:NL - 1], scalar=cvw[:, ds(f, 1)], in1=c,
                                                 op0=ALU.mult, op1=ALU.add)
                        dve.drain()
                        dve.scalar_tensor_tensor(out=cv[:, k, m, 0:SEQ - 1], in0=ps[:, 4 * k + m, 3:NL],
                                                 scalar=cvw[:, ds(f + 2 * FT, 1)], in1=cv[:, k, m, 0:SEQ - 1],
                                                 op0=ALU.mult, op1=ALU.add).then_inc(s_cd, 1)
                    dve.wait_ge(s_used, 16 * i + (U_UP + 8 * (k + 1)))
                    for m in range(2):
                        dve.wait_ge(s_ge, 4 * i + (2 * k + m + 1) + SEED)
                        dve.tensor_tensor(ge[:, k, m, :], ge[:, k, m, :], ps[:, 4 * k + 2 + m, 0:SEQ], ALU.mult)\
                           .then_inc(s_fm, 1)
                    for m in range(2):
                        f = 4 * i + (2 * k + m)
                        dve.wait_ge(s_fh, f + 1)
                        dve.tensor_tensor(al[:, ds(f, 1), :].rearrange("p k n -> p (k n)"), ge[:, k, m, :],
                                          ah[:, ds(f, 1), :].rearrange("p k n -> p (k n)").bitcast(F),
                                          ALU.subtract).then_inc(s_fl, 1)

            for m in range(0, KT, 2):
                dve.wait_ge(s_used, U_END - 1 if m < KH else U_END)
                h = xT[:, m:m + 2, N_META:L]
                dve.tensor_tensor(h, h, ps[:, m // 2, :].rearrange("p (a b) -> p a b", a=2), ALU.add).then_inc(s_h2, 1)
            dve.wait_ge(s_fg, 16)
            for n in range(KT // 2):
                dve.wait_ge(s_ot, n + 1)
                dve.wait_ge(s_sum, n + 1)
                g, t = n // 2, n % 2
                dve.tensor_tensor(otok[:, t, 512 * g:512 * (g + 1)], ps[:, n, :], grep[:, 512 * g:512 * (g + 1)],
                                  ALU.mult)
            dve.drain()
            dve.reduce_sum(fin[:, 1, 0:2], fin[:, 0, :].rearrange("p (g t) -> p t g", t=2), AX.X)
            dve.drain()
            dve.tensor_scalar(fin[:, 1, 2:4], fin[:, 1, 0:2], 1.0 / D_MODEL, EPS, ALU.mult, ALU.add).then_inc(s_var, 1)
            dve.wait_ge(s_sd, 3)
            dve.reciprocal(fin[:, 1, 6:8], fin[:, 1, 4:6]).then_inc(s_rs, 1)
            dve.drain()
            dve.tensor_scalar(otok[:, 0, :], otok[:, 0, :], fin[:, 1, 6:7], None, ALU.mult).then_inc(s_oc, 1)

        @block.tensor
        def _(pe):
            for seeded in (s_pv, s_sq_used, s_vtp, s_ptps, s_wtp, s_sps, s_yps):
                pe.sem_inc(seeded, SEED)
            mm = nc.tensor.matmul

            def half_unit(base_u, k, q, units, m, xh, xl, lo, n, bank):
                if m == 0:
                    pe.wait_ge(s_lo, base_u + (k + 1))
                for t in range(UKT):
                    kt = q * UKT + t
                    cols = slice(t * CB + m * P, t * CB + (m + 1) * P)
                    o = ps[:, bank, 0:n]
                    mm(o, slot(whi, k)[:, cols], xh[:, kt, lo:lo + n], start=kt == 0, stop=False)
                    mm(o, slot(whi, k)[:, cols], xl[:, kt, lo:lo + n], start=False, stop=False)
                    ins = mm(o, slot(wlo, k)[:, cols], xh[:, kt, lo:lo + n], start=False, stop=kt == units * UKT - 1)
                if m == 1:
                    ins.then_inc(s_used, 1)

            def product(base_u, k0, units, xh, xl, lo, n, banks, split_before=None, split=s_nl):
                for q in range(units):
                    if split_before is not None:
                        pe.wait_ge(split, split_before + UKT * (q + 1))
                    for m in range(2):
                        half_unit(base_u, k0 + q, q, units, m, xh, xl, lo, n, banks[m])

            pe.wait_ge(s_const, 2)
            for k in range(KT):
                if k % KH == 0:
                    pe.wait_ge(s_x[k // KH], 64)
                if k >= 4:
                    pe.wait_ge(s_xt, k - 3)
                cs = slice(k * P, (k + 1) * P)
                nc.tensor.transpose(ps[:, k % 4, 0:P], xtok[:, 0, cs], ident[:, :])
                nc.tensor.transpose(ps[:, k % 4, P:2 * P], xtok[:, 1, cs], ident[:, :])
                nc.tensor.transpose(ps[:, k % 4, 2 * P:L], xtok[0:N_META, 2, cs], ident[0:N_META, 0:N_META]).then_inc(s_xtp, 1)
            def norm_sum(t, first, last, ring, k, n):
                pe.wait_ge(s_sq, t)
                mm(ps[:, 6, 0:n], ones[:, :], ring[:, k, 0:n], start=first, stop=last).then_inc(s_sq_used, 1)

            def norm_summed(which):
                pe.wait_ge(s_sq_used, KT * (which + 1) + SEED)
                pe.nop().then_inc(s_ss, 1)

            for k in range(KT):
                norm_sum(k + 1, k == 0, k == KT - 1, tr, k % DEPTH, L)
            norm_summed(0)
            pe.wait_ge(s_gain, 32)
            nc.tensor.transpose(ps[:, 7, 0:2 * KT], grow[:, :], ident[0:2 * KT, 0:2 * KT]).then_inc(s_gtp, 1)
            with pe.Fori(0, ITERS_IN) as i:
                for k in range(2):
                    pe.wait_ge(s_u, 2 * i + (k - 1 + SEED))
                    product(U_U + 8 * i, 4 * k, 4, hnh, hnl, 0, L, (2 * k, 2 * k + 1), SEED)
            pe.wait_ge(s_par, 16 * 16)
            pe.wait_ge(s_rows, 1)
            pe.wait_ge(s_gcp, 1)
            for n in range(2):
                nc.tensor.transpose(ps[:, 7, 48 + 88 * n:48 + 88 * (n + 1)], crow[:, n, :], ident[0:88, 0:88])
            for n in range(3):
                nc.tensor.transpose(ps[:, 7, 224 + 64 * n:224 + 64 * (n + 1)], rows[:, n, :], ident[0:64, 0:64])
            nc.tensor.transpose(ps[0:2 * GROUP, 7, 416:448], drow[:, :], ident[0:32, 0:32])\
              .then_inc(s_ptp, 1)

            for n in range(4):
                d, q = n // 2, n % 2
                if n == 3:
                    pe.wait_ge(s_pcp, 1)
                for b in range(4):
                    ins = nc.tensor.transpose(ps[:, 4 + n, b * P:(b + 1) * P],
                                              cnat[:, d, 4 * q + b, :, :].rearrange("p r n -> p (r n)"), ident[:, :])
                ins.then_inc(s_ctp, 1)
            pe.wait_ge(s_u, 4 + SEED)
            def v_transposes(i, k):
                pe.wait_ge(s_vtd, 2 * i + (k + 1 + SEED))
                pe.wait_ge(s_vcp, 2 * i + (k - 1 + SEED))
                pe.wait_ge(s_ccp, 4)
                b = 4 + 2 * (k % 2)
                for m in range(2):
                    for t in range(2):
                        nc.tensor.transpose(ps[:, b, t * CB + m * P:t * CB + (m + 1) * P],
                                            stg[:, k % 2, m, t * P:(t + 1) * P], ident[:, :])
                    ins = nc.tensor.transpose(ps[0:N_META, b + 1, m * P:(m + 1) * P],
                                              stg[:, k % 2, m, 2 * P:L], ident[:, :])
                ins.then_inc(s_vtp, 1)

            def v_blocks(i, start):
                for k in range(2):
                    pe.wait_ge(s_vtd, 2 * i + (k - 1 + SEED))
                    product(U_V + 8 * i, 4 * k, 4, hnh, hnl, 0, L, (2 * k, 2 * k + 1))
                    if k or not start:
                        v_transposes(i, k - 1)

            v_blocks(0, True)
            with pe.Fori(1, ITERS_IN) as i:
                v_blocks(i, False)
            v_transposes(ITERS_IN - 1, 1)

            def w_trans(p, k):
                pe.wait_ge(s_wd, p + (k + 1))
                pe.wait_ge(s_wp, p + (k + 1))
                pe.wait_ge(s_wts, p + (k - 1 + SEED))
                pe.wait_ge(s_vcp, 4 + SEED)
                for d in range(DIRS):
                    for r in range(2):
                        n = 2 * d + r
                        ins = nc.tensor.transpose(ps[:, 4 + k % 2, n * P:(n + 1) * P], Wn[:, k % WSLOTS, d, r, :], ident[:, :])
                ins.then_inc(s_wtp, 1)

            def chunk_in(p, k):
                pe.wait_ge(s_wts, p + (k + 1 + SEED))
                pe.wait_ge(s_ssb, p + (k - 1 + SEED))
                for n in range(2 * DIRS):
                    u = U[:, ds(p + k, 1), :].rearrange("p a c -> p (a c)")
                    ins = mm(ps[:, 6 + k % 2, n * NCH:(n + 1) * NCH], WT[:, k % 2, n, :], u, start=True, stop=True)
                ins.then_inc(s_sps, 1)

            def beside(base_u, k, n, lo, first, second, p, bank):
                for m, step in ((0, first), (1, second)):
                    half_unit(base_u, k, k % 4, 4, m, hnh, hnl, lo, n, bank + m)
                    step(p, 2 * k)
                    step(p, 2 * k + 1)

            pe.wait_ge(s_vtd, 4 + SEED)
            with pe.Fori(0, ITERS_IN) as i:
                for k in range(8):
                    if k % 4 == 0:
                        pe.wait_ge(s_kev, 2 * i + (k // 4 - 1 + SEED))
                    beside(U_K + 8 * i, k, L, 0, w_trans, chunk_in, 16 * i, k // 4 * 2)
            with pe.Fori(0, ITERS_IN) as i:
                for k in range(2):
                    pe.wait_ge(s_kev, 2 * i + (3 + k + SEED))
                    product(U_Q + 8 * i, 4 * k, 4, hnh, hnl, LIVE, NL, (2 * k, 2 * k + 1))
            pe.wait_ge(s_kev, 8 + SEED)
            with pe.Fori(0, G_SCAN // 2) as i:
                for k in range(2):
                    pe.wait_ge(s_g, 2 * i + (k - 1 + SEED))
                    product(U_G + 8 * i, 4 * k, 4, hnh, hnl, LIVE, NL, (2 * k, 2 * k + 1))

            def kernel(p, k):
                pe.wait_ge(s_gd, p + (k + 1))
                pe.wait_ge(s_gp, p + (k + 1))
                pe.wait_ge(s_bb, p + (k + 1))
                pe.wait_ge(s_tm, p + (k - 1 + SEED))
                g = lambda d, r, a, b: Gn[:, k % GSLOTS, d, r, 32 * a:32 * b]
                bm = lambda d, r: Bm[:, k % GSLOTS, d, r, :]
                o = lambda a, b: ps[0:32, 4 + k % 2, 32 * a:32 * b]
                for r in range(2):
                    mm(o(0, CHUNK - 1), bm(1, r), g(1, r, 1, CHUNK), start=r == 0, stop=r == 1)
                for n in range(4):
                    d, r = n // 2, n % 2
                    e = CHUNK * d
                    mm(o(CHUNK - 1, CHUNK), bm(d, r), g(d, r, e, e + 1), start=n == 0, stop=False)
                mm(o(CHUNK - 1, CHUNK), ident[:, 0:2 * GROUP],
                   dD[:, ds(p + k, 1), :].rearrange("p q c -> p (q c)"), start=False, stop=True)
                for r in range(2):
                    ins = mm(o(CHUNK, 2 * CHUNK - 1), bm(0, r), g(0, r, 1, CHUNK), start=r == 0, stop=r == 1)
                ins.then_inc(s_kps, 1)

            def chunk_out(p, k):
                pe.wait_ge(s_tm, p + (k + 1 + SEED))
                pe.wait_ge(s_ysb, p + (k - 1 + SEED))
                pe.wait_ge(s_ysa, p + (k - 1 + SEED))
                o = ps[:, 6 + k % 2, 0:NCH]
                mm(o, Tm[:, k % 2, :], U[:, ds(p + k, 1), :].rearrange("p a c -> p (a c)"), start=True, stop=False)
                for n in range(2 * DIRS):
                    d, r = n // 2, n % 2
                    st = X[:, 0:NCH, n, ds(p + k, 1)].rearrange("p c q -> p (c q)")
                    a = 32 * (1 - d)
                    ins = mm(o[:, ::-1] if d else o, Gn[:, k % GSLOTS, d, r, a:a + P], st, start=False, stop=n == 3)
                ins.then_inc(s_yps, 1)

            pe.wait_ge(s_ssb, PAIRS + SEED)
            pe.wait_ge(s_g, G_SCAN + SEED)
            for h in range(HEADS):
                b, hh = h // 2, h % 2
                hs = slice(DH * hh, DH * (hh + 1))
                ins = mm(ps[0:2, 2 + hh, b * N_META:(b + 1) * N_META], qm[hs, b, :], km[hs, b, :], start=True, stop=True)
            ins.then_inc(s_m1, 1)
            pe.wait_ge(s_scan, 1)
            with pe.Fori(0, G_SSM) as i:
                pe.wait_ge(s_g, i + (G_SCAN + SEED))
                for k in range(4):
                    for m in range(2):
                        pairs = range(PPU * k + PPU // 2 * m, PPU * k + PPU // 2 * (m + 1))
                        for n in pairs:
                            kernel(4 * PPU * i, n)
                        half_unit(U_G + 4 * G_SCAN + 4 * i, k, k, 4, m, hnh, hnl, LIVE, NL, m)
                        for n in pairs:
                            chunk_out(4 * PPU * i, n)
            pe.wait_ge(s_g, G_SCAN + G_SSM + SEED)
            pe.wait_ge(s_ysb, PAIRS + SEED)
            pe.wait_ge(s_ysa, PAIRS + SEED)

            def scores(i, k):
                j, hh = k // 2, k % 2
                if hh == 0:
                    pe.wait_ge(s_qkv[j], 64 * i + 64)
                pe.wait_ge(s_nm, 4 * i + (k - 1 + SEED))
                pe.wait_ge(s_ptsb, 4 * i + (k - 1 + SEED))
                hs = slice(DH * hh, DH * (hh + 1))
                for t in range(2):
                    ins = mm(ps[:, 2 * hh + t, 0:L], qs[hs, j, 2 + t * P:2 + (t + 1) * P], ks[hs, j, :], start=True, stop=True)
                ins.then_inc(s_qk, 1)

            def probs_t(i, k):
                pe.wait_ge(s_p, 4 * i + (k + 1))
                pe.wait_ge(s_ptsb, 4 * i + (k + SEED))
                for t in range(2):
                    for c in range(2):
                        nc.tensor.transpose(ps[:, 4, c * SEQ + t * P:c * SEQ + (t + 1) * P],
                                            S[:, k % 2, t, c * P:(c + 1) * P], ident[:, :])
                    ins = nc.tensor.transpose(ps[0:N_META, 2 * (k % 2) + t, L:L + P], S[:, k % 2, t, 2 * P:L], ident[:, :])
                ins.then_inc(s_ptps, 1)

            def values(i, k):
                j, hh = k // 2, k % 2
                pe.wait_ge(s_ptsb, 4 * i + (k + 1 + SEED))
                if hh == 0:
                    pe.wait_ge(s_al, 2 * i + (j + SEED))
                hs = slice(DH * hh, DH * (hh + 1))
                o = ps[hs, 5, 0:SEQ]
                mm(o, vs[:, j % 2, 0, hs], PT[:, k % 2, 0:SEQ], start=True, stop=False)
                mm(o, vs[:, j % 2, 1, hs], PT[:, k % 2, SEQ:2 * SEQ], start=False, stop=False)
                mm(o, vs[0:N_META, j % 2, 2, hs], PT2[:, k % 2, :], start=False, stop=True).then_inc(s_pv, 1)

            def att_iteration(i, start):
                for k in range(4):
                    base_u = U_G + 4 * (G_SCAN + G_SSM) + 8 * i
                    first = start and k == 0
                    if not first:
                        scores(i, k)
                    if k % 2 == 0:
                        pe.wait_ge(s_g, 2 * i + (G_SCAN + G_SSM + k // 2 + SEED))
                    for q in range(2):
                        for m in range(2):
                            half_unit(base_u, 2 * k + q, 2 * (k % 2) + q, 4, m, hnh, hnl, LIVE, NL, 6 + m)
                        if q == 0 and first:
                            scores(i, k)
                        elif q == 0:
                            values(i, k - 1)
                    probs_t(i, k)

            att_iteration(0, True)
            with pe.Fori(1, G_ATT // 2) as i:
                att_iteration(i, False)
            values(HEADS // 4 - 1, 3)
            pe.wait_ge(s_ptsb, HEADS + SEED)
            pe.wait_ge(s_m4, 1)
            for h in range(HEADS):
                b, hh = h // 2, h % 2
                ins = nc.tensor.transpose(ps[0:N_META, 2, 2 * h:2 * h + 2], sm[:, hh, b, :], ident[0:2, 0:2])
            ins.then_inc(s_m5, 1)
            pe.wait_ge(s_g, 16 + SEED)
            pe.wait_ge(s_ygl, 1)
            product(U_GLU, 0, 2, ygh, ygl, 0, NL, (0, 1))
            pe.wait_ge(s_m6, 1)
            for h in range(HEADS):
                b, hh = h // 2, h % 2
                hs = slice(DH * hh, DH * (hh + 1))
                ins = mm(ps[hs, 3, 2 * b:2 * b + 2], vm[:, b, hs], ptm[:, 2 * h:2 * h + 2], start=True, stop=True)
            ins.then_inc(s_m7, 1)
            pe.wait_ge(s_mal, 1)
            pe.wait_ge(s_al, KH + SEED)
            for k in range(1, 4):
                product(U_GLU, 2 * k, 2, ygh, ygl, 0, NL, (2 * k, 2 * k + 1))
            with pe.Fori(0, 4) as i:
                for k in range(2):
                    pe.wait_ge(s_mx, 4 * i + (2 * k - 2 + SEED))
                    product(U_PROJ + 8 * i, 4 * k, 2, anh, anl, 0, NL, (4 * k, 4 * k + 1))
                    pe.wait_ge(s_zl, KH)
                    product(U_PROJ + 8 * i, 4 * k + 2, 2, zh, zl, 0, NL, (4 * k + 2, 4 * k + 3))
            def out_blocks(i, start):
                for k in range(2):
                    pe.wait_ge(s_h1, 2 * i + (k - 1 + SEED))
                    product(U_OUT + 8 * i, 4 * k, 4, hnh, hnl, 0, NL, (2 * k, 2 * k + 1), 0, s_ml)
                    for m in range(2):
                        if k or not start:
                            norm_sum(4 * i + (KT + 2 * k + m - 1), start and m == 0, False, sq, m, NL)

            out_blocks(0, True)
            with pe.Fori(1, 4) as i:
                out_blocks(i, False)
            for m in range(2):
                norm_sum(2 * KT + m - 1, False, m == 1, sq, m, NL)
            norm_summed(1)
            with pe.Fori(0, FT // 4) as i:
                for k in range(2):
                    pe.wait_ge(s_fm, 4 * i + (2 * k - 2 + SEED))
                    product(U_UP + 16 * i, 8 * k, 4, hnh, hnl, 0, NL, (4 * k, 4 * k + 1), KT + SEED)
                    product(U_UP + 16 * i, 8 * k + 4, 4, hnh, hnl, 2, SEQ, (4 * k + 2, 4 * k + 3))

            def down(base_u, kt, k, first, final):
                pe.wait_ge(s_lo, base_u + (k + 1))
                pe.wait_ge(s_fl, kt + (1 + SEED))
                xh = ah[:, kt, :] if isinstance(kt, int) else ah[:, ds(kt, 1), :].rearrange("p k n -> p (k n)")
                xl = al[:, kt, :] if isinstance(kt, int) else al[:, ds(kt, 1), :].rearrange("p k n -> p (k n)")
                for m in range(8):
                    g = 8 * (k % 2) + m
                    o = ps[:, g // 2, (g % 2) * SEQ:(g % 2 + 1) * SEQ]
                    cols = slice(m * P, (m + 1) * P)
                    mm(o, slot(whi, k)[:, cols], xh, start=first and g % 2 == 0, stop=False, skip_group_check=True)
                    mm(o, slot(whi, k)[:, cols], xl, start=False, stop=False, skip_group_check=True)
                    ins = mm(o, slot(wlo, k)[:, cols], xh, start=False, stop=final, skip_group_check=True)
                ins.then_inc(s_used, 1)

            pe.wait_ge(s_fm, FT + SEED)
            for k in range(4):
                down(U_DOWN, k // 2, k, k < 2, False)
            with pe.Fori(1, FT // 2 - 1) as i:
                for k in range(4):
                    down(U_DOWN + 4 * i, 2 * i + k // 2, k, False, False)
            for k in range(4):
                down(U_END - 4, FT - 2 + k // 2, k, False, k >= 2)

            for n in range(KT // 2):
                g, t = n // 2, n % 2
                pe.wait_ge(s_h2, max(2 * g + 2, n + 1))
                for k in range(4):
                    ins = nc.tensor.transpose(ps[:, n, k * P:(k + 1) * P],
                                              xT[:, 4 * g + k, N_META + t * P:N_META + (t + 1) * P], ident[:, :])
                ins.then_inc(s_ot, 1)


_INS = ["x", "meta_tokens", "norm1_g", "w_in", "na_rpb", "ssm_lam_re", "ssm_lam_im", "ssm_log_step", "ssm_b_re",
        "ssm_b_im", "ssm_c_re", "ssm_c_im", "ssm_d", "w_glu", "w_proj_na", "w_proj_ssm", "w_out", "norm2_g",
        "w_up", "conv_w", "conv_b", "w_down", "final_g"]


def kernel(**inputs):
    import numpy as _np
    import concourse.bacc as _bacc
    from concourse import mybir as _mybir
    from concourse.bass_utils import run_bass_kernel_spmd as _run

    nc = _bacc.Bacc("TRN2", target_bir_lowering=False, num_devices=1)
    arrays, args = {}, []
    for name in _INS:
        a = _np.ascontiguousarray(inputs[name])
        arrays[f"in_{name}"] = a
        args.append(nc.dram_tensor(f"in_{name}", a.shape, _mybir.dt.from_np(a.dtype), kind="ExternalInput").ap())
    args.append(nc.dram_tensor("out_h", (1, SEQ, D_MODEL), _mybir.dt.float32, kind="ExternalOutput").ap())
    encoder_block(nc, *args)
    r = _run(nc, [arrays], core_ids=[0])
    return r.results[0]["out_h"]
```
